# Optimizing a Trainium2 kernel written in Bass

```python
import math
import jax, jax.numpy as jnp
from jax import lax
import numpy as np

"""One inference step of a hybrid diffusion / flow-matching trunk (DEPTH interleaved layers).

Layer l uses token mixer (l mod 4): 0 = multi-head latent attention (MLA), 1 = differential
attention, 2 = grouped-query attention with 2-D axial rotary, 3 = bidirectional RG-LRU.
Every layer: adaLN-modulated pre-RMSNorm -> token mixer -> gated residual, then
adaLN-modulated pre-RMSNorm -> SwiGLU FFN -> gated residual.
Context tokens (un-noised prefix) use the constant conditioning c_ctx and read only context;
latent tokens use c and read all context tokens plus all latent tokens.

Inputs: x_prompt (BATCH, SEQ, D_MODEL) context tokens of new requests;
        x_sample (DEC_BATCH, DEC_SEQ, D_MODEL) noisy latent grid tokens (row = t // GRID_W);
        cache_* / state_* : cached context tensors for PAST_LEN context tokens (leading dim DEC_BATCH);
        c (DEC_BATCH, D_MODEL) conditioning vectors; c_ctx (D_MODEL,) context conditioning; weights.
Output tuple:
  y_prompt       (BATCH, SEQ, D_MODEL)
  y_sample       (DEC_BATCH, DEC_SEQ, D_MODEL)
  new_mla_ckv    (BATCH, N_MLA, SEQ, MLA_KV_RANK)          normalised compressed KV latent
  new_mla_krope  (BATCH, N_MLA, SEQ, MLA_ROPE)             normalised decoupled key (context: unrotated)
  new_diff_k     (BATCH, N_DIFF, SEQ, DIFF_HEADS, 2, DIFF_HD)
  new_diff_v     (BATCH, N_DIFF, SEQ, DIFF_HEADS, 2*DIFF_HD)
  new_gqa_k      (BATCH, N_GQA, SEQ, GQA_KV_HEADS, GQA_HD)
  new_gqa_v      (BATCH, N_GQA, SEQ, GQA_KV_HEADS, GQA_HD)
  new_lru_h      (BATCH, N_LRU, 2, D_RNN)                  final context scan state per direction
"""

D_MODEL = 1024
BATCH = 1
SEQ = 128
DEPTH = 4
DEC_BATCH = 1
DEC_SEQ = 512
PAST_LEN = 128

GRID_W = 64
N_MIXERS = 4
N_MLA = (DEPTH + 3) // 4
N_DIFF = (DEPTH + 2) // 4
N_GQA = (DEPTH + 1) // 4
N_LRU = DEPTH // 4
EPS = 1e-6
ROPE_THETA = 10000.0
Q_BLOCK = 128
FFN_HIDDEN = -(-8 * D_MODEL // (3 * 256)) * 256
MLA_HEADS = 8
MLA_NOPE = 128
MLA_ROPE = 64
MLA_V = 128
MLA_Q_RANK = 384
MLA_KV_RANK = 256
DIFF_HD = 64
DIFF_HEADS = D_MODEL // (2 * DIFF_HD)
GQA_HD = 128
GQA_Q_HEADS = D_MODEL // GQA_HD
GQA_KV_HEADS = 2
D_RNN = D_MODEL
LRU_BLOCKS = 8
LRU_BLK = D_RNN // LRU_BLOCKS
CONV_W = 4
CONV_LEFT = 1
LRU_C = 8.0

kernel_name = "hybrid_diffusion_mla_diff_gqa_rglru_step"

def rmsnorm(x, g):
    xf = x.astype(jnp.float32)
    y = xf * lax.rsqrt(jnp.mean(xf * xf, axis=-1, keepdims=True) + EPS)
    return (y * g.astype(jnp.float32)).astype(x.dtype)

def axial_rope(n_tok, rot_dim):
    rows = n_tok // GRID_W
    row = jnp.repeat(jnp.arange(rows), GRID_W).astype(jnp.float32)
    col = jnp.tile(jnp.arange(GRID_W), rows).astype(jnp.float32)
    n_freq = rot_dim // 4
    inv = ROPE_THETA ** (-jnp.arange(n_freq, dtype=jnp.float32) / n_freq)
    ang = jnp.concatenate([row[:, None] * inv, col[:, None] * inv], axis=-1)
    return jnp.cos(ang), jnp.sin(ang)

def apply_rope(x, cos, sin):
    half = x.shape[-1] // 2
    shape = (1, x.shape[1]) + (1,) * (x.ndim - 3) + (half,)
    cos, sin = cos.reshape(shape), sin.reshape(shape)
    xf = x.astype(jnp.float32)
    x1, x2 = xf[..., :half], xf[..., half:]
    return jnp.concatenate([x1 * cos - x2 * sin, x1 * sin + x2 * cos], axis=-1).astype(x.dtype)

def blocked_attention(q, k, v):
    b, s, hq, dq = q.shape
    hkv, dv = k.shape[2], v.shape[-1]
    g = hq // hkv
    nb = s // Q_BLOCK
    scale = dq ** -0.5
    qb = jnp.moveaxis(q.reshape(b, nb, Q_BLOCK, hkv, g, dq), 1, 0)

    def attend(qblk):
        sc = jnp.einsum('bqhgd,bkhd->bhgqk', qblk, k).astype(jnp.float32) * scale
        p = jax.nn.softmax(sc, axis=-1).astype(v.dtype)
        return jnp.einsum('bhgqk,bkhd->bqhgd', p, v)

    o = lax.map(attend, qb)
    return jnp.moveaxis(o, 0, 1).reshape(b, s, hq, dv)

def mla_mixer(h, w_in, g_cq, g_ckv, w_uq, w_ukv, g_qk, w_o, ctx):
    b, s, _ = h.shape
    proj = h @ w_in
    cq = rmsnorm(proj[..., :MLA_Q_RANK], g_cq)
    ckv = rmsnorm(proj[..., MLA_Q_RANK:MLA_Q_RANK + MLA_KV_RANK], g_ckv)
    kr = rmsnorm(proj[..., MLA_Q_RANK + MLA_KV_RANK:], g_qk[1, MLA_NOPE:])
    q = (cq @ w_uq).reshape(b, s, MLA_HEADS, MLA_NOPE + MLA_ROPE)
    q_nope = rmsnorm(q[..., :MLA_NOPE], g_qk[0, :MLA_NOPE])
    q_rope = rmsnorm(q[..., MLA_NOPE:], g_qk[0, MLA_NOPE:])
    keys_ckv, keys_kr = ckv, kr
    if ctx is not None:
        cos, sin = axial_rope(s, MLA_ROPE)
        q_rope = apply_rope(q_rope, cos, sin)
        keys_ckv = jnp.concatenate([ctx[0], ckv], axis=1)
        keys_kr = jnp.concatenate([ctx[1], apply_rope(kr, cos, sin)], axis=1)
    l = keys_ckv.shape[1]
    kv = (keys_ckv @ w_ukv).reshape(b, l, MLA_HEADS, MLA_NOPE + MLA_V)
    k_nope = rmsnorm(kv[..., :MLA_NOPE], g_qk[1, :MLA_NOPE])
    k = jnp.concatenate([k_nope, jnp.broadcast_to(keys_kr[:, :, None, :], (b, l, MLA_HEADS, MLA_ROPE))], axis=-1)
    o = blocked_attention(jnp.concatenate([q_nope, q_rope], axis=-1), k, kv[..., MLA_NOPE:])
    return o.reshape(b, s, MLA_HEADS * MLA_V) @ w_o, (ckv, kr)

def diff_mixer(h, w_in, g_qk, lam, g_sub, w_o, lambda_init, ctx):
    b, s, _ = h.shape
    q, k, v = jnp.split(h @ w_in, 3, axis=-1)
    q = rmsnorm(q.reshape(b, s, DIFF_HEADS, 2, DIFF_HD), g_qk[0])
    k = rmsnorm(k.reshape(b, s, DIFF_HEADS, 2, DIFF_HD), g_qk[1])
    v = v.reshape(b, s, DIFF_HEADS, 2 * DIFF_HD)
    keys, vals = k, v
    if ctx is not None:
        cos, sin = axial_rope(s, DIFF_HD)
        q = apply_rope(q, cos, sin)
        keys = jnp.concatenate([ctx[0], apply_rope(k, cos, sin)], axis=1)
        vals = jnp.concatenate([ctx[1], v], axis=1)
    lam = lam.astype(jnp.float32)
    lam_full = jnp.exp(jnp.sum(lam[0] * lam[1])) - jnp.exp(jnp.sum(lam[2] * lam[3])) + lambda_init
    o1 = blocked_attention(q[:, :, :, 0], keys[:, :, :, 0], vals)
    o2 = blocked_attention(q[:, :, :, 1], keys[:, :, :, 1], vals)
    o = o1.astype(jnp.float32) - lam_full * o2.astype(jnp.float32)
    o = (rmsnorm(o, g_sub) * (1.0 - lambda_init)).astype(h.dtype)
    return o.reshape(b, s, DIFF_HEADS * 2 * DIFF_HD) @ w_o, (k, v)

def gqa_mixer(h, w_in, g_qk, w_o, ctx):
    b, s, _ = h.shape
    nq, nk = GQA_Q_HEADS * GQA_HD, GQA_KV_HEADS * GQA_HD
    proj = h @ w_in
    q = rmsnorm(proj[..., :nq].reshape(b, s, GQA_Q_HEADS, GQA_HD), g_qk[0])
    k = rmsnorm(proj[..., nq:nq + nk].reshape(b, s, GQA_KV_HEADS, GQA_HD), g_qk[1])
    v = proj[..., nq + nk:].reshape(b, s, GQA_KV_HEADS, GQA_HD)
    keys, vals = k, v
    if ctx is not None:
        cos, sin = axial_rope(s, GQA_HD)
        q = apply_rope(q, cos, sin)
        keys = jnp.concatenate([ctx[0], apply_rope(k, cos, sin)], axis=1)
        vals = jnp.concatenate([ctx[1], v], axis=1)
    o = blocked_attention(q, keys, vals)
    return o.reshape(b, s, nq) @ w_o, (k, v)

def centred_conv(x, w, bias):
    s = x.shape[1]
    xp = jnp.pad(x, ((0, 0), (CONV_LEFT, CONV_W - 1 - CONV_LEFT), (0, 0)))
    y = xp[:, 0:s] * w[0]
    for t in range(1, CONV_W):
        y = y + xp[:, t:t + s] * w[t]
    return y + bias

def _linear_combine(e1, e2):
    a1, b1 = e1
    a2, b2 = e2
    return a1 * a2, a2 * b1 + b2

def rglru_scan(x, w_gate, b_gate, lam, h0):
    b, s, _ = x.shape
    xb = x.reshape(b, s, LRU_BLOCKS, LRU_BLK)
    g = jnp.einsum('bsnk,gnkj->gbsnj', xb, w_gate).reshape(2, b, s, D_RNN)
    g = g.astype(jnp.float32) + b_gate.astype(jnp.float32)[:, None, None, :]
    r, i = jax.nn.sigmoid(g[0]), jax.nn.sigmoid(g[1])
    log_a = -LRU_C * r * jax.nn.softplus(-lam.astype(jnp.float32))
    a = jnp.exp(log_a)
    u = jnp.sqrt(-jnp.expm1(2.0 * log_a)) * (i * x.astype(jnp.float32))
    if h0 is not None:
        u = u.at[:, 0].add(a[:, 0] * h0)
    _, hs = lax.associative_scan(_linear_combine, (a, u), axis=1)
    return hs

def lru_mixer(h, w_in, conv_w, conv_b, w_gate, b_gate, lam, w_out, ctx):
    gate_branch, xr = jnp.split(h @ w_in, 2, axis=-1)
    xr = centred_conv(xr, conv_w, conv_b)
    h0f = None if ctx is None else ctx[0][:, 0].astype(jnp.float32)
    h0b = None if ctx is None else ctx[0][:, 1].astype(jnp.float32)
    hf = rglru_scan(xr, w_gate[0], b_gate[0], lam[0], h0f)
    hb = jnp.flip(rglru_scan(jnp.flip(xr, axis=1), w_gate[1], b_gate[1], lam[1], h0b), axis=1)
    y = (hf + hb).astype(h.dtype) * jax.nn.gelu(gate_branch)
    state = jnp.stack([hf[:, -1], hb[:, 0]], axis=1)
    return y @ w_out, (state,)

def swiglu(h, w_in, w_out):
    gte, up = jnp.split(h @ w_in, 2, axis=-1)
    return (jax.nn.silu(gte) * up) @ w_out

def setup_inputs(seed: int = 0) -> dict:
    key = jax.random.key(seed)
    ks = iter(jax.random.split(key, 48))
    D = D_MODEL

    def nrm(shape, scale=1.0):
        return jax.random.normal(next(ks), shape, jnp.float32) * scale

    def gain(shape):
        return 1.0 + nrm(shape, 0.02)

    u = jax.random.uniform(next(ks), (N_LRU, 2, D_RNN), jnp.float32, 0.9, 0.999)
    a0 = u ** (1.0 / LRU_C)
    lru_lambda = jnp.log(a0 / (1.0 - a0))
    return {
        "x_prompt": nrm((BATCH, SEQ, D)),
        "x_sample": nrm((DEC_BATCH, DEC_SEQ, D)),
        "cache_mla_ckv": nrm((DEC_BATCH, N_MLA, PAST_LEN, MLA_KV_RANK)),
        "cache_mla_krope": nrm((DEC_BATCH, N_MLA, PAST_LEN, MLA_ROPE)),
        "cache_diff_k": nrm((DEC_BATCH, N_DIFF, PAST_LEN, DIFF_HEADS, 2, DIFF_HD)),
        "cache_diff_v": nrm((DEC_BATCH, N_DIFF, PAST_LEN, DIFF_HEADS, 2 * DIFF_HD)),
        "cache_gqa_k": nrm((DEC_BATCH, N_GQA, PAST_LEN, GQA_KV_HEADS, GQA_HD)),
        "cache_gqa_v": nrm((DEC_BATCH, N_GQA, PAST_LEN, GQA_KV_HEADS, GQA_HD)),
        "state_lru_h": nrm((DEC_BATCH, N_LRU, 2, D_RNN), 0.5),
        "c": nrm((DEC_BATCH, D)),
        "c_ctx": nrm((D,)),
        "w_mod": nrm((DEPTH, D, 6 * D), 0.5 * D ** -0.5),
        "b_mod": nrm((DEPTH, 6 * D), 0.01),
        "g_norm1": gain((DEPTH, D)),
        "g_norm2": gain((DEPTH, D)),
        "w_ffn_in": nrm((DEPTH, D, 2 * FFN_HIDDEN), D ** -0.5),
        "w_ffn_out": nrm((DEPTH, FFN_HIDDEN, D), FFN_HIDDEN ** -0.5),
        "mla_w_in": nrm((N_MLA, D, MLA_Q_RANK + MLA_KV_RANK + MLA_ROPE), D ** -0.5),
        "mla_g_cq": gain((N_MLA, MLA_Q_RANK)),
        "mla_g_ckv": gain((N_MLA, MLA_KV_RANK)),
        "mla_w_uq": nrm((N_MLA, MLA_Q_RANK, MLA_HEADS * (MLA_NOPE + MLA_ROPE)), MLA_Q_RANK ** -0.5),
        "mla_w_ukv": nrm((N_MLA, MLA_KV_RANK, MLA_HEADS * (MLA_NOPE + MLA_V)), MLA_KV_RANK ** -0.5),
        "mla_g_qk": gain((N_MLA, 2, MLA_NOPE + MLA_ROPE)),
        "mla_w_o": nrm((N_MLA, MLA_HEADS * MLA_V, D), (MLA_HEADS * MLA_V) ** -0.5),
        "diff_w_in": nrm((N_DIFF, D, 3 * DIFF_HEADS * 2 * DIFF_HD), D ** -0.5),
        "diff_g_qk": gain((N_DIFF, 2, DIFF_HD)),
        "diff_lambda": nrm((N_DIFF, 4, DIFF_HD), 0.1),
        "diff_g_sub": gain((N_DIFF, 2 * DIFF_HD)),
        "diff_w_o": nrm((N_DIFF, DIFF_HEADS * 2 * DIFF_HD, D), (DIFF_HEADS * 2 * DIFF_HD) ** -0.5),
        "gqa_w_in": nrm((N_GQA, D, (GQA_Q_HEADS + 2 * GQA_KV_HEADS) * GQA_HD), D ** -0.5),
        "gqa_g_qk": gain((N_GQA, 2, GQA_HD)),
        "gqa_w_o": nrm((N_GQA, GQA_Q_HEADS * GQA_HD, D), (GQA_Q_HEADS * GQA_HD) ** -0.5),
        "lru_w_in": nrm((N_LRU, D, 2 * D_RNN), D ** -0.5),
        "lru_conv_w": nrm((N_LRU, CONV_W, D_RNN), CONV_W ** -0.5),
        "lru_conv_b": nrm((N_LRU, D_RNN), 0.01),
        "lru_w_gate": nrm((N_LRU, 2, 2, LRU_BLOCKS, LRU_BLK, LRU_BLK), LRU_BLK ** -0.5),
        "lru_b_gate": nrm((N_LRU, 2, 2, D_RNN), 0.01),
        "lru_lambda": lru_lambda,
        "lru_w_out": nrm((N_LRU, D_RNN, D), D_RNN ** -0.5),
    }

def reference(x_prompt, x_sample, cache_mla_ckv, cache_mla_krope, cache_diff_k, cache_diff_v,
              cache_gqa_k, cache_gqa_v, state_lru_h, c, c_ctx, w_mod, b_mod, g_norm1, g_norm2,
              w_ffn_in, w_ffn_out, mla_w_in, mla_g_cq, mla_g_ckv, mla_w_uq, mla_w_ukv, mla_g_qk,
              mla_w_o, diff_w_in, diff_g_qk, diff_lambda, diff_g_sub, diff_w_o, gqa_w_in, gqa_g_qk,
              gqa_w_o, lru_w_in, lru_conv_w, lru_conv_b, lru_w_gate, lru_b_gate, lru_lambda, lru_w_out):

    def token_mixer(l, h, ctx):
        kind, j = l % N_MIXERS, l // N_MIXERS
        if kind == 0:
            return mla_mixer(h, mla_w_in[j], mla_g_cq[j], mla_g_ckv[j], mla_w_uq[j], mla_w_ukv[j],
                             mla_g_qk[j], mla_w_o[j], ctx)
        if kind == 1:
            lambda_init = 0.8 - 0.6 * math.exp(-0.3 * l)
            return diff_mixer(h, diff_w_in[j], diff_g_qk[j], diff_lambda[j], diff_g_sub[j], diff_w_o[j],
                              lambda_init, ctx)
        if kind == 2:
            return gqa_mixer(h, gqa_w_in[j], gqa_g_qk[j], gqa_w_o[j], ctx)
        return lru_mixer(h, lru_w_in[j], lru_conv_w[j], lru_conv_b[j], lru_w_gate[j], lru_b_gate[j],
                         lru_lambda[j], lru_w_out[j], ctx)

    def layer_cache(l):
        kind, j = l % N_MIXERS, l // N_MIXERS
        if kind == 0:
            return (cache_mla_ckv[:, j], cache_mla_krope[:, j])
        if kind == 1:
            return (cache_diff_k[:, j], cache_diff_v[:, j])
        if kind == 2:
            return (cache_gqa_k[:, j], cache_gqa_v[:, j])
        return (state_lru_h[:, j],)

    def trunk_layer(l, x, cond, ctx):
        mod = (jax.nn.silu(cond) @ w_mod[l] + b_mod[l]).reshape(cond.shape[0], 6, D_MODEL)[:, :, None, :]
        h = rmsnorm(x, g_norm1[l]) * (1.0 + mod[:, 1]) + mod[:, 0]
        out, ctx_tensors = token_mixer(l, h, ctx)
        x = x + mod[:, 2] * out
        h = rmsnorm(x, g_norm2[l]) * (1.0 + mod[:, 4]) + mod[:, 3]
        x = x + mod[:, 5] * swiglu(h, w_ffn_in[l], w_ffn_out[l])
        return x, ctx_tensors

    x = x_prompt
    ctx_states = []
    for l in range(DEPTH):
        x, st = trunk_layer(l, x, c_ctx[None, :], None)
        ctx_states.append(st)
    y_prompt = x

    def collect(kind, idx):
        return jnp.stack([ctx_states[l][idx] for l in range(kind, DEPTH, N_MIXERS)], axis=1)

    new_mla_ckv = collect(0, 0)
    new_mla_krope = collect(0, 1)
    new_diff_k = collect(1, 0)
    new_diff_v = collect(1, 1)
    new_gqa_k = collect(2, 0)
    new_gqa_v = collect(2, 1)
    new_lru_h = collect(3, 0)

    x = x_sample
    for l in range(DEPTH):
        x, _ = trunk_layer(l, x, c, layer_cache(l))
    y_sample = x

    return (y_prompt, y_sample, new_mla_ckv, new_mla_krope, new_diff_k, new_diff_v, new_gqa_k, new_gqa_v, new_lru_h)


_drawn_inputs = setup_inputs


def setup_inputs(seed=0):
    import zlib

    import numpy as np

    out = dict(_drawn_inputs(seed))
    spreads = {}
    factors = {'cache_mla_ckv': 3.979,
     'cache_mla_krope': 8.0,
     'cache_gqa_k': 7.243,
     'cache_gqa_v': 5.111,
     'g_norm1': 2.73,
     'g_norm2': 5.011,
     'mla_g_cq': 8.0,
     'mla_g_ckv': 2.873,
     'mla_g_qk': 2.789,
     'diff_g_qk': 2.953,
     'diff_g_sub': 50.816,
     'lru_b_gate': 21.433,
     'cache_diff_k': 8.0,
     'cache_diff_v': 8.0,
     'state_lru_h': 4.692,
     'lru_conv_b': 3.611}
    for name, (base, spread) in spreads.items():
        noise = np.random.default_rng([zlib.crc32(name.encode()), seed]).standard_normal(out[name].shape)
        drawn = base * np.exp(spread * noise) if base else spread * noise
        out[name] = __import__('jax').numpy.asarray(drawn.astype(out[name].dtype))
    for name, factor in factors.items():
        out[name] = (out[name] * factor).astype(out[name].dtype)
    return out
```

```python
import math
from contextlib import ExitStack

import numpy as np
import concourse.bass as bass
from concourse import mybir

F32 = mybir.dt.float32
F32R = mybir.dt.float32r
ALU = mybir.AluOpType
ACT = mybir.ActivationFunctionType
AX = mybir.AxisListType

P = 128
D = 1024
KT = D // P
NCTX, NLAT = 128, 512
T = NCTX + NLAT
TH = T // 2
NKEY = T + 128
DEPTH = 4
EPS = 1e-6
FFN = 2816
FFN_CHUNKS = (8, 8, 6)
HEADS = 8
MLA_QR, MLA_KVR = 384, 256
CQ_AT, CKV_AT = 0, 3 * T
QT = 5
LW = T + 4
LAT0 = 131
SLOT = 8 * P
WORK = 11300
LAMBDA_INIT = 0.8 - 0.6 * math.exp(-0.3)

VEC_ROWS = [("gn1", 32), ("gn2", 32), ("cq", 3), ("ckv", 2), ("convb", 8), ("convw", 32), ("dsub", 1),
            ("gqk", 2), ("mqk", 2), ("mqr", 2), ("dqk", 2), ("pad", 10),
            ("bgate", 32), ("lam", 16), ("h0", 16), ("c", 8), ("cctx", 8), ("pad2", 48)]
VEC = {}
_at = 0
for _name, _n in VEC_ROWS:
    VEC[_name] = _at
    _at += _n
assert VEC["bgate"] == P and _at == 2 * P


class Steps:

    def __init__(self, sem, names, base=0):
        self.sem, self.names, self.base, self.k = sem, names, base, 0

    def open(self, eng):
        assert self.base == 1
        eng.sem_inc(self.sem, 1)

    def mark(self, ins, name):
        assert self.names[self.k % len(self.names)] == name, (name, self.names[self.k % len(self.names)])
        self.k += 1
        ins.then_inc(self.sem, 1)

    def wait(self, eng, name, turn=0):
        eng.wait_ge(self.sem, turn * len(self.names) + (self.base + self.names.index(name) + 1))

    def wait_turns(self, eng, turn):
        eng.wait_ge(self.sem, turn * len(self.names) + self.base)


class Phase:

    def __init__(self, turns, slots, shape, first, landed):
        self.turns, self.slots, self.shape, self.first = turns, slots, shape, first
        self.landed = dict(landed)
        self.n = len(slots)

    def number(self, turn, j):
        return turn * self.n + (self.first + j + 1)


def plan_panels():
    phases, first, landed = {}, 0, {0: 0, 1: 0, 2: 0}

    def add(name, turns, slots, shape):
        nonlocal first
        phases[name] = Phase(turns, slots, shape, first, landed)
        for s in slots:
            landed[s] += turns
        first += turns * len(slots)

    for layer in range(DEPTH):
        if layer == 0:
            add("mla_in", 3, (0, 1), [(KT, P)] * 2)
            add("mla", HEADS, (0, 1), [(3, 192), (2, 256)])
        elif layer == 1:
            add("diff", HEADS, (2, 0, 1), [(KT, P)] * 3)
        elif layer == 2:
            add("gqa_kv", 2, (0, 1), [(KT, P)] * 2)
            add("gqa", HEADS // 2, (0, 1), [(KT, P)] * 2)
        else:
            add("lru", KT, (2, 0, 1), [(KT, P), (KT, P), (4, P)])
        add(f"wo{layer}", KT // 2, (0, 1), [(KT, P)] * 2)
        for c, size in enumerate(FFN_CHUNKS):
            add(f"in{layer}.{c}", size, (0, 1), [(KT, P)] * 2)
            add(f"out{layer}.{c}", KT // 2, (0, 1), [(size, P)] * 2)
    return phases


def attention_names(pre, comps):
    pe, act, dve = [], [], []
    for t in range(QT + 1):
        if t < QT:
            pe += [f"{pre}scores{t}.{c}" for c in range(comps)]
            act += [f"{pre}exp{t}.{c}" for c in range(comps)]
            dve += [f"{pre}max{t}.{c}" for c in range(comps)]
        if t >= 1:
            pe.append(f"{pre}turned{t - 1}")
            act.append(f"{pre}pt{t - 1}")
            dve.append(f"{pre}probs{t - 1}")
    pe.append(f"{pre}pv")
    return pe, act, dve


def build(nc, a):
    phases = plan_panels()

    with ExitStack() as ctx:
        def sb(name, cols, dt=F32):
            return ctx.enter_context(nc.sbuf_tensor(name, [P, cols], dt))

        def sem(name):
            return ctx.enter_context(nc.semaphore(name))

        x = sb("x", KT * T)
        h_hi, h_lo = sb("h_hi", KT * T, F32R), sb("h_lo", KT * T, F32R)
        act_hi, act_lo = sb("act_hi", KT * T, F32R), sb("act_lo", KT * T, F32R)
        raw = [sb(f"raw{s}", SLOT) for s in range(3)]
        w_hi = [sb(f"w_hi{s}", SLOT, F32R) for s in range(3)]
        w_lo = [sb(f"w_lo{s}", SLOT, F32R) for s in range(3)]
        mod_raw = [sb(f"mod_raw{s}", SLOT) for s in range(2)]
        y_hi, y_lo = sb("y_hi", LW, F32R), sb("y_lo", LW, F32R)
        work = sb("work", WORK)
        consts = sb("consts", 5 * P)
        tables = sb("tables", 4 * NLAT)
        vecs = sb("vecs", 2 * P)
        bmod = sb("bmod", 192)
        mods = [sb(f"mods{b}", 96) for b in range(2)]
        gains = sb("gains", 32)
        silu_c = sb("silu_c", 16)
        small = sb("small", 64)
        lru_small = sb("lru_small", 256)
        psum = [ctx.enter_context(nc.psum_tensor(f"ps{n}", [P, 2, 512], F32)) for n in "ABCD"]
        psA, psB, psC, psD = psum

        ident, ones, blocks, rot64, rot128 = (consts[:, k * P:(k + 1) * P] for k in range(5))
        cos64, sin64, cos128, sin128 = (tables[:, k * NLAT:(k + 1) * NLAT] for k in range(4))
        eps = small[:, 40:41]
        neg_lambda = small[:, 41:42]

        class Carve:

            def __init__(self):
                self.at = 0

            def __call__(self, n):
                self.at += n
                assert self.at <= WORK, self.at
                return work[:, self.at - n:self.at]

        const_in = sem("const_in")
        x_in = sem("x_in")
        raw_in = [sem(f"raw_in{s}") for s in range(3)]
        mod_in = [sem(f"mod_in{s}") for s in range(2)]
        pool_hi = sem("pool_hi")
        split_done = sem("split_done")
        gemm_done = sem("gemm_done")
        mod_used = sem("mod_used")
        mod_done = sem("mod_done")
        mod_ready = sem("mod_ready")
        x_done = sem("x_done")
        square_done = sem("square_done")
        sums_done = sem("sums_done")
        rstd_done = sem("rstd_done")
        scaled_done = sem("scaled_done")
        h_hi_done = sem("h_hi_done")
        h_done = sem("h_done")
        silu_done = sem("silu_done")
        hidden_done = sem("hidden_done")
        pre_pe, pre_act, pre_dve = sem("pre_pe"), sem("pre_act"), sem("pre_dve")
        cache_in, gcache_in = sem("cache_in"), sem("gcache_in")
        kr_cleared, lru_ready = sem("kr_cleared"), sem("lru_ready")
        outs_done = sem("outs_done")
        y_turned, y_copied, y_out = sem("y_turned"), sem("y_copied"), sem("y_out")

        def steps(name, pe, act, dve, base=1):
            return tuple(Steps(sem(f"{name}_{e}"), names, base) for e, names in (("pe", pe), ("act", act), ("dve", dve)))

        PRE = [Steps(pre_pe, ["vecs", "bmod", "lam", "x0", "x1", "x2", "x3", "x4", "x5", "x6", "x7"]),
               Steps(pre_act, ["vecs", "silu", "lamexp", "sp"]),
               Steps(pre_dve, ["ready", "lamsum", "lamdiff", "lamall", "bmod", "splog"])]
        cpe, cact, cdve = attention_names("", 1)
        MIN = steps("mla_in", ["sscq", "ssckv", "sskr", "rotkr", "turned"],
                    [f"m{t}" for t in range(6)] + ["rscq", "rsckv", "rskr", "outs"],
                    ["cq", "ckv", "kr", "kr_roped", "cache"], 0)
        MLA = steps("mla_head", ["gqn", "gkn", "ssqn", "ssqr", "sskn", "rotqr", "turned_v"] + cpe,
                    ["evqn", "evqr", "evkn", "evv", "rsqn", "rsqr", "rskn", "v"] + cact,
                    ["qn", "qr", "kn", "qroped"] + cdve + ["o"])
        dpe, dact, ddve = attention_names("", 2)
        DIF = steps("diff_head", ["ssq", "ssk", "rotq", "rotk", "turned_v"] + dpe + ["sso"],
                    ["evq", "evk", "rsq", "evv", "rsk", "v"] + dact + ["evo", "rso"],
                    ["q", "k", "qroped", "kroped"] + ddve + ["o"])
        GKV = steps("gqa_kv", ["ssk", "rotk", "turned_v"], ["evk", "evv", "rsk", "v"], ["k", "kroped"], 0)
        gn = [attention_names(p, 1) for p in "ab"]
        GQA = steps("gqa_head",
                    sum([[p + "ssq", p + "rotq"] + gn[k][0] for k, p in enumerate("ab")], []),
                    sum([[p + "evq", p + "rsq"] + gn[k][1] for k, p in enumerate("ab")], []),
                    sum([[p + "q", p + "qroped"] + gn[k][2] + [p + "o"] for k, p in enumerate("ab")], []))
        LRU = steps("lru", ["rf", "if", "rb"], ["gelu", "xp", "tf", "tb", "th", "sq"], ["y", "o"])

        def products(pe, out, slot, kts, cols, c0, rhs_hi, rhs_lo, at, stride, half):
            last = None
            for kt in range(kts):
                for p, (w, r) in enumerate(((w_hi, rhs_hi), (w_hi, rhs_lo), (w_lo, rhs_hi))):
                    for b in range(2):
                        o = at + kt * stride + b * half
                        last = nc.tensor.matmul(out[:, b, 0:half], w[slot][:, kt * cols + c0:kt * cols + c0 + P],
                                                r[:, o:o + half], start=(kt == 0 and p == 0),
                                                stop=(kt == kts - 1 and p == 2))
            return last

        def take_panel(pe, name, turn, j):
            ph = phases[name]
            pe.wait_ge(split_done, ph.number(turn, j))
            return ph.slots[j]

        def sum_rows(out, ones_, pieces, half):
            last = None
            for b in range(2):
                for k, sq in enumerate(pieces):
                    last = nc.tensor.matmul(out[:, b, 0:half], ones_, sq[:, b * half:(b + 1) * half],
                                            start=(k == 0), stop=(k == len(pieces) - 1))
            return last

        def attention_pe(pe, S, pre, comps, scores, V, PT, PTp, probs, turn):
            pes, acts, dves = S
            for t in range(QT + 1):
                if t < QT:
                    for c in range(comps):
                        j = t * comps + c
                        s = psum[j % 2]
                        if j >= 2:
                            acts.wait(pe, f"{pre}exp{(j - 2) // comps}.{(j - 2) % comps}", turn)
                        q0 = 128 + t * P if t < 4 else 0
                        spans = ((0, 128, TH), (1, 128 + TH, TH)) if t < 4 else ((0, 0, P),)
                        for b, k0, n in spans:
                            for m, (q, k) in enumerate(scores[c]):
                                last = nc.tensor.matmul(s[:, b, 0:n], q[:, q0:q0 + P], k[:, k0:k0 + n],
                                                        start=(m == 0), stop=(m == len(scores[c]) - 1))
                        pes.mark(last, f"{pre}scores{t}.{c}")
                if t >= 1:
                    u = t - 1
                    dves.wait(pe, f"{pre}probs{u}", turn)
                    if u >= 2:
                        acts.wait(pe, f"{pre}pt{u - 2}", turn)
                    d = psum[2 + u % 2]
                    for k in range(5 if u < 4 else 1):
                        last = nc.tensor.transpose(d[:, k // 4, (k % 4) * P:(k % 4 + 1) * P],
                                                   probs[u % 2][0][:, k * P:(k + 1) * P], ident)
                    pes.mark(last, f"{pre}turned{u}")
            acts.wait(pe, f"{pre}pt4", turn)
            for k in range(5):
                nc.tensor.matmul(psD[:, 0, 0:NLAT], V[:, (k + 1) * P:(k + 2) * P], PT[:, k * NLAT:(k + 1) * NLAT],
                                 start=(k == 0), stop=(k == 4))
            pes.mark(nc.tensor.matmul(psD[:, 1, 0:P], V[:, 0:P], PTp, start=True, stop=True), pre + "pv")

        def halves(ap, half):
            return ap.rearrange("p (b n) -> p b n", b=2)

        def evacuate(out, sq, ps, half):
            nc.scalar.activation(halves(out, half), ps[:, :, 0:half], ACT.Copy)
            return nc.scalar.activation(halves(sq, half), ps[:, :, 0:half], ACT.Square)

        def rstd(act, out, ps, count, half):
            nc.scalar.activation(halves(out, half), ps[:, :, 0:half], ACT.Ln, bias=eps, scale=1.0 / count)
            act.drain()
            return nc.scalar.activation(out, out, ACT.Exp, scale=-0.5)

        def attention_act(act, S, pre, comps, scale, PT, PTp, probs, stats, turn):
            pes, acts, dves = S
            mx, nm, sm, rs = stats
            for t in range(QT + 1):
                if t < QT:
                    if t >= 2:
                        pes.wait(act, f"{pre}turned{t - 2}", turn)
                    for c in range(comps):
                        j = t * comps + c
                        s = psum[j % 2]
                        dves.wait(act, f"{pre}max{t}.{c}", turn)
                        if t < 4:
                            o, i = halves(probs[t % 2][c], TH), s[:, :, 0:TH]
                        else:
                            o, i = probs[t % 2][c][:, 0:P], s[:, 0, 0:P]
                        acts.mark(nc.scalar.activation(o, i, ACT.Exp, bias=nm[:, j:j + 1], scale=scale,
                                                       accum_out=sm[:, j:j + 1]), f"{pre}exp{t}.{c}")
                if t >= 1:
                    u = t - 1
                    pes.wait(act, f"{pre}turned{u}", turn)
                    d = psum[2 + u % 2]
                    if u < 4:
                        dst = PT.rearrange("p (k q) -> p k q", k=5)
                        nc.scalar.activation(dst[:, 0:4, u * P:(u + 1) * P],
                                             d[:, 0, :].rearrange("p (k q) -> p k q", k=4), ACT.Copy)
                        last = nc.scalar.activation(dst[:, 4, u * P:(u + 1) * P], d[:, 1, 0:P], ACT.Copy)
                    else:
                        last = nc.scalar.activation(PTp, d[:, 0, 0:P], ACT.Copy)
                    acts.mark(last, f"{pre}pt{u}")

        def attention_dve(dve, S, pre, comps, scale, probs, stats, turn):
            pes, acts, dves = S
            mx, nm, sm, rs = stats
            for t in range(QT + 1):
                if t < QT:
                    for c in range(comps):
                        j = t * comps + c
                        s = psum[j % 2]
                        pes.wait(dve, f"{pre}scores{t}.{c}", turn)
                        if t < 4:
                            nc.vector.tensor_reduce(mx[:, j:j + 1], s[:, :, 0:TH], AX.XY, ALU.max)
                        else:
                            nc.vector.tensor_reduce(mx[:, j:j + 1], s[:, 0, 0:P], AX.X, ALU.max)
                        dve.drain()
                        dves.mark(nc.vector.tensor_scalar(nm[:, j:j + 1], mx[:, j:j + 1], -scale, None, ALU.mult),
                                  f"{pre}max{t}.{c}")
                if t >= 1:
                    u = t - 1
                    n = T if u < 4 else P
                    j = u * comps
                    acts.wait(dve, f"{pre}exp{u}.{comps - 1}", turn)
                    nc.vector.reciprocal(rs[:, j:j + comps], sm[:, j:j + comps])
                    dve.drain()
                    p0 = probs[u % 2][0][:, 0:n]
                    last = nc.vector.tensor_scalar(p0, p0, rs[:, j:j + 1], None, ALU.mult)
                    if comps == 2:
                        nc.vector.tensor_scalar(rs[:, j + 1:j + 2], rs[:, j + 1:j + 2], neg_lambda, None, ALU.mult)
                        dve.drain()
                        last = nc.vector.scalar_tensor_tensor(p0, probs[u % 2][1][:, 0:n], rs[:, j + 1:j + 2], p0,
                                                              ALU.mult, ALU.add)
                    dves.mark(last, f"{pre}probs{u}")

        def normed(raw_, g, rs):
            return nc.vector.scalar_tensor_tensor(raw_, raw_, g, rs, ALU.mult, ALU.mult)

        def roped(dve, t_, ps, cos, sin, tmp):
            nc.vector.tensor_tensor(tmp, ps[:, 0, 0:NLAT], sin, ALU.mult)
            nc.vector.tensor_tensor(t_[:, NCTX:T], t_[:, NCTX:T], cos, ALU.mult)
            dve.drain()
            return nc.vector.tensor_tensor(t_[:, NCTX:T], t_[:, NCTX:T], tmp, ALU.add)

        def split(dve, hi, lo, src):
            nc.vector.tensor_copy(hi, src)
            dve.drain()
            return nc.vector.tensor_tensor(lo, src, hi.bitcast(F32), ALU.subtract)

        def split_head(dve, head):
            nc.vector.tensor_copy(act_hi[:, bass.ds(head * T + NCTX, NLAT)], psD[:, 0, 0:NLAT])
            nc.vector.tensor_copy(act_hi[:, bass.ds(head * T, NCTX)], psD[:, 1, 0:P])
            dve.drain()
            nc.vector.tensor_tensor(act_lo[:, bass.ds(head * T + NCTX, NLAT)], psD[:, 0, 0:NLAT],
                                    act_hi[:, bass.ds(head * T + NCTX, NLAT)].bitcast(F32), ALU.subtract)
            return nc.vector.tensor_tensor(act_lo[:, bass.ds(head * T, NCTX)], psD[:, 1, 0:P],
                                           act_hi[:, bass.ds(head * T, NCTX)].bitcast(F32), ALU.subtract)

        c = Carve()
        x_tok = c(QT * D)
        vec_rows = [c(P) for _ in range(4)]
        lam_row = c(256)
        lam_tmp = c(132)

        c = Carve()
        squares = c(KT * T)
        rms = c(T)

        c = Carve()
        mla_raw = [c(T) for _ in range(6)]
        mla_sq = [c(T) for _ in range(6)]
        mla_rs = mla_sq[0], mla_sq[3], mla_sq[5]
        mla_cache = c(2 * P)
        kr_cache = c(P)
        mla_tmp = c(NLAT)
        c = Carve()
        c(0)
        qn_t, qr_t = c(T), c(T)
        sq_n, sq_r = c(T), c(T)
        kn_t, vt_t, sq_k = c(NKEY), c(NKEY), c(NKEY)
        mV = c(6 * P)
        m_probs = [[c(T)], [c(T)]]
        m_PT, m_PTp = c(5 * NLAT), c(P)
        m_tmp = c(NLAT)
        m_stats = [c(QT) for _ in range(4)]
        kr_t = work[:, WORK - NKEY:WORK]
        mla_out = work[:, WORK - NKEY - 384:WORK - NKEY]
        assert c.at <= WORK - NKEY - 384

        c = Carve()
        dq_t, dk_t = c(T), c(NKEY)
        dsq_q, dsq_k = c(T), c(T)
        dvt = c(T)
        dV = c(6 * P)
        d_probs = [[c(T), c(T)], [c(T), c(T)]]
        d_PT, d_PTp = c(5 * NLAT), c(P)
        d_tmp = c(NLAT)
        d_cache = c(P)
        d_kout = c(P)
        d_stats = [c(2 * QT) for _ in range(4)]

        c = Carve()
        gk_t = [c(NKEY), c(NKEY)]
        gV = [c(6 * P), c(6 * P)]
        g_cache = [c(P), c(P)]
        g_kout = [c(P), c(P)]
        gsq, gvt = c(T), c(T)
        gq_t = c(T)
        g_probs = [[c(T)], [c(T)]]
        g_PT, g_PTp = c(5 * NLAT), c(P)
        g_tmp = c(NLAT)
        g_stats = [c(QT) for _ in range(4)]

        c = Carve()
        l_xp = c(LW + 4)
        l_gelu = c(T)
        l_y = c(LW)
        l_tr = [c(LW), c(LW)]
        l_ti = [c(LW), c(LW)]
        l_th = [c(LW), c(LW)]
        l_sq = [c(LW), c(LW)]
        l_a = [c(LW), c(LW)]
        l_h = [c(LW), c(LW)]
        sp2 = lru_small[:, 0:16]
        hb = lru_small[:, 16:48]
        l_state = lru_small[:, 48:64]
        l_s = lru_small[:, 64:144].rearrange("p (k n) -> p k n", k=5)

        c = Carve()
        gate_silu = c(T)
        prod = c(T)
        c = Carve()
        y_tok = c(QT * D)

        mixer_shift = lambda layer: mods[layer % 2]

        def mod_col(layer, kind, tile, cond):
            k = (kind * KT + tile) * 2 + cond
            return mods[layer % 2][:, k:k + 1]

        block = ctx.enter_context(nc.Block())

        @block.sync
        def _(sp):
            mod_count = [0]
            def mod_burst(layer, first, panels):
                w = a["w_mod"][layer].rearrange("(k p) n -> p k n", p=P)
                base = mod_count[0]
                mod_count[0] += panels
                with sp.Fori(0, panels // 2) as i:
                    for j in range(2):
                        if base:
                            sp.wait_ge(mod_used, i * 2 + (base + j - 1))
                        sp.dma_start(mod_raw[j][:, :].rearrange("p (k n) -> p k n", k=KT),
                                     w[:, :, bass.ds(i * 2 * P + (first + j) * P, P)]).then_inc(mod_in[j], 16)

            def panels(name, source):
                ph = phases[name]

                def turn(i):
                    for j, s in enumerate(ph.slots):
                        kts, cols = ph.shape[j]
                        if ph.first or True:
                            behind = ph.first + j + 1 - ph.n
                            if behind > 0:
                                sp.wait_ge(split_done, i * ph.n + behind)
                        sp.dma_start(raw[s][:, 0:kts * cols].rearrange("p (k n) -> p k n", k=kts),
                                     source(i, j)).then_inc(raw_in[s], 16)

                if ph.first:
                    with sp.Fori(0, ph.turns) as i:
                        turn(i)
                else:
                    turn(0)
                    with sp.Fori(1, ph.turns) as i:
                        for j, s in enumerate(ph.slots):
                            kts, cols = ph.shape[j]
                            sp.wait_ge(split_done, i * ph.n + (j + 1 - ph.n))
                            sp.dma_start(raw[s][:, 0:kts * cols].rearrange("p (k n) -> p k n", k=kts),
                                         source(i, j)).then_inc(raw_in[s], 16)

            mod_raw_first = True
            sp.dma_start(consts[:, :], a["consts"]).then_inc(const_in, 16)
            sp.wait_ge(const_in, 16)
            pre = PRE
            pre[2].wait(sp, "ready")
            flat = lambda ap, n: ap.rearrange("(r n) -> r n", n=n)
            rows = [("gn1", a["g_norm1"].rearrange("l (k n) -> (l k) n", n=P)),
                    ("gn2", a["g_norm2"].rearrange("l (k n) -> (l k) n", n=P)),
                    ("cq", a["mla_g_cq"].rearrange("l (k n) -> (l k) n", n=P)),
                    ("ckv", a["mla_g_ckv"].rearrange("l (k n) -> (l k) n", n=P)),
                    ("convb", a["lru_conv_b"].rearrange("l (k n) -> (l k) n", n=P)),
                    ("convw", a["lru_conv_w"].rearrange("l w (k n) -> (l w k) n", n=P)),
                    ("dsub", a["diff_g_sub"]),
                    ("gqk", a["gqa_g_qk"][0]),
                    ("mqk", a["mla_g_qk"][0][:, 0:P]),
                    ("bgate", a["lru_b_gate"].rearrange("l d g (k n) -> (l d g k) n", n=P)),
                    ("lam", a["lru_lambda"].rearrange("l d (k n) -> (l d k) n", n=P)),
                    ("h0", a["state_lru_h"].rearrange("b l d (k n) -> (b l d k) n", n=P)),
                    ("c", a["c"].rearrange("l (k n) -> (l k) n", n=P)),
                    ("cctx", a["c_ctx"].rearrange("(k n) -> k n", n=P))]
            n = 0
            for name, src in rows:
                r = VEC[name]
                tile = vec_rows[r // P]
                sp.dma_start(tile[r % P:r % P + src.shape[0], :], src).then_inc(const_in, 16)
                n += 1
            for half in range(2):
                for name, src in (("mqr", a["mla_g_qk"][0][:, P:P + 64]), ("dqk", a["diff_g_qk"][0])):
                    r = VEC[name]
                    sp.dma_start(vec_rows[0][r:r + 2, half * 64:half * 64 + 64], src).then_inc(const_in, 16)
                    n += 1
            bm = a["b_mod"].rearrange("l (k n) -> (l k) n", n=P)
            sp.dma_start(vec_rows[2][0:P, :], bm[0:P, :]).then_inc(const_in, 16)
            sp.dma_start(vec_rows[3][0:64, :], bm[P:192, :]).then_inc(const_in, 16)
            sp.dma_start(lam_row[0:1, :], a["diff_lambda"].rearrange("l a d -> l (a d)")).then_inc(const_in, 16)
            sp.dma_start(x_tok[:, 0:D], a["x_prompt"][0]).then_inc(x_in, 16)
            sp.dma_start(x_tok[:, D:QT * D].rearrange("p (t n) -> p t n", t=4),
                         a["x_sample"][0].rearrange("(t p) n -> p t n", p=P)).then_inc(x_in, 16)
            sp.dma_start(tables[:, :], a["tables"]).then_inc(const_in, 16)

            w = a["w_mod"][0].rearrange("(k p) n -> p k n", p=P)
            for j in range(2):
                sp.dma_start(mod_raw[j][:, :].rearrange("p (k n) -> p k n", k=KT),
                             w[:, :, j * P:(j + 1) * P]).then_inc(mod_in[j], 16)
            with sp.Fori(1, 24) as i:
                for j in range(2):
                    sp.wait_ge(mod_used, i * 2 + (j - 1))
                    sp.dma_start(mod_raw[j][:, :].rearrange("p (k n) -> p k n", k=KT),
                                 w[:, :, bass.ds(i * 2 * P + j * P, P)]).then_inc(mod_in[j], 16)
            mod_count[0] = 48

            for layer in range(DEPTH):
                if layer + 1 < DEPTH:
                    mod_burst(layer + 1, 0, 24)
                if layer == 0:
                    win = a["mla_w_in"][0].rearrange("(k p) n -> p k n", p=P)
                    uq = a["mla_w_uq"][0].rearrange("(k p) n -> p k n", p=P)
                    ukv = a["mla_w_ukv"][0].rearrange("(k p) n -> p k n", p=P)
                    wo = a["mla_w_o"][0]
                    ph = phases["mla_in"]
                    for t in range(6):
                        c0 = t * P if t < 5 else 576
                        if t >= 2:
                            sp.wait_ge(split_done, t - 1)
                        sp.dma_start(raw[t % 2][:, :].rearrange("p (k n) -> p k n", k=KT),
                                     win[:, :, c0:c0 + P]).then_inc(raw_in[t % 2], 16)
                    panels("mla", lambda i, j: uq[:, :, bass.ds(i * 192, 192)] if j == 0
                           else ukv[:, :, bass.ds(i * 256, 256)])
                elif layer == 1:
                    win = a["diff_w_in"][0].rearrange("(k p) n -> p k n", p=P)
                    wo = a["diff_w_o"][0]
                    kc = a["cache_diff_k"][0, 0].rearrange("t h c d -> t (h c d)")
                    vc = a["cache_diff_v"][0, 0].rearrange("t h d -> t (h d)")
                    panels("diff", lambda i, j: win[:, :, bass.ds(i * P + j * D, P)])
                elif layer == 2:
                    win = a["gqa_w_in"][0].rearrange("(k p) n -> p k n", p=P)
                    wo = a["gqa_w_o"][0]
                    panels("gqa_kv", lambda i, j: win[:, :, bass.ds(i * P + (D + j * 256), P)])
                    panels("gqa", lambda i, j: win[:, :, bass.ds(i * P + j * 512, P)])
                else:
                    win = a["lru_w_in"][0].rearrange("(k p) n -> p k n", p=P)
                    wo = a["lru_w_out"][0]
                    wg = a["lru_w_gate"][0].rearrange("d g b k j -> k (d g) b j")
                    panels("lru", lambda i, j: win[:, :, bass.ds(i * P + j * D, P)] if j < 2
                           else wg[:, :, bass.ds(i, 1), :].rearrange("k g o j -> k g (o j)"))
                wov = wo.rearrange("(k p) n -> p k n", p=P)
                panels(f"wo{layer}", lambda i, j: wov[:, :, bass.ds(i * 2 * P + j * P, P)])
                if layer + 1 < DEPTH:
                    mod_burst(layer + 1, 24, 24)
                f_in = a["w_ffn_in"][layer].rearrange("(k p) n -> p k n", p=P)
                f_out = a["w_ffn_out"][layer].rearrange("(k p) n -> p k n", p=P)
                m0 = 0
                for ch, size in enumerate(FFN_CHUNKS):
                    panels(f"in{layer}.{ch}", lambda i, j: f_in[:, :, bass.ds(i * P + (m0 * P + j * FFN), P)])
                    panels(f"out{layer}.{ch}", lambda i, j: f_out[:, m0:m0 + size, bass.ds(i * 2 * P + j * P, P)])
                    m0 += size

        @block.gpsimd
        def _(pool):
            def turn(name, i, peeled=False):
                ph = phases[name]
                for j, s in enumerate(ph.slots):
                    n = ph.shape[j][0] * ph.shape[j][1]
                    pool.wait_ge(raw_in[s], i * 16 + 16 * (ph.landed[s] + 1))
                    if not peeled:
                        pool.wait_ge(gemm_done, i * ph.n + (ph.first + j + 1 - ph.n))
                    nc.gpsimd.tensor_tensor(w_hi[s][:, 0:n], raw[s][:, 0:n], ones[:, 0:1].to_broadcast([P, n]),
                                            ALU.mult).then_inc(pool_hi, 1)
                    pool.wait_ge(pool_hi, i * ph.n + (ph.first + j + 1))
                    nc.gpsimd.tensor_tensor(w_lo[s][:, 0:n], raw[s][:, 0:n], w_hi[s][:, 0:n].bitcast(F32),
                                            ALU.subtract).then_inc(split_done, 1)

            pool.wait_ge(const_in, 16)
            for name, ph in phases.items():
                if ph.first == 0:
                    turn(name, 0, peeled=True)
                    with pool.Fori(1, ph.turns) as i:
                        turn(name, i)
                else:
                    with pool.Fori(0, ph.turns) as i:
                        turn(name, i)

        @block.tensor
        def _(pe):
            mod_count = [0, 0]

            def mod_burst(panels):
                base, burst = mod_count
                if burst:
                    pe.wait_ge(mod_ready, burst)
                with pe.Fori(0, panels // 2) as i:
                    for j in range(2):
                        pe.wait_ge(mod_in[j], i * 16 + 16 * (base // 2 + 1))
                        for kt in range(KT):
                            last = nc.tensor.matmul(psD[:, 1, bass.ds(i * 4 + j * 2, 2)],
                                                    mod_raw[j][:, kt * P:(kt + 1) * P],
                                                    silu_c[:, kt * 2:kt * 2 + 2], start=(kt == 0), stop=(kt == KT - 1))
                        last.then_inc(mod_used, 1)
                mod_count[0] += panels
                mod_count[1] += 1

            def norm(n):
                for kt in range(KT):
                    pe.wait_ge(square_done, n * KT + kt + 1)
                    for b in range(2):
                        last = nc.tensor.matmul(psC[:, b, 0:TH], ones, squares[:, kt * T + b * TH:kt * T + (b + 1) * TH],
                                                start=(kt == 0), stop=(kt == KT - 1))
                last.then_inc(sums_done, 1)

            x_tiles = [KT]

            def project(name, kts, src_ready=None):
                base = x_tiles[0]
                with pe.Fori(0, KT // 2) as i:
                    for j in range(2):
                        slot = take_panel(pe, name, i, j)
                        pe.wait_ge(x_done, i * 2 + (base + j - 1))
                        products(pe, psum[j], slot, kts, P, 0, act_hi, act_lo, 0, T, TH).then_inc(gemm_done, 1)
                x_tiles[0] += KT

            pes, acts, dves = PRE
            pe.wait_ge(const_in, 16 * 23)
            for k in range(2):
                last = nc.tensor.transpose(psC[:, 0, k * P:(k + 1) * P], vec_rows[k], ident)
            pes.mark(last, "vecs")
            nc.tensor.transpose(psD[:, 0, 0:P], vec_rows[2], ident)
            pes.mark(nc.tensor.transpose(psD[:, 0, P:2 * P], vec_rows[3], ident), "bmod")
            dves.wait(pe, "lamdiff")
            pes.mark(nc.tensor.matmul(psC[:, 1, 0:1], ones[0:1, :], lam_tmp[0:1, 4:5], start=True, stop=True), "lam")
            pe.wait_ge(x_in, 32)
            for kt in range(KT):
                if kt >= 2:
                    pe.wait_ge(x_done, kt - 1)
                d = psum[kt % 2]
                for t in range(QT):
                    last = nc.tensor.transpose(d[:, t // 4, (t % 4) * P:(t % 4 + 1) * P],
                                               x_tok[:, t * D + kt * P:t * D + (kt + 1) * P], ident)
                pes.mark(last, f"x{kt}")
            acts.wait(pe, "silu")
            dves.wait(pe, "bmod")
            mod_burst(48)
            last = None
            nc.tensor.matmul(psD[:, 1, 500:501], ones, small[:, 40:41], start=True, stop=True).then_inc(mod_done, 1)

            for layer in range(DEPTH):
                norm(2 * layer)
                if layer + 1 < DEPTH:
                    mod_burst(24)
                    nc.tensor.matmul(psD[:, 1, 500:501], ones, small[:, 40:41], start=True, stop=True).then_inc(mod_done, 1)
                    pe.wait_ge(mod_ready, mod_count[1])
                else:
                    pe.wait_ge(mod_ready, mod_count[1])
                pe.wait_ge(h_done, (2 * layer + 1) * KT)

                def h_tile(out, name, i, j):
                    slot = take_panel(pe, name, i, j)
                    return products(pe, out, slot, KT, P, 0, h_hi, h_lo, 0, T, TH)

                if layer == 0:
                    S = MIN
                    pes, acts, dves = S
                    for t in range(6):
                        if t >= 2:
                            acts.wait(pe, f"m{t - 2}")
                        h_tile(psum[t % 2], "mla_in", t // 2, t % 2).then_inc(gemm_done, 1)
                    acts.wait(pe, "m2")
                    pes.mark(sum_rows(psC, ones, mla_sq[0:3], TH), "sscq")
                    acts.wait(pe, "m4")
                    pes.mark(sum_rows(psD, ones, mla_sq[3:5], TH), "ssckv")
                    acts.wait(pe, "m5")
                    pes.mark(sum_rows(psA, blocks, mla_sq[5:6], TH), "sskr")
                    dves.wait(pe, "kr")
                    pes.mark(nc.tensor.matmul(psB[:, 0, 0:NLAT], rot64, kr_t[:, NCTX:T], start=True, stop=True), "rotkr")
                    pe.wait_ge(const_in, 16 * 25)
                    nc.tensor.transpose(psC[:, 0, 0:P], mla_cache[:, 0:P], ident)
                    nc.tensor.transpose(psC[:, 0, P:2 * P], mla_cache[:, P:2 * P], ident)
                    nc.tensor.transpose(psC[:, 0, 2 * P:3 * P], kr_cache, ident)
                    nc.tensor.transpose(psD[:, 0, 0:P], mla_raw[3][:, 0:P], ident)
                    nc.tensor.transpose(psD[:, 0, P:2 * P], mla_raw[4][:, 0:P], ident)
                    pes.mark(nc.tensor.transpose(psD[:, 0, 2 * P:3 * P], kr_t[:, 0:P], ident), "turned")
                    dves.wait(pe, "cache")
                    acts.wait(pe, "outs")
                    S = MLA
                    pes, acts, dves = S
                    pes.open(pe)
                    with pe.Fori(0, HEADS) as i:
                        dves.wait_turns(pe, i)
                        uq = take_panel(pe, "mla", i, 0)
                        pes.mark(products(pe, psA, uq, 3, 192, 0, h_hi, h_lo, CQ_AT, T, TH), "gqn")
                        products(pe, psB, uq, 3, 192, 64, h_hi, h_lo, CQ_AT, T, TH).then_inc(gemm_done, 1)
                        ukv = take_panel(pe, "mla", i, 1)
                        pes.mark(products(pe, psC, ukv, 2, 256, 0, h_hi, h_lo, CKV_AT, NKEY, NKEY // 2), "gkn")
                        products(pe, psD, ukv, 2, 256, P, h_hi, h_lo, CKV_AT, NKEY, NKEY // 2).then_inc(gemm_done, 1)
                        acts.wait(pe, "evqn", i)
                        pes.mark(sum_rows(psA, ones, [sq_n], TH), "ssqn")
                        acts.wait(pe, "evqr", i)
                        pes.mark(sum_rows(psB, blocks, [sq_r], TH), "ssqr")
                        acts.wait(pe, "evkn", i)
                        pes.mark(sum_rows(psC, ones, [sq_k], NKEY // 2), "sskn")
                        dves.wait(pe, "qr", i)
                        pes.mark(nc.tensor.matmul(psB[:, 0, 0:NLAT], rot64, qr_t[:, NCTX:T], start=True, stop=True),
                                 "rotqr")
                        acts.wait(pe, "evv", i)
                        for k in range(6):
                            last = nc.tensor.transpose(psD[:, k // 4, (k % 4) * P:(k % 4 + 1) * P],
                                                       vt_t[:, k * P:(k + 1) * P], ident)
                        pes.mark(last, "turned_v")
                        dves.wait(pe, "qroped", i)
                        acts.wait(pe, "v", i)
                        attention_pe(pe, S, "", 1, [[(qn_t, kn_t), (qr_t[64:P], kr_t[64:P])]], mV, m_PT, m_PTp,
                                     m_probs, i)
                elif layer == 1:
                    S = DIF
                    pes, acts, dves = S
                    pes.open(pe)
                    with pe.Fori(0, HEADS) as i:
                        dves.wait_turns(pe, i)
                        h_tile(psA, "diff", i, 0).then_inc(gemm_done, 1)
                        h_tile(psB, "diff", i, 1).then_inc(gemm_done, 1)
                        acts.wait(pe, "evq", i)
                        pes.mark(sum_rows(psC, blocks, [dsq_q], TH), "ssq")
                        h_tile(psA, "diff", i, 2).then_inc(gemm_done, 1)
                        acts.wait(pe, "evk", i)
                        pes.mark(sum_rows(psD, blocks, [dsq_k], TH), "ssk")
                        dves.wait(pe, "q", i)
                        pes.mark(nc.tensor.matmul(psC[:, 0, 0:NLAT], rot64, dq_t[:, NCTX:T], start=True, stop=True),
                                 "rotq")
                        dves.wait(pe, "k", i)
                        pes.mark(nc.tensor.matmul(psD[:, 0, 0:NLAT], rot64, dk_t[:, NCTX:T], start=True, stop=True),
                                 "rotk")
                        acts.wait(pe, "evv", i)
                        pe.wait_ge(cache_in, i * 32 + 16 * (2))
                        for k in range(1, 5):
                            nc.tensor.transpose(psA[:, 0, (k - 1) * P:k * P], dvt[:, k * P:(k + 1) * P], ident)
                        nc.tensor.transpose(psA[:, 1, 0:P], dvt[:, 0:P], ident)
                        nc.tensor.transpose(psA[:, 1, P:2 * P], d_cache, ident)
                        pes.mark(nc.tensor.transpose(psA[:, 1, 2 * P:3 * P], dk_t[:, 0:P], ident), "turned_v")
                        dves.wait(pe, "kroped", i)
                        acts.wait(pe, "v", i)
                        attention_pe(pe, S, "", 2, [[(dq_t[0:64], dk_t[0:64])], [(dq_t[64:P], dk_t[64:P])]],
                                     dV, d_PT, d_PTp, d_probs, i)
                        acts.wait(pe, "evo", i)
                        pes.mark(sum_rows(psC, ones, [dsq_q], TH), "sso")
                elif layer == 2:
                    S = GKV
                    pes, acts, dves = S
                    for j in range(2):
                        h_tile(psA, "gqa_kv", j, 0).then_inc(gemm_done, 1)
                        h_tile(psB, "gqa_kv", j, 1).then_inc(gemm_done, 1)
                        acts.wait(pe, "evk", j)
                        pes.mark(sum_rows(psC, ones, [gsq], TH), "ssk")
                        dves.wait(pe, "k", j)
                        pes.mark(nc.tensor.matmul(psC[:, 0, 0:NLAT], rot128, gk_t[j][:, NCTX:T], start=True, stop=True),
                                 "rotk")
                        acts.wait(pe, "evv", j)
                        pe.wait_ge(gcache_in, 16 * 4)
                        for k in range(1, 5):
                            nc.tensor.transpose(psD[:, 0, (k - 1) * P:k * P], gvt[:, k * P:(k + 1) * P], ident)
                        nc.tensor.transpose(psD[:, 1, 0:P], gvt[:, 0:P], ident)
                        nc.tensor.transpose(psD[:, 1, P:2 * P], g_cache[j], ident)
                        pes.mark(nc.tensor.transpose(psD[:, 1, 2 * P:3 * P], gk_t[j][:, 0:P], ident), "turned_v")
                        dves.wait(pe, "kroped", j)
                        acts.wait(pe, "v", j)
                    S = GQA
                    pes, acts, dves = S
                    pes.open(pe)
                    with pe.Fori(0, HEADS // 2) as i:
                        for k, p in enumerate("ab"):
                            if k == 0:
                                dves.wait_turns(pe, i)
                            else:
                                dves.wait(pe, "ao", i)
                            h_tile(psA, "gqa", i, k).then_inc(gemm_done, 1)
                            acts.wait(pe, p + "evq", i)
                            pes.mark(sum_rows(psC, ones, [gsq], TH), p + "ssq")
                            dves.wait(pe, p + "q", i)
                            pes.mark(nc.tensor.matmul(psC[:, 0, 0:NLAT], rot128, gq_t[:, NCTX:T],
                                                      start=True, stop=True), p + "rotq")
                            dves.wait(pe, p + "qroped", i)
                            attention_pe(pe, S, p, 1, [[(gq_t, gk_t[k])]], gV[k], g_PT, g_PTp, g_probs, i)
                else:
                    S = LRU
                    pes, acts, dves = S
                    pes.open(pe)
                    with pe.Fori(0, KT) as i:
                        acts.wait_turns(pe, i)
                        h_tile(psA, "lru", i, 0).then_inc(gemm_done, 1)
                        h_tile(psB, "lru", i, 1).then_inc(gemm_done, 1)
                        slot = take_panel(pe, "lru", i, 2)
                        dves.wait(pe, "y", i)
                        for g, name in enumerate(("rf", "if", "rb", None)):
                            ps = psum[g]
                            for p_, (w, r) in enumerate(((w_hi, y_hi), (w_hi, y_lo), (w_lo, y_hi))):
                                for b in range(2):
                                    last = nc.tensor.matmul(ps[:, b, 0:LW // 2], w[slot][:, g * P:(g + 1) * P],
                                                            r[:, b * (LW // 2):(b + 1) * (LW // 2)],
                                                            start=(p_ == 0), stop=(p_ == 2))
                            if name:
                                pes.mark(last, name)
                            else:
                                last.then_inc(gemm_done, 1)
                if layer < 3:
                    dves.wait_turns(pe, len_turns(layer))
                else:
                    dves.wait_turns(pe, KT)
                project(f"wo{layer}", KT)

                norm(2 * layer + 1)
                if layer + 1 < DEPTH:
                    mod_burst(24)
                    nc.tensor.matmul(psD[:, 1, 500:501], ones, small[:, 40:41], start=True, stop=True).then_inc(mod_done, 1)
                pe.wait_ge(h_done, (2 * layer + 2) * KT)
                for ch, size in enumerate(FFN_CHUNKS):
                    base = layer * (FFN // P) + sum(FFN_CHUNKS[:ch])
                    pe.wait_ge(x_done, x_tiles[0])
                    with pe.Fori(0, size) as i:
                        pe.wait_ge(silu_done, i + (base + 1))
                        h_tile(psA, f"in{layer}.{ch}", i, 0).then_inc(gemm_done, 1)
                        pe.wait_ge(hidden_done, i + (base + 1))
                        h_tile(psB, f"in{layer}.{ch}", i, 1).then_inc(gemm_done, 1)
                    pe.wait_ge(hidden_done, base + size + 1)
                    project(f"out{layer}.{ch}", size)

            pe.wait_ge(x_done, x_tiles[0])
            for t in range(QT):
                if t >= 2:
                    pe.wait_ge(y_copied, t - 1)
                d = psum[t % 2]
                for kt in range(KT):
                    last = nc.tensor.transpose(d[:, kt // 4, (kt % 4) * P:(kt % 4 + 1) * P],
                                               x[:, kt * T + t * P:kt * T + (t + 1) * P], ident)
                last.then_inc(y_turned, 1)

        @block.scalar
        def _(act):
            pes, acts, dves = PRE
            pes.wait(act, "vecs")
            act.sem_inc(silu_done, 1)
            acts.mark(nc.scalar.activation(vecs[:, :], psC[:, 0, 0:2 * P], ACT.Copy), "vecs")
            act.drain()
            sc = silu_c[:, :].rearrange("p (k c) -> p k c", c=2)
            nc.scalar.activation(sc[:, :, 0], vecs[:, VEC["cctx"]:VEC["cctx"] + KT], ACT.Silu)
            acts.mark(nc.scalar.activation(sc[:, :, 1], vecs[:, VEC["c"]:VEC["c"] + KT], ACT.Silu), "silu")
            dves.wait(act, "lamsum")
            acts.mark(nc.scalar.activation(lam_tmp[0:1, 2:4], lam_tmp[0:1, 0:2], ACT.Exp), "lamexp")
            nc.scalar.activation(l_s[:, 0, :].bitcast(F32) if False else lru_small[:, 64:80],
                                 vecs[:, VEC["lam"]:VEC["lam"] + 16], ACT.Abs)
            act.drain()
            acts.mark(nc.scalar.activation(lru_small[:, 80:96], lru_small[:, 64:80], ACT.Exp, scale=-1.0), "sp")

            x_tiles = [KT]
            outs = [0]

            def norm(n):
                layer, which = n // 2, n % 2
                act.wait_ge(x_done, x_tiles[0])
                if outs[0]:
                    act.wait_ge(outs_done, outs[0])
                for kt in range(KT):
                    nc.scalar.activation(squares[:, kt * T:(kt + 1) * T], x[:, kt * T:(kt + 1) * T],
                                         ACT.Square).then_inc(square_done, 1)
                act.wait_ge(sums_done, n + 1)
                rstd(act, rms, psC, D, TH).then_inc(rstd_done, 1)
                for kt in range(KT):
                    act.wait_ge(scaled_done, n * KT + kt + 1)
                    for cond, (t0, t1) in enumerate(((0, NCTX), (NCTX, T))):
                        last = nc.scalar.activation(h_hi[:, kt * T + t0:kt * T + t1],
                                                    squares[:, kt * T + t0:kt * T + t1], ACT.Identity,
                                                    bias=mod_col(layer, 3 * which, kt, cond))
                    last.then_inc(h_hi_done, 1)
                act.wait_ge(h_done, (n + 1) * KT)

            def g_panel(name, i, j):
                act.wait_ge(gemm_done, phases[name].number(i, j))

            for layer in range(DEPTH):
                norm(2 * layer)
                if layer == 0:
                    S = MIN
                    pes, acts, dves = S
                    act.dma_start(mla_cache, a["cache_mla_ckv"][0, 0]).then_inc(const_in, 16)
                    dves_pre = PRE[2]
                    act.wait_ge(kr_cleared, 1)
                    act.dma_start(kr_cache[:, 64:P], a["cache_mla_krope"][0, 0]).then_inc(const_in, 16)
                    for t in range(6):
                        g_panel("mla_in", t // 2, t % 2)
                        acts.mark(evacuate(mla_raw[t], mla_sq[t], psum[t % 2], TH), f"m{t}")
                    pes.wait(act, "sscq")
                    acts.mark(rstd(act, mla_rs[0], psC, MLA_QR, TH), "rscq")
                    pes.wait(act, "ssckv")
                    acts.mark(rstd(act, mla_rs[1], psD, MLA_KVR, TH), "rsckv")
                    pes.wait(act, "sskr")
                    acts.mark(rstd(act, mla_rs[2], psA, 64, TH), "rskr")
                    pes.wait(act, "turned")
                    acts.mark(nc.scalar.activation(mla_out, psD[:, 0, 0:3 * P], ACT.Copy), "outs")
                    act.wait_ge(acts.sem, len(acts.names))
                    act.dma_start(a["new_mla_ckv"][0, 0], mla_out[:, 0:2 * P]).then_inc(outs_done, 16)
                    act.dma_start(a["new_mla_krope"][0, 0], mla_out[:, 2 * P + 64:3 * P]).then_inc(outs_done, 16)
                    outs[0] = 32
                    S = MLA
                    pes, acts, dves = S
                    acts.open(act)
                    act.wait_ge(MIN[2].sem, len(MIN[2].names))
                    act.wait_ge(outs_done, 32)
                    with act.Fori(0, HEADS) as i:
                        pes.wait(act, "gqn", i)
                        acts.mark(evacuate(qn_t, sq_n, psA, TH), "evqn")
                        g_panel("mla", i, 0)
                        acts.mark(evacuate(qr_t, sq_r, psB, TH), "evqr")
                        pes.wait(act, "gkn", i)
                        acts.mark(evacuate(kn_t, sq_k, psC, NKEY // 2), "evkn")
                        g_panel("mla", i, 1)
                        acts.mark(nc.scalar.activation(halves(vt_t, NKEY // 2), psD[:, :, 0:NKEY // 2], ACT.Copy),
                                  "evv")
                        pes.wait(act, "ssqn", i)
                        acts.mark(rstd(act, sq_n, psA, P, TH), "rsqn")
                        pes.wait(act, "ssqr", i)
                        acts.mark(rstd(act, sq_r, psB, 64, TH), "rsqr")
                        pes.wait(act, "sskn", i)
                        acts.mark(rstd(act, sq_k, psC, P, NKEY // 2), "rskn")
                        pes.wait(act, "turned_v", i)
                        nc.scalar.activation(mV[:, 0:4 * P], psD[:, 0, :], ACT.Copy)
                        acts.mark(nc.scalar.activation(mV[:, 4 * P:6 * P], psD[:, 1, 0:2 * P], ACT.Copy), "v")
                        attention_act(act, S, "", 1, 192 ** -0.5, m_PT, m_PTp, m_probs, m_stats, i)
                        pes.wait(act, "pv", i)
                elif layer == 1:
                    S = DIF
                    pes, acts, dves = S
                    acts.open(act)
                    kc = a["cache_diff_k"][0, 0].rearrange("t h c d -> t (h c d)")
                    vc = a["cache_diff_v"][0, 0].rearrange("t h d -> t (h d)")
                    ko = a["new_diff_k"][0, 0].rearrange("t h c d -> t (h c d)")
                    vo = a["new_diff_v"][0, 0].rearrange("t h d -> t (h d)")
                    with act.Fori(0, HEADS) as i:
                        act.wait_ge(outs_done, i * 32 + 32)
                        act.dma_start(d_cache, kc[:, bass.ds(i * P, P)]).then_inc(cache_in, 16)
                        act.dma_start(dV[:, 5 * P:6 * P], vc[:, bass.ds(i * P, P)]).then_inc(cache_in, 16)
                        g_panel("diff", i, 0)
                        acts.mark(evacuate(dq_t, dsq_q, psA, TH), "evq")
                        g_panel("diff", i, 1)
                        acts.mark(evacuate(dk_t[:, 0:T], dsq_k, psB, TH), "evk")
                        pes.wait(act, "ssq", i)
                        acts.mark(rstd(act, dsq_q, psC, 64, TH), "rsq")
                        g_panel("diff", i, 2)
                        acts.mark(nc.scalar.activation(halves(dvt, TH), psA[:, :, 0:TH], ACT.Copy), "evv")
                        pes.wait(act, "ssk", i)
                        acts.mark(rstd(act, dsq_k, psD, 64, TH), "rsk")
                        pes.wait(act, "turned_v", i)
                        nc.scalar.activation(dV[:, P:5 * P], psA[:, 0, :], ACT.Copy)
                        nc.scalar.activation(dV[:, 0:P], psA[:, 1, 0:P], ACT.Copy)
                        nc.scalar.activation(dk_t[:, T:NKEY], psA[:, 1, P:2 * P], ACT.Copy)
                        acts.mark(nc.scalar.activation(d_kout, psA[:, 1, 2 * P:3 * P], ACT.Copy), "v")
                        acts.wait(act, "v", i)
                        act.dma_start(ko[:, bass.ds(i * P, P)], d_kout).then_inc(outs_done, 16)
                        act.dma_start(vo[:, bass.ds(i * P, P)], dV[:, 0:P]).then_inc(outs_done, 16)
                        attention_act(act, S, "", 2, 64 ** -0.5, d_PT, d_PTp, d_probs, d_stats, i)
                        pes.wait(act, "pv", i)
                        nc.scalar.activation(dq_t[:, NCTX:T], psD[:, 0, 0:NLAT], ACT.Copy)
                        nc.scalar.activation(dq_t[:, 0:NCTX], psD[:, 1, 0:P], ACT.Copy)
                        nc.scalar.activation(dsq_q[:, NCTX:T], psD[:, 0, 0:NLAT], ACT.Square)
                        acts.mark(nc.scalar.activation(dsq_q[:, 0:NCTX], psD[:, 1, 0:P], ACT.Square), "evo")
                        pes.wait(act, "sso", i)
                        acts.mark(rstd(act, dsq_q, psC, P, TH), "rso")
                        dves.wait(act, "o", i)
                    outs[0] += 32 * HEADS
                elif layer == 2:
                    S = GKV
                    pes, acts, dves = S
                    kc = a["cache_gqa_k"][0, 0]
                    vc = a["cache_gqa_v"][0, 0]
                    act.wait_ge(outs_done, outs[0])
                    for j in range(2):
                        act.dma_start(g_cache[j], kc[:, j, :]).then_inc(gcache_in, 16)
                        act.dma_start(gV[j][:, 5 * P:6 * P], vc[:, j, :]).then_inc(gcache_in, 16)
                    for j in range(2):
                        g_panel("gqa_kv", j, 0)
                        acts.mark(evacuate(gk_t[j][:, 0:T], gsq, psA, TH), "evk")
                        g_panel("gqa_kv", j, 1)
                        acts.mark(nc.scalar.activation(halves(gvt, TH), psB[:, :, 0:TH], ACT.Copy), "evv")
                        pes.wait(act, "ssk", j)
                        acts.mark(rstd(act, gsq, psC, P, TH), "rsk")
                        pes.wait(act, "turned_v", j)
                        nc.scalar.activation(gV[j][:, P:5 * P], psD[:, 0, :], ACT.Copy)
                        nc.scalar.activation(gV[j][:, 0:P], psD[:, 1, 0:P], ACT.Copy)
                        nc.scalar.activation(gk_t[j][:, T:NKEY], psD[:, 1, P:2 * P], ACT.Copy)
                        acts.mark(nc.scalar.activation(g_kout[j], psD[:, 1, 2 * P:3 * P], ACT.Copy), "v")
                        acts.wait(act, "v", j)
                        act.dma_start(a["new_gqa_k"][0, 0][:, j, :], g_kout[j]).then_inc(outs_done, 16)
                        act.dma_start(a["new_gqa_v"][0, 0][:, j, :], gV[j][:, 0:P]).then_inc(outs_done, 16)
                        dves.wait(act, "k", j)
                    outs[0] += 64
                    S = GQA
                    pes, acts, dves = S
                    acts.open(act)
                    with act.Fori(0, HEADS // 2) as i:
                        for k, p in enumerate("ab"):
                            g_panel("gqa", i, k)
                            acts.mark(evacuate(gq_t, gsq, psA, TH), p + "evq")
                            pes.wait(act, p + "ssq", i)
                            acts.mark(rstd(act, gsq, psC, P, TH), p + "rsq")
                            attention_act(act, S, p, 1, P ** -0.5, g_PT, g_PTp, g_probs, g_stats, i)
                            pes.wait(act, p + "pv", i)
                else:
                    S = LRU
                    pes, acts, dves = S
                    acts.open(act)
                    act.wait_ge(outs_done, outs[0])
                    act.wait_ge(lru_ready, 1)
                    with act.Fori(0, KT) as i:
                        dves.wait_turns(act, i)
                        g_panel("lru", i, 0)
                        acts.mark(nc.scalar.activation(halves(l_gelu, TH), psA[:, :, 0:TH], ACT.Gelu_apprx_tanh),
                                  "gelu")
                        g_panel("lru", i, 1)
                        nc.scalar.activation(l_xp[:, 1:1 + NCTX], psB[:, 0, 0:NCTX], ACT.Copy)
                        nc.scalar.activation(l_xp[:, LAT0 + 1:LAT0 + 1 + TH - NCTX], psB[:, 0, NCTX:TH], ACT.Copy)
                        acts.mark(nc.scalar.activation(l_xp[:, LAT0 + 1 + TH - NCTX:LAT0 + 1 + NLAT], psB[:, 1, 0:TH],
                                                       ACT.Copy), "xp")
                        hw = LW // 2
                        for d, name in enumerate(("tf", "tb")):
                            if d == 0:
                                pes.wait(act, "if", i)
                            else:
                                g_panel("lru", i, 2)
                            for g, dst in enumerate((l_tr[d], l_ti[d])):
                                last = nc.scalar.activation(halves(dst, hw), psum[2 * d + g][:, :, 0:hw], ACT.Tanh,
                                                            bias=hb[:, bass.ds(i + (2 * d + g) * KT, 1)], scale=0.5)
                            acts.mark(last, name)
                        act.drain()
                        for d in range(2):
                            s_ = sp2[:, bass.ds(i + d * KT, 1)]
                            last = nc.scalar.activation(l_th[d], l_tr[d], ACT.Tanh, bias=s_, scale=s_)
                        acts.mark(last, "th")
                        act.drain()
                        for d in range(2):
                            last = nc.scalar.activation(l_sq[d], l_th[d], ACT.Sqrt)
                        acts.mark(last, "sq")
                x_tiles[0] += KT
                norm(2 * layer + 1)
                if layer == 3:
                    with nc.allow_non_contiguous_dma(reason="1024 floats per direction"):
                        act.dma_start(a["new_lru_h"][0, 0].rearrange("d (k p) -> p d k", p=P),
                                      l_state.rearrange("p (d k) -> p d k", d=2)).then_inc(outs_done, 16)
                    outs[0] += 16
                for ch, size in enumerate(FFN_CHUNKS):
                    base = layer * (FFN // P) + sum(FFN_CHUNKS[:ch])
                    with act.Fori(0, size) as i:
                        g_panel(f"in{layer}.{ch}", i, 0)
                        act.wait_ge(hidden_done, i + (base + 1))
                        nc.scalar.activation(halves(gate_silu, TH), psA[:, :, 0:TH], ACT.Silu).then_inc(silu_done, 1)
                    x_tiles[0] += KT
            for t in range(QT):
                act.wait_ge(y_turned, t + 1)
                nc.scalar.activation(y_tok[:, t * D:(t + 1) * D].rearrange("p (b n) -> p b n", b=2),
                                     psum[t % 2][:, :, :], ACT.Copy).then_inc(y_copied, 1)
                act.wait_ge(y_copied, t + 1)
                dst = a["y_prompt"][0] if t == 0 else a["y_sample"][0, (t - 1) * P:t * P, :]
                act.dma_start(dst, y_tok[:, t * D:(t + 1) * D]).then_inc(y_out, 16)
            act.wait_ge(y_out, 16 * QT)
            act.wait_ge(outs_done, outs[0])

        @block.vector
        def _(dve):
            pes, acts, dves = PRE
            dve.sem_inc(hidden_done, 1)
            for k in range(4):
                last = nc.vector.memset(vec_rows[k], 0.0)
            nc.vector.memset(eps, EPS)
            dve.drain()
            dves.mark(nc.vector.memset(lam_tmp[:, :], 0.0), "ready")
            dve.drain()
            dve.wait_ge(const_in, 16 * 23)
            lr = lam_row[0:1, :].rearrange("p (a b d) -> p a b d", a=2, b=2)
            nc.vector.tensor_tensor(lam_tmp[0:1, 4:132].rearrange("p (a d) -> p a d", a=2), lr[:, :, 0, :],
                                    lr[:, :, 1, :], ALU.mult)
            dve.drain()
            dves.mark(nc.vector.tensor_reduce(lam_tmp[0:1, 0:2],
                                              lam_tmp[0:1, 4:132].rearrange("p (a d) -> p a d", a=2),
                                              AX.X, ALU.add), "lamsum")
            acts.wait(dve, "lamexp")
            nc.vector.tensor_tensor(lam_tmp[0:1, 4:5], lam_tmp[0:1, 3:4], lam_tmp[0:1, 2:3], ALU.subtract)
            dve.drain()
            dves.mark(nc.vector.tensor_scalar(lam_tmp[0:1, 4:5], lam_tmp[0:1, 4:5], -LAMBDA_INIT, None, ALU.add),
                      "lamdiff")
            pes.wait(dve, "lam")
            dves.mark(nc.vector.tensor_copy(neg_lambda, psC[:, 1, 0:1]), "lamall")
            pes.wait(dve, "bmod")
            dves.mark(nc.vector.tensor_copy(bmod[:, :], psD[:, 0, 0:192]), "bmod")
            acts.wait(dve, "sp")
            ys, s_, s2, acc, tmp = (lru_small[:, 80 + 16 * k:96 + 16 * k] for k in range(5))
            nc.vector.tensor_scalar(tmp, ys, 2.0, None, ALU.add)
            dve.drain()
            nc.vector.reciprocal(tmp, tmp)
            dve.drain()
            nc.vector.tensor_tensor(s_, ys, tmp, ALU.mult)
            dve.drain()
            nc.vector.tensor_tensor(s2, s_, s_, ALU.mult)
            nc.vector.memset(acc, 1.0 / 17)
            dve.drain()
            for k in (15, 13, 11, 9, 7, 5, 3, 1):
                nc.vector.tensor_tensor(acc, acc, s2, ALU.mult)
                dve.drain()
                nc.vector.tensor_scalar(acc, acc, 1.0 / k, None, ALU.add)
                dve.drain()
            nc.vector.tensor_tensor(acc, acc, s_, ALU.mult)
            nc.vector.tensor_scalar(tmp, vecs[:, VEC["lam"]:VEC["lam"] + 16], -1.0, 0.0, ALU.mult, ALU.max)
            dve.drain()
            nc.vector.tensor_scalar(tmp, tmp, 2.0, None, ALU.mult)
            dve.drain()
            nc.vector.scalar_tensor_tensor(sp2, acc, 4.0, tmp, ALU.mult, ALU.add)
            nc.vector.tensor_scalar(hb, vecs[:, VEC["bgate"]:VEC["bgate"] + 32], 0.5, None, ALU.mult)
            dves.mark(nc.vector.tensor_scalar(small[:, 43:44], vecs[:, VEC["dsub"]:VEC["dsub"] + 1],
                                              1.0 - LAMBDA_INIT, None, ALU.mult), "splog")
            dve.drain()

            def vec(name, k=0, n=1):
                return vecs[:, VEC[name] + k:VEC[name] + k + n]

            for kt in range(KT):
                pes.wait(dve, f"x{kt}")
                nc.vector.tensor_copy(x[:, kt * T:kt * T + 4 * P], psum[kt % 2][:, 0, :])
                nc.vector.tensor_copy(x[:, kt * T + 4 * P:(kt + 1) * T], psum[kt % 2][:, 1, 0:P]).then_inc(x_done, 1)
            x_tiles = [KT]
            bursts = [0]

            def mod_take(layer, first, panels):
                bursts[0] += 1
                dve.wait_ge(mod_done, bursts[0])
                m = mods[layer % 2][:, first * 2:(first + panels) * 2].rearrange("p (k c) -> p k c", c=2)
                s = psD[:, 1, 0:panels * 2].rearrange("p (k c) -> p k c", c=2)
                for cond in range(2):
                    last = nc.vector.tensor_tensor(m[:, :, cond], s[:, :, cond],
                                                   bmod[:, layer * 48 + first:layer * 48 + first + panels], ALU.add)
                last.then_inc(mod_ready, 1)
                dve.drain()

            def norm(n):
                layer, which = n // 2, n % 2
                m = mods[layer % 2][:, :].rearrange("p (v k c) -> p v k c", v=6, c=2)
                for cond in range(2):
                    nc.vector.scalar_tensor_tensor(gains[:, cond * KT:(cond + 1) * KT], m[:, 3 * which + 1, :, cond],
                                                   1.0, vec("gn1" if which == 0 else "gn2", layer * KT, KT),
                                                   ALU.add, ALU.mult)
                dve.drain()
                dve.wait_ge(rstd_done, n + 1)
                for kt in range(KT):
                    for cond, (t0, t1) in enumerate(((0, NCTX), (NCTX, T))):
                        last = nc.vector.scalar_tensor_tensor(
                            squares[:, kt * T + t0:kt * T + t1], x[:, kt * T + t0:kt * T + t1],
                            gains[:, cond * KT + kt:cond * KT + kt + 1], rms[:, t0:t1], ALU.mult, ALU.mult)
                    last.then_inc(scaled_done, 1)
                for kt in range(KT):
                    dve.wait_ge(h_hi_done, n * KT + kt + 1)
                    for cond, (t0, t1) in enumerate(((0, NCTX), (NCTX, T))):
                        o = kt * T
                        last = nc.vector.scalar_tensor_tensor(
                            h_lo[:, o + t0:o + t1], squares[:, o + t0:o + t1], mod_col(layer, 3 * which, kt, cond),
                            h_hi[:, o + t0:o + t1].bitcast(F32), ALU.add, ALU.subtract)
                    last.then_inc(h_done, 1)
                dve.wait_ge(h_done, (n + 1) * KT)

            def add_projection(name, layer, kind):
                m = mods[layer % 2]
                with dve.Fori(0, KT // 2) as i:
                    for j in range(2):
                        dve.wait_ge(gemm_done, phases[name].number(i, j))
                        for cond, b, c0, t0, n in ((0, 0, 0, 0, NCTX), (1, 0, NCTX, NCTX, TH - NCTX), (1, 1, 0, TH, TH)):
                            xs = x[:, bass.ds(i * 2 * T + (j * T + t0), n)]
                            last = nc.vector.scalar_tensor_tensor(
                                xs, psum[j][:, b, c0:c0 + n],
                                m[:, bass.ds(i * 4 + ((kind * KT + j) * 2 + cond), 1)], xs, ALU.mult, ALU.add)
                        last.then_inc(x_done, 1)
                x_tiles[0] += KT
                dve.wait_ge(x_done, x_tiles[0])

            mod_take(0, 0, 48)
            for layer in range(DEPTH):
                norm(2 * layer)
                if layer + 1 < DEPTH:
                    mod_take(layer + 1, 0, 24)
                if layer == 0:
                    S = MIN
                    pes, acts, dves = S
                    nc.vector.memset(kr_cache, 0.0).then_inc(kr_cleared, 1)
                    acts.wait(dve, "rscq")
                    for t in range(3):
                        normed(mla_raw[t], vec("cq", t), mla_rs[0])
                    dve.drain()
                    for t in range(3):
                        nc.vector.tensor_copy(h_hi[:, CQ_AT + t * T:CQ_AT + (t + 1) * T], mla_raw[t])
                    dve.drain()
                    for t in range(3):
                        last = nc.vector.tensor_tensor(h_lo[:, CQ_AT + t * T:CQ_AT + (t + 1) * T], mla_raw[t],
                                                       h_hi[:, CQ_AT + t * T:CQ_AT + (t + 1) * T].bitcast(F32),
                                                       ALU.subtract)
                    dves.mark(last, "cq")
                    acts.wait(dve, "rsckv")
                    for t in range(2):
                        normed(mla_raw[3 + t], vec("ckv", t), mla_rs[1])
                    dve.drain()
                    for t in range(2):
                        o = CKV_AT + t * NKEY
                        last = split(dve, h_hi[:, o:o + T], h_lo[:, o:o + T], mla_raw[3 + t])
                    dves.mark(last, "ckv")
                    acts.wait(dve, "rskr")
                    dves.mark(nc.vector.scalar_tensor_tensor(kr_t[:, 0:T], mla_raw[5], vec("mqr", 1), mla_rs[2],
                                                             ALU.mult, ALU.mult), "kr")
                    pes.wait(dve, "rotkr")
                    dves.mark(roped(dve, kr_t, psB, cos64, sin64, mla_tmp), "kr_roped")
                    pes.wait(dve, "turned")
                    for t in range(2):
                        o = CKV_AT + t * NKEY + T
                        split(dve, h_hi[:, o:o + P], h_lo[:, o:o + P], psC[:, 0, t * P:(t + 1) * P])
                    dves.mark(nc.vector.tensor_copy(kr_t[:, T:NKEY], psC[:, 0, 2 * P:3 * P]), "cache")
                    S = MLA
                    pes, acts, dves = S
                    dves.open(dve)
                    with dve.Fori(0, HEADS) as i:
                        acts.wait(dve, "rsqn", i)
                        dves.mark(normed(qn_t, vec("mqk", 0), sq_n), "qn")
                        acts.wait(dve, "rsqr", i)
                        dves.mark(normed(qr_t, vec("mqr", 0), sq_r), "qr")
                        acts.wait(dve, "rskn", i)
                        dves.mark(normed(kn_t, vec("mqk", 1), sq_k), "kn")
                        pes.wait(dve, "rotqr", i)
                        dves.mark(roped(dve, qr_t, psB, cos64, sin64, m_tmp), "qroped")
                        attention_dve(dve, S, "", 1, 192 ** -0.5, m_probs, m_stats, i)
                        pes.wait(dve, "pv", i)
                        dves.mark(split_head(dve, i), "o")
                elif layer == 1:
                    S = DIF
                    pes, acts, dves = S
                    dves.open(dve)
                    with dve.Fori(0, HEADS) as i:
                        acts.wait(dve, "rsq", i)
                        dves.mark(normed(dq_t, vec("dqk", 0), dsq_q), "q")
                        acts.wait(dve, "rsk", i)
                        dves.mark(normed(dk_t[:, 0:T], vec("dqk", 1), dsq_k), "k")
                        pes.wait(dve, "rotq", i)
                        dves.mark(roped(dve, dq_t, psC, cos64, sin64, d_tmp), "qroped")
                        dve.drain()
                        pes.wait(dve, "rotk", i)
                        dves.mark(roped(dve, dk_t, psD, cos64, sin64, d_tmp), "kroped")
                        attention_dve(dve, S, "", 2, 64 ** -0.5, d_probs, d_stats, i)
                        acts.wait(dve, "rso", i)
                        normed(dq_t, small[:, 43:44], dsq_q)
                        dve.drain()
                        o = bass.ds(i * T, T)
                        dves.mark(split(dve, act_hi[:, o], act_lo[:, o], dq_t), "o")
                elif layer == 2:
                    S = GKV
                    pes, acts, dves = S
                    for j in range(2):
                        acts.wait(dve, "rsk", j)
                        dves.mark(normed(gk_t[j][:, 0:T], vec("gqk", 1), gsq), "k")
                        pes.wait(dve, "rotk", j)
                        dves.mark(roped(dve, gk_t[j], psC, cos128, sin128, g_tmp), "kroped")
                        dve.drain()
                    S = GQA
                    pes, acts, dves = S
                    dves.open(dve)
                    with dve.Fori(0, HEADS // 2) as i:
                        for k, p in enumerate("ab"):
                            acts.wait(dve, p + "rsq", i)
                            dves.mark(normed(gq_t, vec("gqk", 0), gsq), p + "q")
                            pes.wait(dve, p + "rotq", i)
                            dves.mark(roped(dve, gq_t, psC, cos128, sin128, g_tmp), p + "qroped")
                            attention_dve(dve, S, p, 1, P ** -0.5, g_probs, g_stats, i)
                            pes.wait(dve, p + "pv", i)
                            dves.mark(split_head(dve, i + k * 4), p + "o")
                else:
                    S = LRU
                    pes, acts, dves = S
                    dves.open(dve)
                    nc.vector.memset(l_xp, 0.0).then_inc(lru_ready, 1)
                    with dve.Fori(0, KT) as i:
                        acts.wait(dve, "xp", i)
                        cw = [vecs[:, bass.ds(i + (VEC["convw"] + k * KT), 1)] for k in range(4)]
                        cb = vecs[:, bass.ds(i + VEC["convb"], 1)]
                        nc.vector.tensor_scalar(l_y, l_xp[:, 0:LW], cw[0], cb, ALU.mult, ALU.add)
                        for k in range(1, 4):
                            dve.drain()
                            nc.vector.scalar_tensor_tensor(l_y, l_xp[:, k:k + LW], cw[k], l_y, ALU.mult, ALU.add)
                        dve.drain()
                        dves.mark(split(dve, y_hi[:, :], y_lo[:, :], l_y), "y")
                        acts.wait(dve, "tb", i)
                        for d in range(2):
                            nc.vector.scalar_tensor_tensor(l_ti[d], l_ti[d], 1.0, l_y, ALU.add, ALU.mult)
                        acts.wait(dve, "th", i)
                        for d in range(2):
                            nc.vector.tensor_scalar(l_h[d], l_th[d], 1.0, None, ALU.add)
                            nc.vector.tensor_scalar(l_a[d], l_th[d], -1.0, 1.0, ALU.mult, ALU.add)
                        dve.drain()
                        for d in range(2):
                            nc.vector.reciprocal(l_h[d], l_h[d])
                        dve.drain()
                        for d in range(2):
                            nc.vector.tensor_tensor(l_a[d], l_a[d], l_h[d], ALU.mult)
                            nc.vector.tensor_tensor(l_ti[d], l_ti[d], l_h[d], ALU.mult)
                        dve.drain()
                        acts.wait(dve, "sq", i)
                        for d in range(2):
                            nc.vector.tensor_tensor(l_ti[d], l_ti[d], l_sq[d], ALU.mult)
                        dve.drain()
                        for d in range(2):
                            for t0, n, init in ((0, NCTX, 0.0), (LAT0, NLAT, vecs[:, bass.ds(i + (VEC["h0"] + d * KT), 1)])):
                                o, a_, u_ = (b_[d][:, t0:t0 + n] for b_ in (l_h, l_a, l_ti))
                                if d:
                                    o, a_, u_ = o[:, ::-1], a_[:, ::-1], u_[:, ::-1]
                                nc.vector.tensor_tensor_scan(o, a_, u_, init, ALU.mult, ALU.add)
                        dve.drain()
                        nc.vector.tensor_copy(l_state[:, bass.ds(i, 1)], l_h[0][:, NCTX - 1:NCTX])
                        nc.vector.tensor_copy(l_state[:, bass.ds(i + KT, 1)], l_h[1][:, 0:1])
                        for t0, n, g0 in ((0, NCTX, 0), (LAT0, NLAT, NCTX)):
                            nc.vector.tensor_tensor(l_y[:, t0:t0 + n], l_h[0][:, t0:t0 + n], l_h[1][:, t0:t0 + n], ALU.add)
                        dve.drain()
                        for t0, n, g0 in ((0, NCTX, 0), (LAT0, NLAT, NCTX)):
                            nc.vector.tensor_tensor(l_gelu[:, g0:g0 + n], l_y[:, t0:t0 + n], l_gelu[:, g0:g0 + n], ALU.mult)
                        dve.drain()
                        o = bass.ds(i * T, T)
                        dves.mark(split(dve, act_hi[:, o], act_lo[:, o], l_gelu), "o")
                        dve.drain()
                add_projection(f"wo{layer}", layer, 2)
                norm(2 * layer + 1)
                if layer + 1 < DEPTH:
                    mod_take(layer + 1, 24, 24)
                for ch, size in enumerate(FFN_CHUNKS):
                    base = layer * (FFN // P) + sum(FFN_CHUNKS[:ch])
                    with dve.Fori(0, size) as i:
                        dve.wait_ge(silu_done, i + (base + 2))
                        dve.wait_ge(gemm_done, phases[f"in{layer}.{ch}"].number(i, 1))
                        dve.wait_ge(hidden_done, i + (base + 1))
                        nc.vector.tensor_tensor(halves(prod, TH), halves(gate_silu, TH), psB[:, :, 0:TH], ALU.mult)
                        dve.drain()
                        o = bass.ds(i * T, T)
                        split(dve, act_hi[:, o], act_lo[:, o], prod).then_inc(hidden_done, 1)
                    add_projection(f"out{layer}.{ch}", layer, 5)


def len_turns(layer):
    return (HEADS, HEADS, HEADS // 2)[layer]


def host_tables():
    ident = np.eye(P, dtype=np.float32)
    ones = np.ones((P, P), np.float32)
    blocks = np.kron(np.eye(2), np.ones((64, 64))).astype(np.float32)

    def rotation(dim):
        r = np.zeros((P, P), np.float32)
        for m in range(P):
            if m % dim < dim // 2:
                r[m + dim // 2, m] = -1.0
            else:
                r[m - dim // 2, m] = 1.0
        return r

    consts = np.concatenate([ident, ones, blocks, rotation(64), rotation(128)], axis=1)

    def rotary(dim):
        grid_w, n_freq = 64, dim // 4
        tok = np.arange(NLAT)
        inv = np.float32(10000.0) ** (-np.arange(n_freq, dtype=np.float32) / n_freq)
        ang = np.concatenate([(tok // grid_w).astype(np.float32)[:, None] * inv,
                              (tok % grid_w).astype(np.float32)[:, None] * inv], axis=1)
        full = np.tile(ang, (1, P // (dim // 2))).T.astype(np.float32)
        return np.cos(full), np.sin(full)

    tables = np.concatenate([*rotary(64), *rotary(128)], axis=1).astype(np.float32)
    return np.ascontiguousarray(consts), np.ascontiguousarray(tables)


_OUTS = [("y_prompt", (1, 128, 1024)), ("y_sample", (1, 512, 1024)), ("new_mla_ckv", (1, 1, 128, 256)),
         ("new_mla_krope", (1, 1, 128, 64)), ("new_diff_k", (1, 1, 128, 8, 2, 64)),
         ("new_diff_v", (1, 1, 128, 8, 128)), ("new_gqa_k", (1, 1, 128, 2, 128)),
         ("new_gqa_v", (1, 1, 128, 2, 128)), ("new_lru_h", (1, 1, 2, 1024))]


def kernel(**inputs):
    import concourse.bacc as _bacc
    from concourse.bass_utils import run_bass_kernel_spmd as _run

    nc = _bacc.Bacc("TRN2", target_bir_lowering=False, num_devices=1)
    arrays, aps = {}, {}
    consts, tables = host_tables()
    for name, value in list(inputs.items()) + [("consts", consts), ("tables", tables)]:
        v = np.ascontiguousarray(value)
        arrays[f"in_{name}"] = v
        aps[name] = nc.dram_tensor(f"in_{name}", v.shape, mybir.dt.from_np(v.dtype), kind="ExternalInput").ap()
    for name, shape in _OUTS:
        aps[name] = nc.dram_tensor(f"out_{name}", shape, F32, kind="ExternalOutput").ap()
    build(nc, aps)
    r = _run(nc, [arrays], core_ids=[0])
    return tuple(r.results[0][f"out_{name}"] for name, _ in _OUTS)
```

```python
import math
from contextlib import ExitStack

import numpy as np
import concourse.bass as bass
from concourse import mybir

F32 = mybir.dt.float32
F32R = mybir.dt.float32r
ALU = mybir.AluOpType
ACT = mybir.ActivationFunctionType
AX = mybir.AxisListType

P = 128
D = 1024
KT = D // P
NCTX, NLAT = 128, 512
T = NCTX + NLAT
TH = T // 2
NKEY = T + 128
DEPTH = 4
EPS = 1e-6
FFN = 2816
FFN_CHUNKS = (8, 8, 6)
HEADS = 8
MLA_QR, MLA_KVR = 384, 256
CQ_AT, CKV_AT = 0, 3 * T
QT = 5
LW = T + 4
LAT0 = 131
SLOT = 8 * P
WORK = 13312
MCOLS = 256
MCHUNKS = 6 * D // MCOLS
LAMBDA_INIT = 0.8 - 0.6 * math.exp(-0.3)

VEC_ROWS = [("gn1", 32), ("gn2", 32), ("cq", 3), ("ckv", 2), ("convb", 8), ("convw", 32), ("dsub", 1),
            ("gqk", 2), ("mqk", 2), ("mqr", 2), ("dqk", 2), ("pad", 10),
            ("bgate", 32), ("lam", 16), ("h0", 16), ("c", 8), ("cctx", 8), ("pad2", 48)]
VEC = {}
_at = 0
for _name, _n in VEC_ROWS:
    VEC[_name] = _at
    _at += _n
assert VEC["bgate"] == P and _at == 2 * P


class Steps:

    def __init__(self, sem, names, base=0):
        self.sem, self.names, self.base, self.k = sem, names, base, 0

    def open(self, eng):
        assert self.base == 1
        eng.sem_inc(self.sem, 1)

    def mark(self, ins, name):
        assert self.names[self.k % len(self.names)] == name, (name, self.names[self.k % len(self.names)])
        self.k += 1
        ins.then_inc(self.sem, 1)

    def wait(self, eng, name, turn=0):
        eng.wait_ge(self.sem, turn * len(self.names) + (self.base + self.names.index(name) + 1))

    def wait_turns(self, eng, turn):
        eng.wait_ge(self.sem, turn * len(self.names) + self.base)


class Phase:

    def __init__(self, turns, slots, shape, first, landed):
        self.turns, self.slots, self.shape, self.first = turns, slots, shape, first
        self.landed = dict(landed)
        self.n = len(slots)

    def number(self, turn, j):
        return turn * self.n + (self.first + j + 1)


def plan_panels():
    phases, first, landed = {}, 0, {0: 0, 1: 0, 2: 0}

    def add(name, turns, slots, shape):
        nonlocal first
        phases[name] = Phase(turns, slots, shape, first, landed)
        for s in slots:
            landed[s] += turns
        first += turns * len(slots)

    for layer in range(DEPTH):
        if layer == 0:
            add("mla_in", 3, (0, 1), [(KT, P)] * 2)
            add("mla", HEADS, (0, 1), [(3, 192), (2, 256)])
        elif layer == 1:
            add("diff", HEADS, (2, 0, 1), [(KT, P)] * 3)
        elif layer == 2:
            add("gqa_kv", 2, (0, 1), [(KT, P)] * 2)
            add("gqa", HEADS // 2, (0, 1), [(KT, P)] * 2)
        else:
            add("lru", KT, (2, 0, 1), [(KT, P), (KT, P), (4, P)])
        add(f"wo{layer}", KT // 2, (0, 1), [(KT, P)] * 2)
        for c, size in enumerate(FFN_CHUNKS):
            add(f"in{layer}.{c}", size, (0, 1), [(KT, P)] * 2)
            add(f"out{layer}.{c}", KT // 2, (0, 1), [(size, P)] * 2)
    return phases


def attention_names(pre, comps):
    pe, act, dve = [], [], []
    for t in range(QT + 1):
        if t < QT:
            pe += [f"{pre}scores{t}.{c}" for c in range(comps)]
            act += [f"{pre}exp{t}.{c}" for c in range(comps)]
            dve += [f"{pre}max{t}.{c}" for c in range(comps)] + [f"{pre}probs{t}"]
        if t >= 1:
            pe.append(f"{pre}turned{t - 1}")
            act.append(f"{pre}pt{t - 1}")
    pe.append(f"{pre}pv")
    return pe, act, dve


def build(nc, a):
    phases = plan_panels()

    with ExitStack() as ctx:
        def sb(name, cols, dt=F32):
            return ctx.enter_context(nc.sbuf_tensor(name, [P, cols], dt))

        def sem(name):
            return ctx.enter_context(nc.semaphore(name))

        x = sb("x", KT * T)
        h_hi, h_lo = sb("h_hi", KT * T, F32R), sb("h_lo", KT * T, F32R)
        act_hi, act_lo = sb("act_hi", KT * T, F32R), sb("act_lo", KT * T, F32R)
        raw = [sb(f"raw{s}", SLOT) for s in range(3)]
        w_hi = [sb(f"w_hi{s}", SLOT, F32R) for s in range(3)]
        w_lo = [sb(f"w_lo{s}", SLOT, F32R) for s in range(3)]
        y_hi, y_lo = sb("y_hi", LW, F32R), sb("y_lo", LW, F32R)
        work = sb("work", WORK)
        consts = sb("consts", 5 * P)
        tables = sb("tables", 4 * NLAT)
        vecs = sb("vecs", 2 * P)
        bmod = sb("bmod", 192)
        mods = [sb(f"mods{b}", 96) for b in range(2)]
        gains = sb("gains", 32)
        silu_c = sb("silu_c", 16)
        small = sb("small", 64)
        lru_small = sb("lru_small", 256)
        psum = [ctx.enter_context(nc.psum_tensor(f"ps{n}", [P, 2, 512], F32)) for n in "ABCD"]
        psA, psB, psC, psD = psum

        ident, ones, blocks, rot64, rot128 = (consts[:, k * P:(k + 1) * P] for k in range(5))
        cos64, sin64, cos128, sin128 = (tables[:, k * NLAT:(k + 1) * NLAT] for k in range(4))
        eps = small[:, 40:41]
        neg_lambda = small[:, 41:42]

        class Carve:

            def __init__(self):
                self.at = 0

            def __call__(self, n):
                self.at += n
                assert self.at <= WORK, self.at
                return work[:, self.at - n:self.at]

        const_in = sem("const_in")
        x_in = sem("x_in")
        raw_in = [sem(f"raw_in{s}") for s in range(3)]
        first_mod_in = [sem(f"first_mod_in{b}") for b in range(3)]
        first_mod_row = sem("first_mod_row")
        mod_in = [sem(f"mod_in{b}") for b in range(2)]
        pool_hi = sem("pool_hi")
        split_done = sem("split_done")
        gemm_done = sem("gemm_done")
        first_mod_used = sem("first_mod_used")
        first_mod_turned = sem("first_mod_turned")
        mod_ready = sem("mod_ready")
        mod_mac = sem("mod_mac")
        mod_turned = sem("mod_turned")
        mod_summed = sem("mod_summed")
        x_done = sem("x_done")
        square_done = sem("square_done")
        sums_done = sem("sums_done")
        rstd_done = sem("rstd_done")
        scaled_done = sem("scaled_done")
        h_hi_done = sem("h_hi_done")
        h_done = sem("h_done")
        silu_done = sem("silu_done")
        hidden_done = sem("hidden_done")
        pre_pe, pre_act, pre_dve = sem("pre_pe"), sem("pre_act"), sem("pre_dve")
        cache_in, gcache_in = sem("cache_in"), sem("gcache_in")
        kr_cleared, lru_ready = sem("kr_cleared"), sem("lru_ready")
        outs_done = sem("outs_done")
        y_turned, y_copied, y_out = sem("y_turned"), sem("y_copied"), sem("y_out")

        def steps(name, pe, act, dve, base=1):
            return tuple(Steps(sem(f"{name}_{e}"), names, base) for e, names in (("pe", pe), ("act", act), ("dve", dve)))

        PRE = [Steps(pre_pe, ["vecs", "bmod", "lam", "x0", "x1", "x2", "x3", "x4", "x5", "x6", "x7"]),
               Steps(pre_act, ["vecs", "silu", "lamexp", "sp"]),
               Steps(pre_dve, ["ready", "lamsum", "lamdiff", "lamall", "bmod", "splog"])]
        cpe, cact, cdve = attention_names("", 1)
        MIN = steps("mla_in", ["sscq", "ssckv", "sskr", "rotkr", "turned"],
                    [f"m{t}" for t in range(6)] + ["rscq", "rsckv", "rskr", "outs"],
                    ["cq", "ckv", "kr", "kr_roped", "cache"], 0)
        MLA = steps("mla_head", ["gqn", "gkn", "ssqn", "ssqr", "sskn", "rotqr", "turned_v"] + cpe,
                    ["evqn", "evqr", "evkn", "rsqn", "rsqr", "evv", "rskn", "v"] + cact,
                    ["qn", "qr", "kn", "qroped"] + cdve + ["o"])
        dpe, dact, ddve = attention_names("", 2)
        DIF = steps("diff_head", ["ssq", "ssk", "rotq", "turned_v", "rotk"] + dpe + ["sso"],
                    ["evq", "evk", "rsq", "evv", "rsk", "v", "kout"] + dact + ["evo", "rso"],
                    ["q", "k", "qroped", "kroped"] + ddve + ["o"])
        GKV = steps("gqa_kv", ["ssk", "rotk", "turned_v"], ["evk", "evv", "rsk", "v"], ["k", "kroped"], 0)
        gn = [attention_names(p, 1) for p in "ab"]
        GQA = steps("gqa_head",
                    sum([[p + "ssq", p + "rotq"] + gn[k][0] for k, p in enumerate("ab")], []),
                    sum([[p + "evq", p + "rsq"] + gn[k][1] for k, p in enumerate("ab")], []),
                    sum([[p + "q", p + "qroped"] + gn[k][2] + [p + "o"] for k, p in enumerate("ab")], []))
        LRU = steps("lru", ["rf", "if", "rb"], ["gelu", "xp", "tf", "tb", "th", "sq"], ["y", "o"])

        def products(pe, out, slot, kts, cols, c0, rhs_hi, rhs_lo, at, stride, half):
            last = None
            for kt in range(kts):
                for p, (w, r) in enumerate(((w_hi, rhs_hi), (w_hi, rhs_lo), (w_lo, rhs_hi))):
                    for b in range(2):
                        o = at + kt * stride + b * half
                        last = nc.tensor.matmul(out[:, b, 0:half], w[slot][:, kt * cols + c0:kt * cols + c0 + P],
                                                r[:, o:o + half], start=(kt == 0 and p == 0),
                                                stop=(kt == kts - 1 and p == 2))
            return last

        def take_panel(pe, name, turn, j):
            ph = phases[name]
            pe.wait_ge(split_done, ph.number(turn, j))
            return ph.slots[j]

        def sum_rows(out, ones_, pieces, half):
            last = None
            for b in range(2):
                for k, sq in enumerate(pieces):
                    last = nc.tensor.matmul(out[:, b, 0:half], ones_, sq[:, b * half:(b + 1) * half],
                                            start=(k == 0), stop=(k == len(pieces) - 1))
            return last

        def attention_pe(pe, S, pre, comps, scores, V, PT, PTp, probs, turn):
            pes, acts, dves = S
            for t in range(QT + 1):
                if t < QT:
                    for c in range(comps):
                        j = t * comps + c
                        s = psum[j % 2]
                        if j >= 2:
                            acts.wait(pe, f"{pre}exp{(j - 2) // comps}.{(j - 2) % comps}", turn)
                        q0 = 128 + t * P if t < 4 else 0
                        spans = ((0, 128, TH), (1, 128 + TH, TH)) if t < 4 else ((0, 0, P),)
                        for b, k0, n in spans:
                            for m, (q, k) in enumerate(scores[c]):
                                last = nc.tensor.matmul(s[:, b, 0:n], q[:, q0:q0 + P], k[:, k0:k0 + n],
                                                        start=(m == 0), stop=(m == len(scores[c]) - 1))
                        pes.mark(last, f"{pre}scores{t}.{c}")
                if t >= 1:
                    u = t - 1
                    dves.wait(pe, f"{pre}probs{u}", turn)
                    if u >= 2:
                        acts.wait(pe, f"{pre}pt{u - 2}", turn)
                    d = psum[2 + u % 2]
                    for k in range(5 if u < 4 else 1):
                        last = nc.tensor.transpose(d[:, k // 4, (k % 4) * P:(k % 4 + 1) * P],
                                                   probs[u % 2][0][:, k * P:(k + 1) * P], ident)
                    pes.mark(last, f"{pre}turned{u}")
            acts.wait(pe, f"{pre}pt4", turn)
            for k in range(5):
                nc.tensor.matmul(psD[:, 0, 0:NLAT], V[:, (k + 1) * P:(k + 2) * P], PT[:, k * NLAT:(k + 1) * NLAT],
                                 start=(k == 0), stop=(k == 4))
            pes.mark(nc.tensor.matmul(psD[:, 1, 0:P], V[:, 0:P], PTp, start=True, stop=True), pre + "pv")

        def halves(ap, half):
            return ap.rearrange("p (b n) -> p b n", b=2)

        def evacuate(out, sq, ps, half):
            nc.scalar.activation(halves(out, half), ps[:, :, 0:half], ACT.Copy)
            return nc.scalar.activation(halves(sq, half), ps[:, :, 0:half], ACT.Square)

        def rstd(act, out, ps, count, half):
            nc.scalar.activation(halves(out, half), ps[:, :, 0:half], ACT.Ln, bias=eps, scale=1.0 / count)
            act.drain()
            return nc.scalar.activation(out, out, ACT.Exp, scale=-0.5)

        def attention_act(act, S, pre, comps, scale, PT, PTp, probs, stats, turn):
            pes, acts, dves = S
            mx, nm, sm, rs = stats
            for t in range(QT + 1):
                if t < QT:
                    if t >= 2:
                        pes.wait(act, f"{pre}turned{t - 2}", turn)
                    for c in range(comps):
                        j = t * comps + c
                        s = psum[j % 2]
                        dves.wait(act, f"{pre}max{t}.{c}", turn)
                        if t < 4:
                            o, i = halves(probs[t % 2][c], TH), s[:, :, 0:TH]
                        else:
                            o, i = probs[t % 2][c][:, 0:P], s[:, 0, 0:P]
                        acts.mark(nc.scalar.activation(o, i, ACT.Exp, bias=nm[:, j:j + 1], scale=scale,
                                                       accum_out=sm[:, j:j + 1]), f"{pre}exp{t}.{c}")
                if t >= 1:
                    u = t - 1
                    pes.wait(act, f"{pre}turned{u}", turn)
                    d = psum[2 + u % 2]
                    if u < 4:
                        dst = PT.rearrange("p (k q) -> p k q", k=5)
                        nc.scalar.activation(dst[:, 0:4, u * P:(u + 1) * P],
                                             d[:, 0, :].rearrange("p (k q) -> p k q", k=4), ACT.Copy)
                        last = nc.scalar.activation(dst[:, 4, u * P:(u + 1) * P], d[:, 1, 0:P], ACT.Copy)
                    else:
                        last = nc.scalar.activation(PTp, d[:, 0, 0:P], ACT.Copy)
                    acts.mark(last, f"{pre}pt{u}")

        def attention_dve(dve, S, pre, comps, scale, probs, stats, turn):
            pes, acts, dves = S
            mx, nm, sm, rs = stats
            for t in range(QT):
                for c in range(comps):
                    j = t * comps + c
                    s = psum[j % 2]
                    pes.wait(dve, f"{pre}scores{t}.{c}", turn)
                    if t < 4:
                        nc.vector.tensor_reduce(mx[:, j:j + 1], s[:, :, 0:TH], AX.XY, ALU.max)
                    else:
                        nc.vector.tensor_reduce(mx[:, j:j + 1], s[:, 0, 0:P], AX.X, ALU.max)
                    dve.drain()
                    dves.mark(nc.vector.tensor_scalar(nm[:, j:j + 1], mx[:, j:j + 1], -scale, None, ALU.mult),
                              f"{pre}max{t}.{c}")
                n = T if t < 4 else P
                j = t * comps
                acts.wait(dve, f"{pre}exp{t}.{comps - 1}", turn)
                nc.vector.reciprocal(rs[:, j:j + comps], sm[:, j:j + comps])
                dve.drain()
                p0 = probs[t % 2][0][:, 0:n]
                last = nc.vector.tensor_scalar(p0, p0, rs[:, j:j + 1], None, ALU.mult)
                if comps == 2:
                    nc.vector.tensor_scalar(rs[:, j + 1:j + 2], rs[:, j + 1:j + 2], neg_lambda, None, ALU.mult)
                    dve.drain()
                    last = nc.vector.scalar_tensor_tensor(p0, probs[t % 2][1][:, 0:n], rs[:, j + 1:j + 2], p0,
                                                          ALU.mult, ALU.add)
                dves.mark(last, f"{pre}probs{t}")

        def normed(raw_, g, rs):
            return nc.vector.scalar_tensor_tensor(raw_, raw_, g, rs, ALU.mult, ALU.mult)

        def roped(dve, t_, ps, cos, sin, tmp):
            nc.vector.tensor_tensor(tmp, ps[:, 0, 0:NLAT], sin, ALU.mult)
            nc.vector.tensor_tensor(t_[:, NCTX:T], t_[:, NCTX:T], cos, ALU.mult)
            dve.drain()
            return nc.vector.tensor_tensor(t_[:, NCTX:T], t_[:, NCTX:T], tmp, ALU.add)

        def split(dve, hi, lo, src):
            nc.vector.tensor_copy(hi, src)
            dve.drain()
            return nc.vector.tensor_tensor(lo, src, hi.bitcast(F32), ALU.subtract)

        def split_head(dve, head):
            nc.vector.tensor_copy(act_hi[:, bass.ds(head * T + NCTX, NLAT)], psD[:, 0, 0:NLAT])
            nc.vector.tensor_copy(act_hi[:, bass.ds(head * T, NCTX)], psD[:, 1, 0:P])
            dve.drain()
            nc.vector.tensor_tensor(act_lo[:, bass.ds(head * T + NCTX, NLAT)], psD[:, 0, 0:NLAT],
                                    act_hi[:, bass.ds(head * T + NCTX, NLAT)].bitcast(F32), ALU.subtract)
            return nc.vector.tensor_tensor(act_lo[:, bass.ds(head * T, NCTX)], psD[:, 1, 0:P],
                                           act_hi[:, bass.ds(head * T, NCTX)].bitcast(F32), ALU.subtract)

        c = Carve()
        x_tok = c(QT * D)
        vec_rows = [c(P) for _ in range(4)]
        lam_row = c(256)
        lam_tmp = c(132)

        c = Carve()
        squares = c(KT * T)
        rms = c(T)

        c = Carve()
        mla_raw = [c(T) for _ in range(6)]
        mla_sq = [c(T) for _ in range(6)]
        mla_rs = mla_sq[0], mla_sq[3], mla_sq[5]
        mla_cache = c(2 * P)
        kr_cache = c(P)
        mla_tmp = c(NLAT)
        c = Carve()
        c(0)
        qn_t, qr_t = c(T), c(T)
        sq_n, sq_r = c(T), c(T)
        kn_t, vt_t, sq_k = c(NKEY), c(NKEY), c(NKEY)
        mV = c(6 * P)
        m_probs = [[c(T)], [c(T)]]
        m_PT, m_PTp = c(5 * NLAT), c(P)
        m_tmp = c(NLAT)
        m_stats = [c(QT) for _ in range(4)]
        kr_t = work[:, WORK - NKEY:WORK]
        mla_out = work[:, WORK - NKEY - 384:WORK - NKEY]
        assert c.at <= WORK - NKEY - 384

        c = Carve()
        dq_t, dk_t = c(T), c(NKEY)
        dsq_q, dsq_k = c(T), c(T)
        dvt = c(T)
        dV = c(6 * P)
        d_probs = [[c(T), c(T)], [c(T), c(T)]]
        d_PT, d_PTp = c(5 * NLAT), c(P)
        d_tmp = c(NLAT)
        d_cache = c(P)
        d_kout = c(P)
        d_stats = [c(2 * QT) for _ in range(4)]

        c = Carve()
        gk_t = [c(NKEY), c(NKEY)]
        gV = [c(6 * P), c(6 * P)]
        g_cache = [c(P), c(P)]
        g_kout = [c(P), c(P)]
        gsq, gvt = c(T), c(T)
        gq_t = c(T)
        g_probs = [[c(T)], [c(T)]]
        g_PT, g_PTp = c(5 * NLAT), c(P)
        g_tmp = c(NLAT)
        g_stats = [c(QT) for _ in range(4)]

        c = Carve()
        l_xp = c(LW + 4)
        l_gelu = c(T)
        l_y = c(LW)
        l_tr = [c(LW), c(LW)]
        l_ti = [c(LW), c(LW)]
        l_th = [c(LW), c(LW)]
        l_sq = [c(LW), c(LW)]
        l_a = [c(LW), c(LW)]
        l_h = [c(LW), c(LW)]
        sp2 = lru_small[:, 0:16]
        hb = lru_small[:, 16:48]
        l_state = lru_small[:, 48:64]
        l_s = lru_small[:, 64:144].rearrange("p (k n) -> p k n", k=5)

        c = Carve()
        gate_silu = c(T)
        prod = c(T)
        mod_w = [c(KT * MCOLS) for _ in range(2)]
        mod_acc = c(2 * MCOLS)
        mod_acc_ = mod_acc.rearrange("p (h c n) -> p h c n", h=2, c=2)
        first_mod_w = [work[:, k * KT * 512:(k + 1) * KT * 512] for k in (2, 1, 0)]
        first_mod_rows = work[0:2, WORK - 2 * 512:WORK].rearrange("p (b n) -> p b n", b=2)
        c = Carve()
        y_tok = c(QT * D)

        def mod_col(layer, kind, tile, cond):
            k = (kind * KT + tile) * 2 + cond
            return mods[layer % 2][:, k:k + 1]

        def mod_at(layer, ch, out):
            if layer + 1 == DEPTH or ch > 1:
                return None
            return layer + 1, ch * (8 + KT // 2) + (8 if out else 0)
        assert FFN_CHUNKS[0] == FFN_CHUNKS[1] == 8 and 2 * (8 + KT // 2) == MCHUNKS

        block = ctx.enter_context(nc.Block())

        @block.sync
        def _(sp):
            def panels(name, source, mod=None):
                ph = phases[name]
                unroll = 2 if mod else 1

                def turn(g, k):
                    for j, s in enumerate(ph.slots):
                        kts, cols = ph.shape[j]
                        behind = ph.first + k * ph.n + j + 1 - ph.n
                        if not isinstance(g, int) or behind > 0:
                            sp.wait_ge(split_done, g * (unroll * ph.n) + behind)
                        sp.dma_start(raw[s][:, 0:kts * cols].rearrange("p (k n) -> p k n", k=kts),
                                     source(g * unroll + k, j)).then_inc(raw_in[s], 16)
                    if mod:
                        n = MCHUNKS * (mod[0] - 1) + mod[1] + k
                        if isinstance(g, int) and mod[1] == 0:
                            if k == 0:
                                sp.wait_ge(h_done, 2 * mod[0] * KT)
                        else:
                            sp.wait_ge(mod_mac, g * 2 + (n - 1))
                        sp.dma_start(mod_w[k].rearrange("p (k n) -> p k n", k=KT),
                                     a["w_mod"][mod[0]].rearrange("(k p) n -> p k n", p=P)[
                                         :, :, bass.ds(g * (2 * MCOLS) + (mod[1] + k) * MCOLS, MCOLS)]
                                     ).then_inc(mod_in[k], 16)

                peeled = 1 if ph.first == 0 or (mod and mod[1] == 0) else 0
                if peeled:
                    for k in range(unroll):
                        turn(0, k)
                with sp.Fori(peeled, ph.turns // unroll) as g:
                    for k in range(unroll):
                        turn(g, k)

            sp.dma_start(consts[:, :], a["consts"]).then_inc(const_in, 16)
            sp.wait_ge(const_in, 16)
            pre = PRE
            pre[2].wait(sp, "ready")
            rows = [("gn1", a["g_norm1"].rearrange("l (k n) -> (l k) n", n=P)),
                    ("gn2", a["g_norm2"].rearrange("l (k n) -> (l k) n", n=P)),
                    ("cq", a["mla_g_cq"].rearrange("l (k n) -> (l k) n", n=P)),
                    ("ckv", a["mla_g_ckv"].rearrange("l (k n) -> (l k) n", n=P)),
                    ("convb", a["lru_conv_b"].rearrange("l (k n) -> (l k) n", n=P)),
                    ("convw", a["lru_conv_w"].rearrange("l w (k n) -> (l w k) n", n=P)),
                    ("dsub", a["diff_g_sub"]),
                    ("gqk", a["gqa_g_qk"][0]),
                    ("mqk", a["mla_g_qk"][0][:, 0:P]),
                    ("bgate", a["lru_b_gate"].rearrange("l d g (k n) -> (l d g k) n", n=P)),
                    ("lam", a["lru_lambda"].rearrange("l d (k n) -> (l d k) n", n=P)),
                    ("h0", a["state_lru_h"].rearrange("b l d (k n) -> (b l d k) n", n=P)),
                    ("c", a["c"].rearrange("l (k n) -> (l k) n", n=P)),
                    ("cctx", a["c_ctx"].rearrange("(k n) -> k n", n=P))]
            n = 0
            for name, src in rows:
                r = VEC[name]
                tile = vec_rows[r // P]
                sp.dma_start(tile[r % P:r % P + src.shape[0], :], src).then_inc(const_in, 16)
                n += 1
            for half in range(2):
                for name, src in (("mqr", a["mla_g_qk"][0][:, P:P + 64]), ("dqk", a["diff_g_qk"][0])):
                    r = VEC[name]
                    sp.dma_start(vec_rows[0][r:r + 2, half * 64:half * 64 + 64], src).then_inc(const_in, 16)
                    n += 1
            bm = a["b_mod"].rearrange("l (k n) -> (l k) n", n=P)
            sp.dma_start(vec_rows[2][0:P, :], bm[0:P, :]).then_inc(const_in, 16)
            sp.dma_start(vec_rows[3][0:64, :], bm[P:192, :]).then_inc(const_in, 16)
            sp.dma_start(lam_row[0:1, :], a["diff_lambda"].rearrange("l a d -> l (a d)")).then_inc(const_in, 16)
            sp.dma_start(x_tok[:, 0:D], a["x_prompt"][0]).then_inc(x_in, 16)
            sp.dma_start(x_tok[:, D:QT * D].rearrange("p (t n) -> p t n", t=4),
                         a["x_sample"][0].rearrange("(t p) n -> p t n", p=P)).then_inc(x_in, 16)
            sp.dma_start(tables[:, :], a["tables"]).then_inc(const_in, 16)

            w = a["w_mod"][0].rearrange("(k p) n -> p k n", p=P)
            for b in range(3):
                if b == 1:
                    sp.wait_ge(x_done, KT)
                sp.dma_start(first_mod_w[b].rearrange("p (k n) -> p k n", k=KT),
                             w[:, :, b * 512:(b + 1) * 512]).then_inc(first_mod_in[b], 16)
            with sp.Fori(1, 4) as i:
                for b in range(3):
                    sp.wait_ge(first_mod_used, i * 3 + (b + 1 - 3))
                    sp.dma_start(first_mod_w[b].rearrange("p (k n) -> p k n", k=KT),
                                 w[:, :, bass.ds(i * 1536 + b * 512, 512)]).then_inc(first_mod_in[b], 16)

            for layer in range(DEPTH):
                if layer == 0:
                    win = a["mla_w_in"][0].rearrange("(k p) n -> p k n", p=P)
                    uq = a["mla_w_uq"][0].rearrange("(k p) n -> p k n", p=P)
                    ukv = a["mla_w_ukv"][0].rearrange("(k p) n -> p k n", p=P)
                    wo = a["mla_w_o"][0]
                    ph = phases["mla_in"]
                    for t in range(6):
                        c0 = t * P if t < 5 else 576
                        if t >= 2:
                            sp.wait_ge(split_done, t - 1)
                        sp.dma_start(raw[t % 2][:, :].rearrange("p (k n) -> p k n", k=KT),
                                     win[:, :, c0:c0 + P]).then_inc(raw_in[t % 2], 16)
                    panels("mla", lambda i, j: uq[:, :, bass.ds(i * 192, 192)] if j == 0
                           else ukv[:, :, bass.ds(i * 256, 256)])
                elif layer == 1:
                    win = a["diff_w_in"][0].rearrange("(k p) n -> p k n", p=P)
                    wo = a["diff_w_o"][0]
                    kc = a["cache_diff_k"][0, 0].rearrange("t h c d -> t (h c d)")
                    vc = a["cache_diff_v"][0, 0].rearrange("t h d -> t (h d)")
                    panels("diff", lambda i, j: win[:, :, bass.ds(i * P + j * D, P)])
                elif layer == 2:
                    win = a["gqa_w_in"][0].rearrange("(k p) n -> p k n", p=P)
                    wo = a["gqa_w_o"][0]
                    panels("gqa_kv", lambda i, j: win[:, :, bass.ds(i * P + (D + j * 256), P)])
                    panels("gqa", lambda i, j: win[:, :, bass.ds(i * P + j * 512, P)])
                else:
                    win = a["lru_w_in"][0].rearrange("(k p) n -> p k n", p=P)
                    wo = a["lru_w_out"][0]
                    wg = a["lru_w_gate"][0].rearrange("d g b k j -> k (d g) b j")
                    panels("lru", lambda i, j: win[:, :, bass.ds(i * P + j * D, P)] if j < 2
                           else wg[:, :, bass.ds(i, 1), :].rearrange("k g o j -> k g (o j)"))
                wov = wo.rearrange("(k p) n -> p k n", p=P)
                panels(f"wo{layer}", lambda i, j: wov[:, :, bass.ds(i * 2 * P + j * P, P)])
                f_in = a["w_ffn_in"][layer].rearrange("(k p) n -> p k n", p=P)
                f_out = a["w_ffn_out"][layer].rearrange("(k p) n -> p k n", p=P)
                m0 = 0
                for ch, size in enumerate(FFN_CHUNKS):
                    panels(f"in{layer}.{ch}", lambda i, j: f_in[:, :, bass.ds(i * P + (m0 * P + j * FFN), P)],
                           mod_at(layer, ch, False))
                    panels(f"out{layer}.{ch}", lambda i, j: f_out[:, m0:m0 + size, bass.ds(i * 2 * P + j * P, P)],
                           mod_at(layer, ch, True))
                    m0 += size

        @block.gpsimd
        def _(pool):
            def turn(name, i, peeled=False):
                ph = phases[name]
                for j, s in enumerate(ph.slots):
                    n = ph.shape[j][0] * ph.shape[j][1]
                    pool.wait_ge(raw_in[s], i * 16 + 16 * (ph.landed[s] + 1))
                    if not peeled:
                        pool.wait_ge(gemm_done, i * ph.n + (ph.first + j + 1 - ph.n))
                    nc.gpsimd.tensor_tensor(w_hi[s][:, 0:n], raw[s][:, 0:n], ones[:, 0:1].to_broadcast([P, n]),
                                            ALU.mult).then_inc(pool_hi, 1)
                    pool.wait_ge(pool_hi, i * ph.n + (ph.first + j + 1))
                    nc.gpsimd.tensor_tensor(w_lo[s][:, 0:n], raw[s][:, 0:n], w_hi[s][:, 0:n].bitcast(F32),
                                            ALU.subtract).then_inc(split_done, 1)

            pool.wait_ge(const_in, 16)
            for name, ph in phases.items():
                if ph.first == 0:
                    turn(name, 0, peeled=True)
                    with pool.Fori(1, ph.turns) as i:
                        turn(name, i)
                else:
                    with pool.Fori(0, ph.turns) as i:
                        turn(name, i)

        @block.tensor
        def _(pe):
            def first_modulation():
                with pe.Fori(0, 2) as i:
                    for q in range(7):
                        if q < 6:
                            pe.wait_ge(first_mod_in[q % 3], i * 32 + (16 * (q // 3) + 16))
                            for kt in range(KT):
                                last = nc.tensor.matmul(psum[q % 2][0:2, 0, :], silu_c[:, kt * 2:kt * 2 + 2],
                                                        first_mod_w[q % 3][:, kt * 512:(kt + 1) * 512],
                                                        start=(kt == 0), stop=(kt == KT - 1))
                            last.then_inc(first_mod_used, 1)
                        if q:
                            pe.wait_ge(first_mod_row, i * 6 + q)
                            for k in range(4):
                                last = nc.tensor.matmul(psC[:, 1, bass.ds(i * 48 + ((q - 1) * 4 + k) * 2, 2)],
                                                        first_mod_rows[:, (q - 1) % 2, k * P:(k + 1) * P],
                                                        ident[0:2, 0:2], start=True, stop=True)
                            last.then_inc(first_mod_turned, 1)

            def mod_turn(mod, i):
                n = MCHUNKS * (mod[0] - 1) + mod[1]
                pe.wait_ge(mod_mac, i + (n + 1))
                pe.wait_ge(mod_summed, i + (n + 1))
                for k in range(4):
                    last = nc.tensor.transpose(psC[:, 0, k * P:(k + 1) * P], mod_acc[:, k * P:(k + 1) * P], ident)
                last.then_inc(mod_turned, 1)

            def norm(n):
                if n == 0:
                    pe.wait_ge(mod_ready, 1)
                for kt in range(KT):
                    pe.wait_ge(square_done, n * KT + kt + 1)
                    for b in range(2):
                        last = nc.tensor.matmul(psC[:, b, 0:TH], ones, squares[:, kt * T + b * TH:kt * T + (b + 1) * TH],
                                                start=(kt == 0), stop=(kt == KT - 1))
                last.then_inc(sums_done, 1)

            x_tiles = [KT]

            def project(name, kts, mod=None):
                base = x_tiles[0]
                with pe.Fori(0, KT // 2) as i:
                    for j in range(2):
                        slot = take_panel(pe, name, i, j)
                        pe.wait_ge(x_done, i * 2 + (base + j - 1))
                        products(pe, psum[j], slot, kts, P, 0, act_hi, act_lo, 0, T, TH).then_inc(gemm_done, 1)
                    if mod:
                        mod_turn(mod, i)
                x_tiles[0] += KT

            pes, acts, dves = PRE
            pe.wait_ge(const_in, 16 * 23)
            for k in range(2):
                last = nc.tensor.transpose(psC[:, 0, k * P:(k + 1) * P], vec_rows[k], ident)
            pes.mark(last, "vecs")
            nc.tensor.transpose(psD[:, 0, 0:P], vec_rows[2], ident)
            pes.mark(nc.tensor.transpose(psD[:, 0, P:2 * P], vec_rows[3], ident), "bmod")
            dves.wait(pe, "lamdiff")
            pes.mark(nc.tensor.matmul(psC[:, 1, 0:1], ones[0:1, :], lam_tmp[0:1, 4:5], start=True, stop=True), "lam")
            pe.wait_ge(x_in, 32)
            for kt in range(KT):
                if kt >= 2:
                    pe.wait_ge(x_done, kt - 1)
                d = psum[kt % 2]
                for t in range(QT):
                    last = nc.tensor.transpose(d[:, t // 4, (t % 4) * P:(t % 4 + 1) * P],
                                               x_tok[:, t * D + kt * P:t * D + (kt + 1) * P], ident)
                pes.mark(last, f"x{kt}")
            acts.wait(pe, "silu")
            dves.wait(pe, "bmod")
            dves.wait(pe, "lamall")
            pe.wait_ge(x_done, KT)
            first_modulation()

            for layer in range(DEPTH):
                norm(2 * layer)
                pe.wait_ge(h_done, (2 * layer + 1) * KT)

                def h_tile(out, name, i, j):
                    slot = take_panel(pe, name, i, j)
                    return products(pe, out, slot, KT, P, 0, h_hi, h_lo, 0, T, TH)

                if layer == 0:
                    S = MIN
                    pes, acts, dves = S
                    for t in range(6):
                        if t >= 2:
                            acts.wait(pe, f"m{t - 2}")
                        h_tile(psum[t % 2], "mla_in", t // 2, t % 2).then_inc(gemm_done, 1)
                    acts.wait(pe, "m2")
                    pes.mark(sum_rows(psC, ones, mla_sq[0:3], TH), "sscq")
                    acts.wait(pe, "m4")
                    pes.mark(sum_rows(psD, ones, mla_sq[3:5], TH), "ssckv")
                    acts.wait(pe, "m5")
                    pes.mark(sum_rows(psA, blocks, mla_sq[5:6], TH), "sskr")
                    dves.wait(pe, "kr")
                    pes.mark(nc.tensor.matmul(psB[:, 0, 0:NLAT], rot64, kr_t[:, NCTX:T], start=True, stop=True), "rotkr")
                    pe.wait_ge(const_in, 16 * 25)
                    nc.tensor.transpose(psC[:, 0, 0:P], mla_cache[:, 0:P], ident)
                    nc.tensor.transpose(psC[:, 0, P:2 * P], mla_cache[:, P:2 * P], ident)
                    nc.tensor.transpose(psC[:, 0, 2 * P:3 * P], kr_cache, ident)
                    nc.tensor.transpose(psD[:, 0, 0:P], mla_raw[3][:, 0:P], ident)
                    nc.tensor.transpose(psD[:, 0, P:2 * P], mla_raw[4][:, 0:P], ident)
                    pes.mark(nc.tensor.transpose(psD[:, 0, 2 * P:3 * P], kr_t[:, 0:P], ident), "turned")
                    dves.wait(pe, "cache")
                    acts.wait(pe, "outs")
                    S = MLA
                    pes, acts, dves = S
                    pes.open(pe)
                    with pe.Fori(0, HEADS) as i:
                        uq = take_panel(pe, "mla", i, 0)
                        pes.mark(products(pe, psA, uq, 3, 192, 0, h_hi, h_lo, CQ_AT, T, TH), "gqn")
                        products(pe, psB, uq, 3, 192, 64, h_hi, h_lo, CQ_AT, T, TH).then_inc(gemm_done, 1)
                        ukv = take_panel(pe, "mla", i, 1)
                        pes.mark(products(pe, psC, ukv, 2, 256, 0, h_hi, h_lo, CKV_AT, NKEY, NKEY // 2), "gkn")
                        acts.wait(pe, "evqn", i)
                        pes.mark(sum_rows(psA, ones, [sq_n], TH), "ssqn")
                        acts.wait(pe, "evqr", i)
                        pes.mark(sum_rows(psB, blocks, [sq_r], TH), "ssqr")
                        dves.wait_turns(pe, i)
                        products(pe, psD, ukv, 2, 256, P, h_hi, h_lo, CKV_AT, NKEY, NKEY // 2).then_inc(gemm_done, 1)
                        acts.wait(pe, "evkn", i)
                        pes.mark(sum_rows(psC, ones, [sq_k], NKEY // 2), "sskn")
                        dves.wait(pe, "qr", i)
                        pes.mark(nc.tensor.matmul(psB[:, 0, 0:NLAT], rot64, qr_t[:, NCTX:T], start=True, stop=True),
                                 "rotqr")
                        acts.wait(pe, "evv", i)
                        for k in range(6):
                            last = nc.tensor.transpose(psD[:, k // 4, (k % 4) * P:(k % 4 + 1) * P],
                                                       vt_t[:, k * P:(k + 1) * P], ident)
                        pes.mark(last, "turned_v")
                        dves.wait(pe, "qroped", i)
                        acts.wait(pe, "v", i)
                        attention_pe(pe, S, "", 1, [[(qn_t, kn_t), (qr_t[64:P], kr_t[64:P])]], mV, m_PT, m_PTp,
                                     m_probs, i)
                elif layer == 1:
                    S = DIF
                    pes, acts, dves = S
                    pes.open(pe)
                    with pe.Fori(0, HEADS) as i:
                        h_tile(psA, "diff", i, 0).then_inc(gemm_done, 1)
                        h_tile(psB, "diff", i, 1).then_inc(gemm_done, 1)
                        dves.wait_turns(pe, i)
                        acts.wait(pe, "evq", i)
                        pes.mark(sum_rows(psC, blocks, [dsq_q], TH), "ssq")
                        h_tile(psA, "diff", i, 2).then_inc(gemm_done, 1)
                        acts.wait(pe, "evk", i)
                        pes.mark(sum_rows(psD, blocks, [dsq_k], TH), "ssk")
                        dves.wait(pe, "q", i)
                        pes.mark(nc.tensor.matmul(psC[:, 0, 0:NLAT], rot64, dq_t[:, NCTX:T], start=True, stop=True),
                                 "rotq")
                        acts.wait(pe, "evv", i)
                        pe.wait_ge(cache_in, i * 32 + 16 * (2))
                        for k in range(1, 5):
                            nc.tensor.transpose(psA[:, 0, (k - 1) * P:k * P], dvt[:, k * P:(k + 1) * P], ident)
                        nc.tensor.transpose(psA[:, 1, 0:P], dvt[:, 0:P], ident)
                        pes.mark(nc.tensor.transpose(psA[:, 1, P:2 * P], d_cache, ident), "turned_v")
                        dves.wait(pe, "k", i)
                        nc.tensor.matmul(psD[:, 0, 0:NLAT], rot64, dk_t[:, NCTX:T], start=True, stop=True)
                        pes.mark(nc.tensor.transpose(psD[:, 1, 0:P], dk_t[:, 0:P], ident), "rotk")
                        dves.wait(pe, "kroped", i)
                        acts.wait(pe, "v", i)
                        acts.wait(pe, "kout", i)
                        attention_pe(pe, S, "", 2, [[(dq_t[0:64], dk_t[0:64])], [(dq_t[64:P], dk_t[64:P])]],
                                     dV, d_PT, d_PTp, d_probs, i)
                        acts.wait(pe, "evo", i)
                        pes.mark(sum_rows(psC, ones, [dsq_q], TH), "sso")
                elif layer == 2:
                    S = GKV
                    pes, acts, dves = S
                    for j in range(2):
                        h_tile(psA, "gqa_kv", j, 0).then_inc(gemm_done, 1)
                        h_tile(psB, "gqa_kv", j, 1).then_inc(gemm_done, 1)
                        acts.wait(pe, "evk", j)
                        pes.mark(sum_rows(psC, ones, [gsq], TH), "ssk")
                        dves.wait(pe, "k", j)
                        pes.mark(nc.tensor.matmul(psC[:, 0, 0:NLAT], rot128, gk_t[j][:, NCTX:T], start=True, stop=True),
                                 "rotk")
                        acts.wait(pe, "evv", j)
                        pe.wait_ge(gcache_in, 16 * 4)
                        for k in range(1, 5):
                            nc.tensor.transpose(psD[:, 0, (k - 1) * P:k * P], gvt[:, k * P:(k + 1) * P], ident)
                        nc.tensor.transpose(psD[:, 1, 0:P], gvt[:, 0:P], ident)
                        nc.tensor.transpose(psD[:, 1, P:2 * P], g_cache[j], ident)
                        pes.mark(nc.tensor.transpose(psD[:, 1, 2 * P:3 * P], gk_t[j][:, 0:P], ident), "turned_v")
                        dves.wait(pe, "kroped", j)
                        acts.wait(pe, "v", j)
                    S = GQA
                    pes, acts, dves = S
                    pes.open(pe)
                    with pe.Fori(0, HEADS // 2) as i:
                        for k, p in enumerate("ab"):
                            if k == 0:
                                dves.wait_turns(pe, i)
                            else:
                                dves.wait(pe, "ao", i)
                            h_tile(psA, "gqa", i, k).then_inc(gemm_done, 1)
                            acts.wait(pe, p + "evq", i)
                            pes.mark(sum_rows(psC, ones, [gsq], TH), p + "ssq")
                            dves.wait(pe, p + "q", i)
                            pes.mark(nc.tensor.matmul(psC[:, 0, 0:NLAT], rot128, gq_t[:, NCTX:T],
                                                      start=True, stop=True), p + "rotq")
                            dves.wait(pe, p + "qroped", i)
                            attention_pe(pe, S, p, 1, [[(gq_t, gk_t[k])]], gV[k], g_PT, g_PTp, g_probs, i)
                else:
                    S = LRU
                    pes, acts, dves = S
                    pes.open(pe)
                    with pe.Fori(0, KT) as i:
                        acts.wait_turns(pe, i)
                        h_tile(psA, "lru", i, 0).then_inc(gemm_done, 1)
                        h_tile(psB, "lru", i, 1).then_inc(gemm_done, 1)
                        slot = take_panel(pe, "lru", i, 2)
                        dves.wait(pe, "y", i)
                        for g, name in enumerate(("rf", "if", "rb", None)):
                            ps = psum[g]
                            for p_, (w, r) in enumerate(((w_hi, y_hi), (w_hi, y_lo), (w_lo, y_hi))):
                                for b in range(2):
                                    last = nc.tensor.matmul(ps[:, b, 0:LW // 2], w[slot][:, g * P:(g + 1) * P],
                                                            r[:, b * (LW // 2):(b + 1) * (LW // 2)],
                                                            start=(p_ == 0), stop=(p_ == 2))
                            if name:
                                pes.mark(last, name)
                            else:
                                last.then_inc(gemm_done, 1)
                if layer < 3:
                    dves.wait_turns(pe, len_turns(layer))
                else:
                    dves.wait_turns(pe, KT)
                project(f"wo{layer}", KT)

                norm(2 * layer + 1)
                pe.wait_ge(h_done, (2 * layer + 2) * KT)
                for ch, size in enumerate(FFN_CHUNKS):
                    base = layer * (FFN // P) + sum(FFN_CHUNKS[:ch])
                    pe.wait_ge(x_done, x_tiles[0])
                    with pe.Fori(0, size) as i:
                        pe.wait_ge(silu_done, i + (base + 1))
                        h_tile(psA, f"in{layer}.{ch}", i, 0).then_inc(gemm_done, 1)
                        pe.wait_ge(hidden_done, i + (base + 1))
                        h_tile(psB, f"in{layer}.{ch}", i, 1).then_inc(gemm_done, 1)
                        if mod_at(layer, ch, False):
                            mod_turn(mod_at(layer, ch, False), i)
                    pe.wait_ge(hidden_done, base + size + 1)
                    project(f"out{layer}.{ch}", size, mod_at(layer, ch, True))

            pe.wait_ge(x_done, x_tiles[0])
            for t in range(QT):
                if t >= 2:
                    pe.wait_ge(y_copied, t - 1)
                d = psum[t % 2]
                for kt in range(KT):
                    last = nc.tensor.transpose(d[:, kt // 4, (kt % 4) * P:(kt % 4 + 1) * P],
                                               x[:, kt * T + t * P:kt * T + (t + 1) * P], ident)
                last.then_inc(y_turned, 1)

        @block.scalar
        def _(act):
            pes, acts, dves = PRE
            act.sem_inc(first_mod_turned, 2)
            pes.wait(act, "vecs")
            act.sem_inc(silu_done, 1)
            acts.mark(nc.scalar.activation(vecs[:, :], psC[:, 0, 0:2 * P], ACT.Copy), "vecs")
            act.drain()
            sc = silu_c[:, :].rearrange("p (k c) -> p k c", c=2)
            nc.scalar.activation(sc[:, :, 0], vecs[:, VEC["cctx"]:VEC["cctx"] + KT], ACT.Silu)
            acts.mark(nc.scalar.activation(sc[:, :, 1], vecs[:, VEC["c"]:VEC["c"] + KT], ACT.Silu), "silu")
            dves.wait(act, "lamsum")
            acts.mark(nc.scalar.activation(lam_tmp[0:1, 2:4], lam_tmp[0:1, 0:2], ACT.Exp), "lamexp")
            nc.scalar.activation(l_s[:, 0, :].bitcast(F32) if False else lru_small[:, 64:80],
                                 vecs[:, VEC["lam"]:VEC["lam"] + 16], ACT.Abs)
            act.drain()
            acts.mark(nc.scalar.activation(lru_small[:, 80:96], lru_small[:, 64:80], ACT.Exp, scale=-1.0), "sp")

            with act.Fori(0, 6) as i:
                for b in range(2):
                    act.wait_ge(first_mod_used, i * 2 + (b + 1))
                    act.wait_ge(first_mod_turned, i * 2 + (b + 1))
                    nc.scalar.activation(first_mod_rows[:, b, :], psum[b][0:2, 0, :],
                                         ACT.Copy).then_inc(first_mod_row, 1)

            x_tiles = [KT]
            outs = [0]

            def norm(n):
                layer, which = n // 2, n % 2
                act.wait_ge(x_done, x_tiles[0])
                if outs[0]:
                    act.wait_ge(outs_done, outs[0])
                nc.scalar.preload_act_table_set("natural_log_exp_and_others")
                for kt in range(KT):
                    nc.scalar.activation(squares[:, kt * T:(kt + 1) * T], x[:, kt * T:(kt + 1) * T],
                                         ACT.Square).then_inc(square_done, 1)
                act.wait_ge(sums_done, n + 1)
                rstd(act, rms, psC, D, TH).then_inc(rstd_done, 1)
                for kt in range(KT):
                    act.wait_ge(scaled_done, n * KT + kt + 1)
                    for cond, (t0, t1) in enumerate(((0, NCTX), (NCTX, T))):
                        last = nc.scalar.activation(h_hi[:, kt * T + t0:kt * T + t1],
                                                    squares[:, kt * T + t0:kt * T + t1], ACT.Identity,
                                                    bias=mod_col(layer, 3 * which, kt, cond))
                    last.then_inc(h_hi_done, 1)
                act.wait_ge(h_done, (n + 1) * KT)

            def exp_and_ln():
                nc.scalar.preload_act_table_set("natural_log_exp_and_others")

            def g_panel(name, i, j):
                act.wait_ge(gemm_done, phases[name].number(i, j))

            for layer in range(DEPTH):
                norm(2 * layer)
                if layer < 3:
                    exp_and_ln()
                if layer == 0:
                    S = MIN
                    pes, acts, dves = S
                    act.dma_start(mla_cache, a["cache_mla_ckv"][0, 0]).then_inc(const_in, 16)
                    dves_pre = PRE[2]
                    act.wait_ge(kr_cleared, 1)
                    act.dma_start(kr_cache[:, 64:P], a["cache_mla_krope"][0, 0]).then_inc(const_in, 16)
                    for t in range(6):
                        g_panel("mla_in", t // 2, t % 2)
                        acts.mark(evacuate(mla_raw[t], mla_sq[t], psum[t % 2], TH), f"m{t}")
                    pes.wait(act, "sscq")
                    acts.mark(rstd(act, mla_rs[0], psC, MLA_QR, TH), "rscq")
                    pes.wait(act, "ssckv")
                    acts.mark(rstd(act, mla_rs[1], psD, MLA_KVR, TH), "rsckv")
                    pes.wait(act, "sskr")
                    acts.mark(rstd(act, mla_rs[2], psA, 64, TH), "rskr")
                    pes.wait(act, "turned")
                    acts.mark(nc.scalar.activation(mla_out, psD[:, 0, 0:3 * P], ACT.Copy), "outs")
                    act.wait_ge(acts.sem, len(acts.names))
                    act.dma_start(a["new_mla_ckv"][0, 0], mla_out[:, 0:2 * P]).then_inc(outs_done, 16)
                    act.dma_start(a["new_mla_krope"][0, 0], mla_out[:, 2 * P + 64:3 * P]).then_inc(outs_done, 16)
                    outs[0] = 32
                    S = MLA
                    pes, acts, dves = S
                    acts.open(act)
                    act.wait_ge(MIN[2].sem, len(MIN[2].names))
                    act.wait_ge(outs_done, 32)
                    with act.Fori(0, HEADS) as i:
                        pes.wait(act, "gqn", i)
                        acts.mark(evacuate(qn_t, sq_n, psA, TH), "evqn")
                        g_panel("mla", i, 0)
                        acts.mark(evacuate(qr_t, sq_r, psB, TH), "evqr")
                        pes.wait(act, "gkn", i)
                        acts.mark(evacuate(kn_t, sq_k, psC, NKEY // 2), "evkn")
                        pes.wait(act, "ssqn", i)
                        acts.mark(rstd(act, sq_n, psA, P, TH), "rsqn")
                        pes.wait(act, "ssqr", i)
                        acts.mark(rstd(act, sq_r, psB, 64, TH), "rsqr")
                        g_panel("mla", i, 1)
                        acts.mark(nc.scalar.activation(halves(vt_t, NKEY // 2), psD[:, :, 0:NKEY // 2], ACT.Copy),
                                  "evv")
                        pes.wait(act, "sskn", i)
                        acts.mark(rstd(act, sq_k, psC, P, NKEY // 2), "rskn")
                        pes.wait(act, "turned_v", i)
                        nc.scalar.activation(mV[:, 0:4 * P], psD[:, 0, :], ACT.Copy)
                        acts.mark(nc.scalar.activation(mV[:, 4 * P:6 * P], psD[:, 1, 0:2 * P], ACT.Copy), "v")
                        attention_act(act, S, "", 1, 192 ** -0.5, m_PT, m_PTp, m_probs, m_stats, i)
                        pes.wait(act, "pv", i)
                elif layer == 1:
                    S = DIF
                    pes, acts, dves = S
                    acts.open(act)
                    kc = a["cache_diff_k"][0, 0].rearrange("t h c d -> t (h c d)")
                    vc = a["cache_diff_v"][0, 0].rearrange("t h d -> t (h d)")
                    ko = a["new_diff_k"][0, 0].rearrange("t h c d -> t (h c d)")
                    vo = a["new_diff_v"][0, 0].rearrange("t h d -> t (h d)")
                    with act.Fori(0, HEADS) as i:
                        act.wait_ge(outs_done, i * 32 + 32)
                        act.dma_start(d_cache, kc[:, bass.ds(i * P, P)]).then_inc(cache_in, 16)
                        act.dma_start(dV[:, 5 * P:6 * P], vc[:, bass.ds(i * P, P)]).then_inc(cache_in, 16)
                        g_panel("diff", i, 0)
                        acts.mark(evacuate(dq_t, dsq_q, psA, TH), "evq")
                        g_panel("diff", i, 1)
                        acts.mark(evacuate(dk_t[:, 0:T], dsq_k, psB, TH), "evk")
                        pes.wait(act, "ssq", i)
                        acts.mark(rstd(act, dsq_q, psC, 64, TH), "rsq")
                        g_panel("diff", i, 2)
                        acts.mark(nc.scalar.activation(halves(dvt, TH), psA[:, :, 0:TH], ACT.Copy), "evv")
                        pes.wait(act, "ssk", i)
                        acts.mark(rstd(act, dsq_k, psD, 64, TH), "rsk")
                        pes.wait(act, "turned_v", i)
                        nc.scalar.activation(dV[:, P:5 * P], psA[:, 0, :], ACT.Copy)
                        nc.scalar.activation(dV[:, 0:P], psA[:, 1, 0:P], ACT.Copy)
                        acts.mark(nc.scalar.activation(dk_t[:, T:NKEY], psA[:, 1, P:2 * P], ACT.Copy), "v")
                        pes.wait(act, "rotk", i)
                        acts.mark(nc.scalar.activation(d_kout, psD[:, 1, 0:P], ACT.Copy), "kout")
                        acts.wait(act, "kout", i)
                        act.dma_start(ko[:, bass.ds(i * P, P)], d_kout).then_inc(outs_done, 16)
                        act.dma_start(vo[:, bass.ds(i * P, P)], dV[:, 0:P]).then_inc(outs_done, 16)
                        attention_act(act, S, "", 2, 64 ** -0.5, d_PT, d_PTp, d_probs, d_stats, i)
                        pes.wait(act, "pv", i)
                        nc.scalar.activation(dq_t[:, NCTX:T], psD[:, 0, 0:NLAT], ACT.Copy)
                        nc.scalar.activation(dq_t[:, 0:NCTX], psD[:, 1, 0:P], ACT.Copy)
                        nc.scalar.activation(dsq_q[:, NCTX:T], psD[:, 0, 0:NLAT], ACT.Square)
                        acts.mark(nc.scalar.activation(dsq_q[:, 0:NCTX], psD[:, 1, 0:P], ACT.Square), "evo")
                        pes.wait(act, "sso", i)
                        acts.mark(rstd(act, dsq_q, psC, P, TH), "rso")
                        dves.wait(act, "o", i)
                    outs[0] += 32 * HEADS
                elif layer == 2:
                    S = GKV
                    pes, acts, dves = S
                    kc = a["cache_gqa_k"][0, 0]
                    vc = a["cache_gqa_v"][0, 0]
                    act.wait_ge(outs_done, outs[0])
                    for j in range(2):
                        act.dma_start(g_cache[j], kc[:, j, :]).then_inc(gcache_in, 16)
                        act.dma_start(gV[j][:, 5 * P:6 * P], vc[:, j, :]).then_inc(gcache_in, 16)
                    for j in range(2):
                        g_panel("gqa_kv", j, 0)
                        acts.mark(evacuate(gk_t[j][:, 0:T], gsq, psA, TH), "evk")
                        g_panel("gqa_kv", j, 1)
                        acts.mark(nc.scalar.activation(halves(gvt, TH), psB[:, :, 0:TH], ACT.Copy), "evv")
                        pes.wait(act, "ssk", j)
                        acts.mark(rstd(act, gsq, psC, P, TH), "rsk")
                        pes.wait(act, "turned_v", j)
                        nc.scalar.activation(gV[j][:, P:5 * P], psD[:, 0, :], ACT.Copy)
                        nc.scalar.activation(gV[j][:, 0:P], psD[:, 1, 0:P], ACT.Copy)
                        nc.scalar.activation(gk_t[j][:, T:NKEY], psD[:, 1, P:2 * P], ACT.Copy)
                        acts.mark(nc.scalar.activation(g_kout[j], psD[:, 1, 2 * P:3 * P], ACT.Copy), "v")
                        acts.wait(act, "v", j)
                        act.dma_start(a["new_gqa_k"][0, 0][:, j, :], g_kout[j]).then_inc(outs_done, 16)
                        act.dma_start(a["new_gqa_v"][0, 0][:, j, :], gV[j][:, 0:P]).then_inc(outs_done, 16)
                        dves.wait(act, "k", j)
                    outs[0] += 64
                    S = GQA
                    pes, acts, dves = S
                    acts.open(act)
                    with act.Fori(0, HEADS // 2) as i:
                        for k, p in enumerate("ab"):
                            g_panel("gqa", i, k)
                            acts.mark(evacuate(gq_t, gsq, psA, TH), p + "evq")
                            pes.wait(act, p + "ssq", i)
                            acts.mark(rstd(act, gsq, psC, P, TH), p + "rsq")
                            attention_act(act, S, p, 1, P ** -0.5, g_PT, g_PTp, g_probs, g_stats, i)
                            pes.wait(act, p + "pv", i)
                else:
                    S = LRU
                    pes, acts, dves = S
                    acts.open(act)
                    act.wait_ge(outs_done, outs[0])
                    act.wait_ge(lru_ready, 1)
                    with act.Fori(0, KT) as i:
                        dves.wait_turns(act, i)
                        g_panel("lru", i, 0)
                        acts.mark(nc.scalar.activation(halves(l_gelu, TH), psA[:, :, 0:TH], ACT.Gelu_apprx_tanh),
                                  "gelu")
                        g_panel("lru", i, 1)
                        nc.scalar.activation(l_xp[:, 1:1 + NCTX], psB[:, 0, 0:NCTX], ACT.Copy)
                        nc.scalar.activation(l_xp[:, LAT0 + 1:LAT0 + 1 + TH - NCTX], psB[:, 0, NCTX:TH], ACT.Copy)
                        acts.mark(nc.scalar.activation(l_xp[:, LAT0 + 1 + TH - NCTX:LAT0 + 1 + NLAT], psB[:, 1, 0:TH],
                                                       ACT.Copy), "xp")
                        hw = LW // 2
                        for d, name in enumerate(("tf", "tb")):
                            if d == 0:
                                pes.wait(act, "if", i)
                            else:
                                g_panel("lru", i, 2)
                            for g, dst in enumerate((l_tr[d], l_ti[d])):
                                last = nc.scalar.activation(halves(dst, hw), psum[2 * d + g][:, :, 0:hw], ACT.Tanh,
                                                            bias=hb[:, bass.ds(i + (2 * d + g) * KT, 1)], scale=0.5)
                            acts.mark(last, name)
                        act.drain()
                        for d in range(2):
                            s_ = sp2[:, bass.ds(i + d * KT, 1)]
                            last = nc.scalar.activation(l_th[d], l_tr[d], ACT.Tanh, bias=s_, scale=s_)
                        acts.mark(last, "th")
                        act.drain()
                        for d in range(2):
                            last = nc.scalar.activation(l_sq[d], l_th[d], ACT.Sqrt)
                        acts.mark(last, "sq")
                x_tiles[0] += KT
                norm(2 * layer + 1)
                if layer == 3:
                    with nc.allow_non_contiguous_dma(reason="1024 floats per direction"):
                        act.dma_start(a["new_lru_h"][0, 0].rearrange("d (k p) -> p d k", p=P),
                                      l_state.rearrange("p (d k) -> p d k", d=2)).then_inc(outs_done, 16)
                    outs[0] += 16
                for ch, size in enumerate(FFN_CHUNKS):
                    base = layer * (FFN // P) + sum(FFN_CHUNKS[:ch])
                    with act.Fori(0, size) as i:
                        g_panel(f"in{layer}.{ch}", i, 0)
                        act.wait_ge(hidden_done, i + (base + 1))
                        nc.scalar.activation(halves(gate_silu, TH), psA[:, :, 0:TH], ACT.Silu).then_inc(silu_done, 1)
                    x_tiles[0] += KT
            for t in range(QT):
                act.wait_ge(y_turned, t + 1)
                nc.scalar.activation(y_tok[:, t * D:(t + 1) * D].rearrange("p (b n) -> p b n", b=2),
                                     psum[t % 2][:, :, :], ACT.Copy).then_inc(y_copied, 1)
                act.wait_ge(y_copied, t + 1)
                dst = a["y_prompt"][0] if t == 0 else a["y_sample"][0, (t - 1) * P:t * P, :]
                act.dma_start(dst, y_tok[:, t * D:(t + 1) * D]).then_inc(y_out, 16)
            act.wait_ge(y_out, 16 * QT)
            act.wait_ge(outs_done, outs[0])

        @block.vector
        def _(dve):
            pes, acts, dves = PRE
            dve.sem_inc(mod_summed, 1)
            dve.sem_inc(hidden_done, 1)
            for k in range(4):
                last = nc.vector.memset(vec_rows[k], 0.0)
            nc.vector.memset(eps, EPS)
            dve.drain()
            dves.mark(nc.vector.memset(lam_tmp[:, :], 0.0), "ready")
            dve.drain()
            dve.wait_ge(const_in, 16 * 23)
            lr = lam_row[0:1, :].rearrange("p (a b d) -> p a b d", a=2, b=2)
            nc.vector.tensor_tensor(lam_tmp[0:1, 4:132].rearrange("p (a d) -> p a d", a=2), lr[:, :, 0, :],
                                    lr[:, :, 1, :], ALU.mult)
            dve.drain()
            dves.mark(nc.vector.tensor_reduce(lam_tmp[0:1, 0:2],
                                              lam_tmp[0:1, 4:132].rearrange("p (a d) -> p a d", a=2),
                                              AX.X, ALU.add), "lamsum")
            acts.wait(dve, "lamexp")
            nc.vector.tensor_tensor(lam_tmp[0:1, 4:5], lam_tmp[0:1, 3:4], lam_tmp[0:1, 2:3], ALU.subtract)
            dve.drain()
            dves.mark(nc.vector.tensor_scalar(lam_tmp[0:1, 4:5], lam_tmp[0:1, 4:5], -LAMBDA_INIT, None, ALU.add),
                      "lamdiff")
            pes.wait(dve, "lam")
            dves.mark(nc.vector.tensor_copy(neg_lambda, psC[:, 1, 0:1]), "lamall")
            pes.wait(dve, "bmod")
            dves.mark(nc.vector.tensor_copy(bmod[:, :], psD[:, 0, 0:192]), "bmod")
            acts.wait(dve, "sp")
            ys, s_, s2, acc, tmp = (lru_small[:, 80 + 16 * k:96 + 16 * k] for k in range(5))
            nc.vector.tensor_scalar(tmp, ys, 2.0, None, ALU.add)
            dve.drain()
            nc.vector.reciprocal(tmp, tmp)
            dve.drain()
            nc.vector.tensor_tensor(s_, ys, tmp, ALU.mult)
            dve.drain()
            nc.vector.tensor_tensor(s2, s_, s_, ALU.mult)
            nc.vector.memset(acc, 1.0 / 17)
            dve.drain()
            for k in (15, 13, 11, 9, 7, 5, 3, 1):
                nc.vector.tensor_tensor(acc, acc, s2, ALU.mult)
                dve.drain()
                nc.vector.tensor_scalar(acc, acc, 1.0 / k, None, ALU.add)
                dve.drain()
            nc.vector.tensor_tensor(acc, acc, s_, ALU.mult)
            nc.vector.tensor_scalar(tmp, vecs[:, VEC["lam"]:VEC["lam"] + 16], -1.0, 0.0, ALU.mult, ALU.max)
            dve.drain()
            nc.vector.tensor_scalar(tmp, tmp, 2.0, None, ALU.mult)
            dve.drain()
            nc.vector.scalar_tensor_tensor(sp2, acc, 4.0, tmp, ALU.mult, ALU.add)
            nc.vector.tensor_scalar(hb, vecs[:, VEC["bgate"]:VEC["bgate"] + 32], 0.5, None, ALU.mult)
            dves.mark(nc.vector.tensor_scalar(small[:, 43:44], vecs[:, VEC["dsub"]:VEC["dsub"] + 1],
                                              1.0 - LAMBDA_INIT, None, ALU.mult), "splog")
            dve.drain()

            def vec(name, k=0, n=1):
                return vecs[:, VEC[name] + k:VEC[name] + k + n]

            for kt in range(KT):
                pes.wait(dve, f"x{kt}")
                nc.vector.tensor_copy(x[:, kt * T:kt * T + 4 * P], psum[kt % 2][:, 0, :])
                nc.vector.tensor_copy(x[:, kt * T + 4 * P:(kt + 1) * T], psum[kt % 2][:, 1, 0:P]).then_inc(x_done, 1)
            x_tiles = [KT]
            dve.wait_ge(first_mod_turned, 2 + 12)
            for cond in range(2):
                last = nc.vector.tensor_tensor(mods[0][:, :].rearrange("p (k c) -> p k c", c=2)[:, :, cond],
                                               psC[:, 1, 0:96].rearrange("p (k c) -> p k c", c=2)[:, :, cond],
                                               bmod[:, 0:48], ALU.add)
            last.then_inc(mod_ready, 1)
            dve.wait_ge(mod_ready, 1)

            def mod_products(mod, i, b):
                n = MCHUNKS // 2 * (mod[0] - 1) + mod[1] // 2
                dve.wait_ge(mod_in[b], i * 16 + 16 * (n + 1))
                for kt in range(KT):
                    for cond in range(2):
                        w_ = mod_w[b][:, kt * MCOLS:(kt + 1) * MCOLS].rearrange("p (h n) -> p h n", h=2)
                        c_ = silu_c[:, kt * 2 + cond:kt * 2 + cond + 1]
                        acc = mod_acc_[:, :, cond, :]
                        if kt == 0:
                            last = nc.vector.tensor_scalar(acc, w_, c_, None, ALU.mult)
                        else:
                            last = nc.vector.scalar_tensor_tensor(acc, w_, c_, acc, ALU.mult, ALU.add)
                    if kt < KT - 1:
                        dve.drain()
                last.then_inc(mod_mac, 1)

            def mod_sums(mod, i, b):
                n = MCHUNKS * (mod[0] - 1) + mod[1]
                dve.wait_ge(mod_turned, i * 2 + (n + b + 1))
                nc.vector.tensor_reduce(mods[mod[0] % 2][:, bass.ds(i * 8 + (mod[1] + b) * 4, 4)],
                                        psC[:, 0, :].rearrange("p (k n) -> p k n", k=4), AX.X,
                                        ALU.add).then_inc(mod_summed, 1)

            def mod_bias(layer):
                m = mods[layer % 2][:, :].rearrange("p (k c) -> p k c", c=2)
                dve.wait_ge(mod_summed, MCHUNKS * layer + 1)
                for cond in range(2):
                    nc.vector.tensor_tensor(m[:, :, cond], m[:, :, cond], bmod[:, layer * 48:layer * 48 + 48], ALU.add)
                dve.drain()

            def norm(n):
                layer, which = n // 2, n % 2
                if layer and which == 0:
                    mod_bias(layer)
                m = mods[layer % 2][:, :].rearrange("p (v k c) -> p v k c", v=6, c=2)
                for cond in range(2):
                    nc.vector.scalar_tensor_tensor(gains[:, cond * KT:(cond + 1) * KT], m[:, 3 * which + 1, :, cond],
                                                   1.0, vec("gn1" if which == 0 else "gn2", layer * KT, KT),
                                                   ALU.add, ALU.mult)
                dve.drain()
                dve.wait_ge(rstd_done, n + 1)
                for kt in range(KT):
                    for cond, (t0, t1) in enumerate(((0, NCTX), (NCTX, T))):
                        last = nc.vector.scalar_tensor_tensor(
                            squares[:, kt * T + t0:kt * T + t1], x[:, kt * T + t0:kt * T + t1],
                            gains[:, cond * KT + kt:cond * KT + kt + 1], rms[:, t0:t1], ALU.mult, ALU.mult)
                    last.then_inc(scaled_done, 1)
                for kt in range(KT):
                    dve.wait_ge(h_hi_done, n * KT + kt + 1)
                    for cond, (t0, t1) in enumerate(((0, NCTX), (NCTX, T))):
                        o = kt * T
                        last = nc.vector.scalar_tensor_tensor(
                            h_lo[:, o + t0:o + t1], squares[:, o + t0:o + t1], mod_col(layer, 3 * which, kt, cond),
                            h_hi[:, o + t0:o + t1].bitcast(F32), ALU.add, ALU.subtract)
                    last.then_inc(h_done, 1)
                dve.wait_ge(h_done, (n + 1) * KT)

            def add_projection(name, layer, kind, mod=None):
                m = mods[layer % 2]
                k_turns = 2 if mod else 1
                with dve.Fori(0, KT // 2 // k_turns) as i:
                    for k in range(k_turns):
                        if mod:
                            mod_products(mod, i, k)
                        for j in range(2):
                            q = k * 2 + j
                            dve.wait_ge(gemm_done, i * (2 * k_turns) + (phases[name].first + q + 1))
                            for cond, b, c0, t0, n in ((0, 0, 0, 0, NCTX), (1, 0, NCTX, NCTX, TH - NCTX),
                                                       (1, 1, 0, TH, TH)):
                                xs = x[:, bass.ds(i * (2 * k_turns * T) + (q * T + t0), n)]
                                last = nc.vector.scalar_tensor_tensor(
                                    xs, psum[j][:, b, c0:c0 + n],
                                    m[:, bass.ds(i * (4 * k_turns) + ((kind * KT + q) * 2 + cond), 1)], xs,
                                    ALU.mult, ALU.add)
                            last.then_inc(x_done, 1)
                        if mod:
                            mod_sums(mod, i, k)
                x_tiles[0] += KT
                dve.wait_ge(x_done, x_tiles[0])

            for layer in range(DEPTH):
                norm(2 * layer)
                if layer == 0:
                    S = MIN
                    pes, acts, dves = S
                    nc.vector.memset(kr_cache, 0.0).then_inc(kr_cleared, 1)
                    acts.wait(dve, "rscq")
                    for t in range(3):
                        normed(mla_raw[t], vec("cq", t), mla_rs[0])
                    dve.drain()
                    for t in range(3):
                        nc.vector.tensor_copy(h_hi[:, CQ_AT + t * T:CQ_AT + (t + 1) * T], mla_raw[t])
                    dve.drain()
                    for t in range(3):
                        last = nc.vector.tensor_tensor(h_lo[:, CQ_AT + t * T:CQ_AT + (t + 1) * T], mla_raw[t],
                                                       h_hi[:, CQ_AT + t * T:CQ_AT + (t + 1) * T].bitcast(F32),
                                                       ALU.subtract)
                    dves.mark(last, "cq")
                    acts.wait(dve, "rsckv")
                    for t in range(2):
                        normed(mla_raw[3 + t], vec("ckv", t), mla_rs[1])
                    dve.drain()
                    for t in range(2):
                        o = CKV_AT + t * NKEY
                        last = split(dve, h_hi[:, o:o + T], h_lo[:, o:o + T], mla_raw[3 + t])
                    dves.mark(last, "ckv")
                    acts.wait(dve, "rskr")
                    dves.mark(nc.vector.scalar_tensor_tensor(kr_t[:, 0:T], mla_raw[5], vec("mqr", 1), mla_rs[2],
                                                             ALU.mult, ALU.mult), "kr")
                    pes.wait(dve, "rotkr")
                    dves.mark(roped(dve, kr_t, psB, cos64, sin64, mla_tmp), "kr_roped")
                    pes.wait(dve, "turned")
                    for t in range(2):
                        o = CKV_AT + t * NKEY + T
                        split(dve, h_hi[:, o:o + P], h_lo[:, o:o + P], psC[:, 0, t * P:(t + 1) * P])
                    dves.mark(nc.vector.tensor_copy(kr_t[:, T:NKEY], psC[:, 0, 2 * P:3 * P]), "cache")
                    S = MLA
                    pes, acts, dves = S
                    dves.open(dve)
                    with dve.Fori(0, HEADS) as i:
                        acts.wait(dve, "rsqn", i)
                        dves.mark(normed(qn_t, vec("mqk", 0), sq_n), "qn")
                        acts.wait(dve, "rsqr", i)
                        dves.mark(normed(qr_t, vec("mqr", 0), sq_r), "qr")
                        acts.wait(dve, "rskn", i)
                        dves.mark(normed(kn_t, vec("mqk", 1), sq_k), "kn")
                        pes.wait(dve, "rotqr", i)
                        dves.mark(roped(dve, qr_t, psB, cos64, sin64, m_tmp), "qroped")
                        attention_dve(dve, S, "", 1, 192 ** -0.5, m_probs, m_stats, i)
                        pes.wait(dve, "pv", i)
                        dves.mark(split_head(dve, i), "o")
                elif layer == 1:
                    S = DIF
                    pes, acts, dves = S
                    dves.open(dve)
                    with dve.Fori(0, HEADS) as i:
                        acts.wait(dve, "rsq", i)
                        dves.mark(normed(dq_t, vec("dqk", 0), dsq_q), "q")
                        acts.wait(dve, "rsk", i)
                        dves.mark(normed(dk_t[:, 0:T], vec("dqk", 1), dsq_k), "k")
                        pes.wait(dve, "rotq", i)
                        dves.mark(roped(dve, dq_t, psC, cos64, sin64, d_tmp), "qroped")
                        dve.drain()
                        pes.wait(dve, "rotk", i)
                        dves.mark(roped(dve, dk_t, psD, cos64, sin64, d_tmp), "kroped")
                        attention_dve(dve, S, "", 2, 64 ** -0.5, d_probs, d_stats, i)
                        acts.wait(dve, "rso", i)
                        normed(dq_t, small[:, 43:44], dsq_q)
                        dve.drain()
                        o = bass.ds(i * T, T)
                        dves.mark(split(dve, act_hi[:, o], act_lo[:, o], dq_t), "o")
                elif layer == 2:
                    S = GKV
                    pes, acts, dves = S
                    for j in range(2):
                        acts.wait(dve, "rsk", j)
                        dves.mark(normed(gk_t[j][:, 0:T], vec("gqk", 1), gsq), "k")
                        pes.wait(dve, "rotk", j)
                        dves.mark(roped(dve, gk_t[j], psC, cos128, sin128, g_tmp), "kroped")
                        dve.drain()
                    S = GQA
                    pes, acts, dves = S
                    dves.open(dve)
                    with dve.Fori(0, HEADS // 2) as i:
                        for k, p in enumerate("ab"):
                            acts.wait(dve, p + "rsq", i)
                            dves.mark(normed(gq_t, vec("gqk", 0), gsq), p + "q")
                            pes.wait(dve, p + "rotq", i)
                            dves.mark(roped(dve, gq_t, psC, cos128, sin128, g_tmp), p + "qroped")
                            attention_dve(dve, S, p, 1, P ** -0.5, g_probs, g_stats, i)
                            pes.wait(dve, p + "pv", i)
                            dves.mark(split_head(dve, i + k * 4), p + "o")
                else:
                    S = LRU
                    pes, acts, dves = S
                    dves.open(dve)
                    nc.vector.memset(l_xp, 0.0).then_inc(lru_ready, 1)
                    with dve.Fori(0, KT) as i:
                        acts.wait(dve, "xp", i)
                        cw = [vecs[:, bass.ds(i + (VEC["convw"] + k * KT), 1)] for k in range(4)]
                        cb = vecs[:, bass.ds(i + VEC["convb"], 1)]
                        nc.vector.tensor_scalar(l_y, l_xp[:, 0:LW], cw[0], cb, ALU.mult, ALU.add)
                        for k in range(1, 4):
                            dve.drain()
                            nc.vector.scalar_tensor_tensor(l_y, l_xp[:, k:k + LW], cw[k], l_y, ALU.mult, ALU.add)
                        dve.drain()
                        dves.mark(split(dve, y_hi[:, :], y_lo[:, :], l_y), "y")
                        acts.wait(dve, "tb", i)
                        for d in range(2):
                            nc.vector.scalar_tensor_tensor(l_ti[d], l_ti[d], 1.0, l_y, ALU.add, ALU.mult)
                        acts.wait(dve, "th", i)
                        for d in range(2):
                            nc.vector.tensor_scalar(l_h[d], l_th[d], 1.0, None, ALU.add)
                            nc.vector.tensor_scalar(l_a[d], l_th[d], -1.0, 1.0, ALU.mult, ALU.add)
                        dve.drain()
                        for d in range(2):
                            nc.vector.reciprocal(l_h[d], l_h[d])
                        dve.drain()
                        for d in range(2):
                            nc.vector.tensor_tensor(l_a[d], l_a[d], l_h[d], ALU.mult)
                            nc.vector.tensor_tensor(l_ti[d], l_ti[d], l_h[d], ALU.mult)
                        dve.drain()
                        acts.wait(dve, "sq", i)
                        for d in range(2):
                            nc.vector.tensor_tensor(l_ti[d], l_ti[d], l_sq[d], ALU.mult)
                        dve.drain()
                        for d in range(2):
                            for t0, n, init in ((0, NCTX, 0.0), (LAT0, NLAT, vecs[:, bass.ds(i + (VEC["h0"] + d * KT), 1)])):
                                o, a_, u_ = (b_[d][:, t0:t0 + n] for b_ in (l_h, l_a, l_ti))
                                if d:
                                    o, a_, u_ = o[:, ::-1], a_[:, ::-1], u_[:, ::-1]
                                nc.vector.tensor_tensor_scan(o, a_, u_, init, ALU.mult, ALU.add)
                        dve.drain()
                        nc.vector.tensor_copy(l_state[:, bass.ds(i, 1)], l_h[0][:, NCTX - 1:NCTX])
                        nc.vector.tensor_copy(l_state[:, bass.ds(i + KT, 1)], l_h[1][:, 0:1])
                        for t0, n, g0 in ((0, NCTX, 0), (LAT0, NLAT, NCTX)):
                            nc.vector.tensor_tensor(l_y[:, t0:t0 + n], l_h[0][:, t0:t0 + n], l_h[1][:, t0:t0 + n], ALU.add)
                        dve.drain()
                        for t0, n, g0 in ((0, NCTX, 0), (LAT0, NLAT, NCTX)):
                            nc.vector.tensor_tensor(l_gelu[:, g0:g0 + n], l_y[:, t0:t0 + n], l_gelu[:, g0:g0 + n], ALU.mult)
                        dve.drain()
                        o = bass.ds(i * T, T)
                        dves.mark(split(dve, act_hi[:, o], act_lo[:, o], l_gelu), "o")
                        dve.drain()
                add_projection(f"wo{layer}", layer, 2)
                norm(2 * layer + 1)
                for ch, size in enumerate(FFN_CHUNKS):
                    base = layer * (FFN // P) + sum(FFN_CHUNKS[:ch])
                    mod = mod_at(layer, ch, False)
                    k_turns = 2 if mod else 1
                    with dve.Fori(0, size // k_turns) as i:
                        for k in range(k_turns):
                            if mod:
                                mod_products(mod, i, k)
                            dve.wait_ge(silu_done, i * k_turns + (base + k + 2))
                            dve.wait_ge(gemm_done, i * (2 * k_turns) + (phases[f"in{layer}.{ch}"].first + 2 * k + 2))
                            dve.wait_ge(hidden_done, i * k_turns + (base + k + 1))
                            nc.vector.tensor_tensor(halves(prod, TH), halves(gate_silu, TH), psB[:, :, 0:TH], ALU.mult)
                            dve.drain()
                            o = bass.ds(i * (k_turns * T) + k * T, T)
                            split(dve, act_hi[:, o], act_lo[:, o], prod).then_inc(hidden_done, 1)
                            if mod:
                                mod_sums(mod, i, k)
                    add_projection(f"out{layer}.{ch}", layer, 5, mod_at(layer, ch, True))


def len_turns(layer):
    return (HEADS, HEADS, HEADS // 2)[layer]


def host_tables():
    ident = np.eye(P, dtype=np.float32)
    ones = np.ones((P, P), np.float32)
    blocks = np.kron(np.eye(2), np.ones((64, 64))).astype(np.float32)

    def rotation(dim):
        r = np.zeros((P, P), np.float32)
        for m in range(P):
            if m % dim < dim // 2:
                r[m + dim // 2, m] = -1.0
            else:
                r[m - dim // 2, m] = 1.0
        return r

    consts = np.concatenate([ident, ones, blocks, rotation(64), rotation(128)], axis=1)

    def rotary(dim):
        grid_w, n_freq = 64, dim // 4
        tok = np.arange(NLAT)
        inv = np.float32(10000.0) ** (-np.arange(n_freq, dtype=np.float32) / n_freq)
        ang = np.concatenate([(tok // grid_w).astype(np.float32)[:, None] * inv,
                              (tok % grid_w).astype(np.float32)[:, None] * inv], axis=1)
        full = np.tile(ang, (1, P // (dim // 2))).T.astype(np.float32)
        return np.cos(full), np.sin(full)

    tables = np.concatenate([*rotary(64), *rotary(128)], axis=1).astype(np.float32)
    return np.ascontiguousarray(consts), np.ascontiguousarray(tables)


_OUTS = [("y_prompt", (1, 128, 1024)), ("y_sample", (1, 512, 1024)), ("new_mla_ckv", (1, 1, 128, 256)),
         ("new_mla_krope", (1, 1, 128, 64)), ("new_diff_k", (1, 1, 128, 8, 2, 64)),
         ("new_diff_v", (1, 1, 128, 8, 128)), ("new_gqa_k", (1, 1, 128, 2, 128)),
         ("new_gqa_v", (1, 1, 128, 2, 128)), ("new_lru_h", (1, 1, 2, 1024))]


def kernel(**inputs):
    import concourse.bacc as _bacc
    from concourse.bass_utils import run_bass_kernel_spmd as _run

    nc = _bacc.Bacc("TRN2", target_bir_lowering=False, num_devices=1)
    arrays, aps = {}, {}
    consts, tables = host_tables()
    for name, value in list(inputs.items()) + [("consts", consts), ("tables", tables)]:
        v = np.ascontiguousarray(value)
        arrays[f"in_{name}"] = v
        aps[name] = nc.dram_tensor(f"in_{name}", v.shape, mybir.dt.from_np(v.dtype), kind="ExternalInput").ap()
    for name, shape in _OUTS:
        aps[name] = nc.dram_tensor(f"out_{name}", shape, F32, kind="ExternalOutput").ap()
    build(nc, aps)
    r = _run(nc, [arrays], core_ids=[0])
    return tuple(r.results[0][f"out_{name}"] for name, _ in _OUTS)
```

```python
import math
from contextlib import ExitStack

import numpy as np
import concourse.bass as bass
from concourse import mybir

F32 = mybir.dt.float32
F32R = mybir.dt.float32r
ALU = mybir.AluOpType
ACT = mybir.ActivationFunctionType
AX = mybir.AxisListType

P = 128
D = 1024
KT = D // P
NCTX, NLAT = 128, 512
T = NCTX + NLAT
TH = T // 2
NKEY = T + 128
DEPTH = 4
EPS = 1e-6
FFN = 2816
FFN_CHUNKS = (8, 8, 6)
HEADS = 8
MLA_QR, MLA_KVR = 384, 256
CQ_AT, CKV_AT = 0, 3 * T
QT = 5
LW = T + 4
LAT0 = 131
SLOT = 8 * P
WORK = 13312
MCOLS = 256
MCHUNKS = 6 * D // MCOLS
LAMBDA_INIT = 0.8 - 0.6 * math.exp(-0.3)

VEC_ROWS = [("gn1", 32), ("gn2", 32), ("cq", 3), ("ckv", 2), ("convb", 8), ("convw", 32), ("dsub", 1),
            ("gqk", 2), ("mqk", 2), ("mqr", 2), ("dqk", 2), ("pad", 10),
            ("bgate", 32), ("lam", 16), ("h0", 16), ("c", 8), ("cctx", 8), ("pad2", 48)]
VEC = {}
_at = 0
for _name, _n in VEC_ROWS:
    VEC[_name] = _at
    _at += _n
assert VEC["bgate"] == P and _at == 2 * P


class Head:

    def __init__(self, i, k, per=2):
        self.i, self.k, self.per = i, k, per

    def at(self, n, c):
        return self.i * (self.per * n) + (self.k * n + c)

    def next(self):
        return Head(self.i, self.k + 1, self.per)

    def last(self):
        return Head(self.i, self.k - 1, self.per)


class Steps:

    def __init__(self, sem, names, base=0):
        self.sem, self.names, self.base, self.k = sem, names, base, 0

    def open(self, eng):
        assert self.base >= 1
        eng.sem_inc(self.sem, self.base)

    def mark(self, ins, name):
        assert self.names[self.k % len(self.names)] == name, (name, self.names[self.k % len(self.names)])
        self.k += 1
        ins.then_inc(self.sem, 1)

    def wait(self, eng, name, turn=0):
        if isinstance(turn, Head):
            eng.wait_ge(self.sem, turn.at(len(self.names), self.base + self.names.index(name) + 1))
            return
        eng.wait_ge(self.sem, turn * len(self.names) + (self.base + self.names.index(name) + 1))

    def wait_turns(self, eng, turn):
        eng.wait_ge(self.sem, turn * len(self.names) + self.base)


class Phase:

    def __init__(self, turns, slots, shape, first, landed):
        self.turns, self.slots, self.shape, self.first = turns, slots, shape, first
        self.landed = dict(landed)
        self.n = len(slots)

    def of_head(self, h, j=0, per=1):
        return h.at(per, self.first + j + 1)

    def number(self, turn, j):
        return turn * self.n + (self.first + j + 1)


def plan_panels():
    phases, first, landed = {}, 0, {0: 0, 1: 0, 2: 0}

    def add(name, turns, slots, shape):
        nonlocal first
        phases[name] = Phase(turns, slots, shape, first, landed)
        for s in slots:
            landed[s] += turns
        first += turns * len(slots)

    for layer in range(DEPTH):
        if layer == 0:
            add("mla_in", 3, (0, 1), [(KT, P)] * 2)
            add("mla", HEADS, (0, 1), [(3, 192), (2, 256)])
        elif layer == 1:
            add("diff", HEADS, (2, 0, 1), [(KT, P)] * 3)
        elif layer == 2:
            add("gqa_kv", 2, (0, 1), [(KT, P)] * 2)
            add("gqa", HEADS // 2, (0, 1), [(KT, P)] * 2)
        else:
            add("lru", KT, (2, 0, 1), [(KT, P), (KT, P), (4, P)])
        add(f"wo{layer}", KT // 2, (0, 1), [(KT, P)] * 2)
        for c, size in enumerate(FFN_CHUNKS):
            add(f"in{layer}.{c}", size, (0, 1), [(KT, P)] * 2)
            add(f"out{layer}.{c}", KT // 2, (0, 1), [(size, P)] * 2)
    return phases


def pipelined_names(comps):
    def each(name, t):
        return [f"{name}{t}.{c}" for c in range(comps)]

    pe, act = each("scores", 0) + each("scores", 1), each("exp", 0) + each("exp", 1)
    for t in range(QT - 2):
        pe += [f"turned{t}"] + each("scores", t + 2)
        act += [f"pt{t}"] + each("exp", t + 2)
    pe += [f"turned{QT - 2}", f"turned{QT - 1}"]
    act += [f"pt{QT - 2}", f"pt{QT - 1}"]
    dve = sum([each("max", t) + [f"probs{t}"] for t in range(QT)], [])
    return pe, act, dve


def build(nc, a):
    phases = plan_panels()

    with ExitStack() as ctx:
        def sb(name, cols, dt=F32):
            return ctx.enter_context(nc.sbuf_tensor(name, [P, cols], dt))

        def sem(name):
            return ctx.enter_context(nc.semaphore(name))

        x = sb("x", KT * T)
        h_hi, h_lo = sb("h_hi", KT * T, F32R), sb("h_lo", KT * T, F32R)
        act_hi, act_lo = sb("act_hi", KT * T, F32R), sb("act_lo", KT * T, F32R)
        raw = [sb(f"raw{s}", SLOT) for s in range(3)]
        w_hi = [sb(f"w_hi{s}", SLOT, F32R) for s in range(3)]
        w_lo = [sb(f"w_lo{s}", SLOT, F32R) for s in range(3)]
        y_hi, y_lo = sb("y_hi", LW, F32R), sb("y_lo", LW, F32R)
        work = sb("work", WORK)
        consts = sb("consts", 5 * P)
        tables = sb("tables", 4 * NLAT)
        vecs = sb("vecs", 2 * P)
        bmod = sb("bmod", 192)
        mods = [sb(f"mods{b}", 96) for b in range(2)]
        gains = sb("gains", 32)
        silu_c = sb("silu_c", 16)
        small = sb("small", 64)
        lru_small = sb("lru_small", 256)
        psum = [ctx.enter_context(nc.psum_tensor(f"ps{n}", [P, 2, 512], F32)) for n in "ABCD"]
        psA, psB, psC, psD = psum

        ident, ones, blocks, rot64, rot128 = (consts[:, k * P:(k + 1) * P] for k in range(5))
        cos64, sin64, cos128, sin128 = (tables[:, k * NLAT:(k + 1) * NLAT] for k in range(4))
        eps = small[:, 40:41]
        neg_lambda = small[:, 41:42]

        class Carve:

            def __init__(self):
                self.at = 0

            def __call__(self, n):
                self.at += n
                assert self.at <= WORK, self.at
                return work[:, self.at - n:self.at]

        const_in = sem("const_in")
        x_in, tables_in = sem("x_in"), sem("tables_in")
        raw_in = [sem(f"raw_in{s}") for s in range(3)]
        first_mod_in = [sem(f"first_mod_in{b}") for b in range(3)]
        first_mod_row = sem("first_mod_row")
        mod_in = [sem(f"mod_in{b}") for b in range(2)]
        pool_hi = sem("pool_hi")
        split_done = sem("split_done")
        gemm_done = sem("gemm_done")
        first_mod_used = sem("first_mod_used")
        first_mod_turned = sem("first_mod_turned")
        mod_ready = sem("mod_ready")
        mod_mac = sem("mod_mac")
        mod_turned = sem("mod_turned")
        mod_summed = sem("mod_summed")
        scratch_free = sem("scratch_free")
        x_done = sem("x_done")
        square_done = sem("square_done")
        sums_done = sem("sums_done")
        rstd_done = sem("rstd_done")
        scaled_done = sem("scaled_done")
        h_hi_done = sem("h_hi_done")
        h_done = sem("h_done")
        silu_done = sem("silu_done")
        hidden_done = sem("hidden_done")
        pre_pe, pre_act, pre_dve = sem("pre_pe"), sem("pre_act"), sem("pre_dve")
        cache_in, gcache_in = sem("cache_in"), sem("gcache_in")
        kr_cleared, lru_ready = sem("kr_cleared"), sem("lru_ready")
        outs_done = sem("outs_done")
        y_turned, y_copied, y_out = sem("y_turned"), sem("y_copied"), sem("y_out")

        def steps(name, pe, act, dve, base=1):
            return tuple(Steps(sem(f"{name}_{e}"), names, base) for e, names in (("pe", pe), ("act", act), ("dve", dve)))

        PRE = [Steps(pre_pe, ["x0", "x1", "x2", "x3", "x4", "x5", "x6", "x7", "vecs", "bmod", "lam"]),
               Steps(pre_act, ["vecs", "silu", "lamexp", "sp"]),
               Steps(pre_dve, ["ready", "lamsum", "lamdiff", "lamall", "bmod", "splog"])]
        MIN = steps("mla_in", ["sscq", "ssckv", "sskr", "rotkr", "turned"],
                    [f"m{t}" for t in range(6)] + ["rscq", "rsckv", "rskr", "outs"],
                    ["cq", "ckv", "kr", "kr_roped", "cache"], 0)
        GKV = steps("gqa_kv", ["ssk", "rotk", "turned_v"], ["evk", "evv", "rsk", "v"], ["k", "kroped"], 0)

        def pipeline(name, comps, pe, act, dve):
            att = tuple(Steps(sem(f"{name}_att_{e}"), n, len(n)) for e, n in zip(("pe", "act", "dve"), pipelined_names(comps)))
            return att, Steps(sem(f"{name}_pv"), ["pv"], 1), Steps(sem(f"{name}_out"), ["o"], 1), steps(f"{name}_prep", pe, act, dve)

        MLA = pipeline("mla", 1, ["gqn", "gkn", "ssqn", "ssqr", "sskn", "rotqr", "turned_v"],
                       ["evqn", "evqr", "evkn", "rsqn", "rsqr", "rskn", "evv", "v"], ["qn", "qr", "kn", "qroped"])
        DIF = pipeline("diff", 2, ["ssq", "ssk", "rotq", "rotk", "turned_v"],
                       ["evq", "evk", "rsq", "rsk", "evv", "kout", "v"], ["q", "k", "qroped", "kroped"])
        DIF_SSO = Steps(sem("diff_sso"), ["sso"], 1)
        DIF_NORM = Steps(sem("diff_norm"), ["evo", "rso"], 2)
        GQA = pipeline("gqa", 1, ["ssq", "rotq"], ["evq", "rsq"], ["q", "qroped"])
        LRU_PE = Steps(sem("lru_pe"), ["rb", "rf", "if"], 1)
        LRU_XP = Steps(sem("lru_xp"), ["xp"], 1)
        LRU_ACT = Steps(sem("lru_act"), ["gelu", "trb", "t", "a2", "sq"], 5)
        LRU_Y = Steps(sem("lru_y"), ["y"], 1)
        LRU_DVE = Steps(sem("lru_dve"), ["m", "u", "h", "g", "o"], 5)

        def products(pe, out, slot, kts, cols, c0, rhs_hi, rhs_lo, at, stride, half, part=None,
                     fresh=None, before_last=None):
            last = None
            for kt in part or range(kts):
                if fresh is not None:
                    pe.wait_ge(h_done, fresh * KT + kt + 1)
                if before_last and kt == kts - 1:
                    before_last()
                for p, (w, r) in enumerate(((w_hi, rhs_hi), (w_hi, rhs_lo), (w_lo, rhs_hi))):
                    for b in range(2):
                        o = at + kt * stride + b * half
                        last = nc.tensor.matmul(out[:, b, 0:half], w[slot][:, kt * cols + c0:kt * cols + c0 + P],
                                                r[:, o:o + half], start=(kt == 0 and p == 0),
                                                stop=(kt == kts - 1 and p == 2))
            return last

        def take_panel(pe, name, turn, j):
            ph = phases[name]
            pe.wait_ge(split_done, ph.number(turn, j))
            return ph.slots[j]

        def sum_rows(out, ones_, pieces, half):
            last = None
            for b in range(2):
                for k, sq in enumerate(pieces):
                    last = nc.tensor.matmul(out[:, b, 0:half], ones_, sq[:, b * half:(b + 1) * half],
                                            start=(k == 0), stop=(k == len(pieces) - 1))
            return last

        def item(h, t, comps, back):
            flat = t * comps - back
            if flat < 0:
                h, flat = h.last(), flat + QT * comps
            return h, flat // comps, flat % comps

        def score_bank(h, t, c, comps):
            return psum[((h.k % 2 * QT + t) * comps + c) % 2]

        def pe_scores(pe, A, h, t, pairs):
            pes, acts, dves = A
            comps = len(pairs)
            for c in range(comps):
                h_, t_, c_ = item(h, t, comps, 2 - c)
                acts.wait(pe, f"exp{t_}.{c_}", h_)
                s = score_bank(h, t, c, comps)
                q0 = 128 + t * P if t < 4 else 0
                for b, k0, n in ((0, 128, TH), (1, 128 + TH, TH)) if t < 4 else ((0, 0, P),):
                    for m, (q, k) in enumerate(pairs[c]):
                        last = nc.tensor.matmul(s[:, b, 0:n], q[:, q0:q0 + P], k[:, k0:k0 + n],
                                                start=(m == 0), stop=(m == len(pairs[c]) - 1))
                pes.mark(last, f"scores{t}.{c}")

        def pe_turned(pe, A, free, h, t, probs):
            pes, acts, dves = A
            dves.wait(pe, f"probs{t}", h)
            if t == 0:
                free[0].wait(pe, free[1], h.last())
            else:
                acts.wait(pe, f"pt{t - 1}", h)
            for k in range(5 if t < 4 else 1):
                last = nc.tensor.transpose(psC[:, k // 4, (k % 4) * P:(k % 4 + 1) * P],
                                           probs[(h.k % 2 * QT + t) % 2][0][:, k * P:(k + 1) * P], ident)
            pes.mark(last, f"turned{t}")

        def pe_output(pe, A, pv, h, V, PT, PTp):
            A[1].wait(pe, "pt4", h)
            for k in range(5):
                nc.tensor.matmul(psC[:, 0, 0:NLAT], V[:, (k + 1) * P:(k + 2) * P], PT[:, k * NLAT:(k + 1) * NLAT],
                                 start=(k == 0), stop=(k == 4))
            pv.mark(nc.tensor.matmul(psC[:, 1, 0:P], V[:, 0:P], PTp, start=True, stop=True), "pv")

        def act_exp(act, A, h, t, comps, scale, probs, stats):
            pes, acts, dves = A
            mx, nm, sm, rs = stats
            h_, t_, _ = item(h, t, 1, 2)
            pes.wait(act, f"turned{t_}", h_)
            for c in range(comps):
                j = t * comps + c
                dves.wait(act, f"max{t}.{c}", h)
                s, p_ = score_bank(h, t, c, comps), probs[(h.k % 2 * QT + t) % 2][c]
                o, i_ = (halves(p_, TH), s[:, :, 0:TH]) if t < 4 else (p_[:, 0:P], s[:, 0, 0:P])
                acts.mark(nc.scalar.activation(o, i_, ACT.Exp, bias=nm[:, j:j + 1], scale=scale,
                                               accum_out=sm[:, j:j + 1]), f"exp{t}.{c}")

        def act_pt(act, A, h, t, PT, PTp):
            A[0].wait(act, f"turned{t}", h)
            if t < 4:
                dst = PT.rearrange("p (k q) -> p k q", k=5)
                nc.scalar.activation(dst[:, 0:4, t * P:(t + 1) * P],
                                     psC[:, 0, :].rearrange("p (k q) -> p k q", k=4), ACT.Copy)
                last = nc.scalar.activation(dst[:, 4, t * P:(t + 1) * P], psC[:, 1, 0:P], ACT.Copy)
            else:
                last = nc.scalar.activation(PTp, psC[:, 0, 0:P], ACT.Copy)
            A[1].mark(last, f"pt{t}")

        def halves(ap, half):
            return ap.rearrange("p (b n) -> p b n", b=2)

        def evacuate(out, sq, ps, half):
            nc.scalar.activation(halves(out, half), ps[:, :, 0:half], ACT.Copy)
            return nc.scalar.activation(halves(sq, half), ps[:, :, 0:half], ACT.Square)

        def rstd(act, out, ps, count, half):
            nc.scalar.activation(halves(out, half), ps[:, :, 0:half], ACT.Ln, bias=eps, scale=1.0 / count)
            act.drain()
            return nc.scalar.activation(out, out, ACT.Exp, scale=-0.5)

        def dve_tile(dve, A, h, t, comps, scale, probs, stats):
            pes, acts, dves = A
            mx, nm, sm, rs = stats
            for c in range(comps):
                j = t * comps + c
                s = score_bank(h, t, c, comps)
                pes.wait(dve, f"scores{t}.{c}", h)
                if t < 4:
                    nc.vector.tensor_reduce(mx[:, j:j + 1], s[:, :, 0:TH], AX.XY, ALU.max)
                else:
                    nc.vector.tensor_reduce(mx[:, j:j + 1], s[:, 0, 0:P], AX.X, ALU.max)
                dve.drain()
                dves.mark(nc.vector.tensor_scalar(nm[:, j:j + 1], mx[:, j:j + 1], -scale, None, ALU.mult), f"max{t}.{c}")
            n = T if t < 4 else P
            j = t * comps
            acts.wait(dve, f"exp{t}.{comps - 1}", h)
            nc.vector.reciprocal(rs[:, j:j + comps], sm[:, j:j + comps])
            dve.drain()
            p_ = probs[(h.k % 2 * QT + t) % 2]
            last = nc.vector.tensor_scalar(p_[0][:, 0:n], p_[0][:, 0:n], rs[:, j:j + 1], None, ALU.mult)
            if comps == 2:
                nc.vector.tensor_scalar(rs[:, j + 1:j + 2], rs[:, j + 1:j + 2], neg_lambda, None, ALU.mult)
                dve.drain()
                last = nc.vector.scalar_tensor_tensor(p_[0][:, 0:n], p_[1][:, 0:n], rs[:, j + 1:j + 2], p_[0][:, 0:n],
                                                      ALU.mult, ALU.add)
            dves.mark(last, f"probs{t}")

        def normed(raw_, g, rs):
            return nc.vector.scalar_tensor_tensor(raw_, raw_, g, rs, ALU.mult, ALU.mult)

        def roped(dve, t_, ps, cos, sin, tmp):
            nc.vector.tensor_tensor(tmp, ps[:, 0, 0:NLAT], sin, ALU.mult)
            nc.vector.tensor_tensor(t_[:, NCTX:T], t_[:, NCTX:T], cos, ALU.mult)
            dve.drain()
            return nc.vector.tensor_tensor(t_[:, NCTX:T], t_[:, NCTX:T], tmp, ALU.add)

        def split(dve, hi, lo, src):
            nc.vector.tensor_copy(hi, src)
            dve.drain()
            return nc.vector.tensor_tensor(lo, src, hi.bitcast(F32), ALU.subtract)

        def split_head(dve, at):
            nc.vector.tensor_copy(act_hi[:, bass.ds(at + NCTX, NLAT)], psC[:, 0, 0:NLAT])
            nc.vector.tensor_copy(act_hi[:, bass.ds(at, NCTX)], psC[:, 1, 0:P])
            dve.drain()
            nc.vector.tensor_tensor(act_lo[:, bass.ds(at + NCTX, NLAT)], psC[:, 0, 0:NLAT],
                                    act_hi[:, bass.ds(at + NCTX, NLAT)].bitcast(F32), ALU.subtract)
            return nc.vector.tensor_tensor(act_lo[:, bass.ds(at, NCTX)], psC[:, 1, 0:P],
                                           act_hi[:, bass.ds(at, NCTX)].bitcast(F32), ALU.subtract)

        c = Carve()
        x_tok = c(QT * D)
        vec_rows = [c(P) for _ in range(4)]
        lam_row = c(256)
        lam_tmp = c(132)

        c = Carve()
        scaled = c(KT * T)
        rms = c(T)
        square, square_sum = work[:, WORK - 2 * T:WORK - T], work[:, WORK - T:WORK]
        square0, square_sum0 = work[:, QT * D + 1024:QT * D + 1024 + T], raw[2][:, 0:T]

        c = Carve()
        mla_raw = [c(T) for _ in range(6)]
        mla_sq = [c(T) for _ in range(6)]
        mla_rs = mla_sq[0], mla_sq[3], mla_sq[5]
        mla_cache = c(2 * P)
        kr_cache = c(P)
        mla_tmp = c(NLAT)
        c = Carve()
        qn_t, qr_t, kn_t = [c(T), c(T)], [c(T), c(T)], [c(NKEY), c(NKEY)]
        sq_n, sq_r = c(T), c(T)
        sq_k = vt_t = c(NKEY)
        mV = [c(6 * P), c(6 * P)]
        m_probs = [[c(T)], [c(T)]]
        m_PT, m_PTp = c(5 * NLAT), c(P)
        m_tmp = c(NLAT)
        m_stats = [c(QT) for _ in range(4)]
        kr_t = work[:, WORK - NKEY:WORK]
        mla_out = work[:, WORK - NKEY - 384:WORK - NKEY]
        assert c.at <= WORK - NKEY

        c = Carve()
        dq_t, dk_t = [c(T), c(T)], [c(NKEY), c(NKEY)]
        dsq_q = c(T)
        dsq_k = dvt = c(T)
        dV = [c(6 * P), c(6 * P)]
        do_t, do_sq = c(T), c(T)
        d_probs = [[c(T), c(T)], [c(T), c(T)]]
        d_PT, d_PTp = c(5 * NLAT), c(P)
        d_tmp = c(NLAT)
        d_cache = c(P)
        d_kout = c(P)
        d_stats = [c(2 * QT) for _ in range(4)]

        c = Carve()
        gk_t = [c(NKEY), c(NKEY)]
        gV = [c(6 * P), c(6 * P)]
        g_cache = [c(P), c(P)]
        g_kout = [c(P), c(P)]
        gsq, gvt = c(T), c(T)
        gq_t = [c(T), c(T)]
        g_probs = [[c(T)], [c(T)]]
        g_PT, g_PTp = c(5 * NLAT), c(P)
        g_tmp = c(NLAT)
        g_stats = [c(QT) for _ in range(4)]

        c = Carve()
        l_xp = c(LW + 4)
        l_gelu = c(KT * T)
        l_y = c(LW)
        l_tr = [c(LW), c(LW)]
        l_ti = [c(LW), c(LW)]
        l_th = [c(LW), c(LW)]
        l_a = [c(LW), c(LW)]
        sp4 = lru_small[:, 0:16]
        neg_sp4 = lru_small[:, 144:160]
        hb = lru_small[:, 16:48]
        l_state = lru_small[:, 48:64]

        c = Carve()
        gate_silu = c(T)
        prod = c(T)
        mod_w = [c(KT * MCOLS) for _ in range(2)]
        mod_acc = c(2 * MCOLS)
        mod_acc_ = mod_acc.rearrange("p (h c n) -> p h c n", h=2, c=2)
        first_mod_w = [work[:, k * KT * 512:(k + 1) * KT * 512] for k in (2, 1, 0)]
        first_mod_rows = work[0:2, WORK - 2 * 512:WORK].rearrange("p (b n) -> p b n", b=2)
        c = Carve()
        y_tok = c(QT * D)

        def mod_col(layer, kind, tile, cond):
            k = (kind * KT + tile) * 2 + cond
            return mods[layer % 2][:, k:k + 1]

        def mod_at(layer, ch, out):
            if layer + 1 == DEPTH or ch > 1:
                return None
            return layer + 1, ch * (8 + KT // 2) + (8 if out else 0)
        assert FFN_CHUNKS[0] == FFN_CHUNKS[1] == 8 and 2 * (8 + KT // 2) == MCHUNKS

        block = ctx.enter_context(nc.Block())

        @block.sync
        def _(sp):
            def panels(name, source, mod=None, order=None):
                ph = phases[name]
                unroll = 2 if mod else 1

                def turn(g, k):
                    for j in order or range(ph.n):
                        s = ph.slots[j]
                        kts, cols = ph.shape[j]
                        behind = ph.first + k * ph.n + j + 1 - ph.n
                        if not isinstance(g, int) or behind > 0:
                            sp.wait_ge(split_done, g * (unroll * ph.n) + behind)
                        sp.dma_start(raw[s][:, 0:kts * cols].rearrange("p (k n) -> p k n", k=kts),
                                     source(g * unroll + k, j)).then_inc(raw_in[s], 16)
                    if mod:
                        n = MCHUNKS * (mod[0] - 1) + mod[1] + k
                        if isinstance(g, int) and mod[1] == 0:
                            if k == 0:
                                sp.wait_ge(h_done, 2 * mod[0] * KT)
                        else:
                            sp.wait_ge(mod_mac, g * 2 + (n - 1))
                        sp.dma_start(mod_w[k].rearrange("p (k n) -> p k n", k=KT),
                                     a["w_mod"][mod[0]].rearrange("(k p) n -> p k n", p=P)[
                                         :, :, bass.ds(g * (2 * MCOLS) + (mod[1] + k) * MCOLS, MCOLS)]
                                     ).then_inc(mod_in[k], 16)

                peeled = 1 if ph.first == 0 or (mod and mod[1] == 0) else 0
                if peeled:
                    for k in range(unroll):
                        turn(0, k)
                with sp.Fori(peeled, ph.turns // unroll) as g:
                    for k in range(unroll):
                        turn(g, k)

            sp.dma_start(consts[:, :], a["consts"]).then_inc(const_in, 16)
            sp.wait_ge(const_in, 16)
            pre = PRE
            pre[2].wait(sp, "ready")
            rows = [("gn1", a["g_norm1"].rearrange("l (k n) -> (l k) n", n=P)),
                    ("gn2", a["g_norm2"].rearrange("l (k n) -> (l k) n", n=P)),
                    ("cq", a["mla_g_cq"].rearrange("l (k n) -> (l k) n", n=P)),
                    ("ckv", a["mla_g_ckv"].rearrange("l (k n) -> (l k) n", n=P)),
                    ("dsub", a["diff_g_sub"]),
                    ("gqk", a["gqa_g_qk"][0]),
                    ("mqk", a["mla_g_qk"][0][:, 0:P]),
                    ("c", a["c"].rearrange("l (k n) -> (l k) n", n=P)),
                    ("cctx", a["c_ctx"].rearrange("(k n) -> k n", n=P))]
            for name, src in rows:
                r = VEC[name]
                tile = vec_rows[r // P]
                sp.dma_start(tile[r % P:r % P + src.shape[0], :], src).then_inc(const_in, 16)
            for half in range(2):
                for name, src in (("mqr", a["mla_g_qk"][0][:, P:P + 64]), ("dqk", a["diff_g_qk"][0])):
                    r = VEC[name]
                    sp.dma_start(vec_rows[0][r:r + 2, half * 64:half * 64 + 64], src).then_inc(const_in, 16)

            w = a["w_mod"][0].rearrange("(k p) n -> p k n", p=P)
            for b in range(3):
                if b == 1:
                    sp.wait_ge(scratch_free, 1)
                sp.dma_start(first_mod_w[b].rearrange("p (k n) -> p k n", k=KT),
                             w[:, :, b * 512:(b + 1) * 512]).then_inc(first_mod_in[b], 16)
            with sp.Fori(1, 4) as i:
                for b in range(3):
                    sp.wait_ge(first_mod_used, i * 3 + (b + 1 - 3))
                    sp.dma_start(first_mod_w[b].rearrange("p (k n) -> p k n", k=KT),
                                 w[:, :, bass.ds(i * 1536 + b * 512, 512)]).then_inc(first_mod_in[b], 16)

            for layer in range(DEPTH):
                if layer == 0:
                    win = a["mla_w_in"][0].rearrange("(k p) n -> p k n", p=P)
                    uq = a["mla_w_uq"][0].rearrange("(k p) n -> p k n", p=P)
                    ukv = a["mla_w_ukv"][0].rearrange("(k p) n -> p k n", p=P)
                    wo = a["mla_w_o"][0]
                    ph = phases["mla_in"]
                    for t in range(6):
                        c0 = t * P if t < 5 else 576
                        if t >= 2:
                            sp.wait_ge(split_done, t - 1)
                        sp.dma_start(raw[t % 2][:, :].rearrange("p (k n) -> p k n", k=KT),
                                     win[:, :, c0:c0 + P]).then_inc(raw_in[t % 2], 16)
                    panels("mla", lambda i, j: uq[:, :, bass.ds(i * 192, 192)] if j == 0
                           else ukv[:, :, bass.ds(i * 256, 256)])
                elif layer == 1:
                    win = a["diff_w_in"][0].rearrange("(k p) n -> p k n", p=P)
                    wo = a["diff_w_o"][0]
                    kc = a["cache_diff_k"][0, 0].rearrange("t h c d -> t (h c d)")
                    vc = a["cache_diff_v"][0, 0].rearrange("t h d -> t (h d)")
                    panels("diff", lambda i, j: win[:, :, bass.ds(i * P + j * D, P)])
                elif layer == 2:
                    win = a["gqa_w_in"][0].rearrange("(k p) n -> p k n", p=P)
                    wo = a["gqa_w_o"][0]
                    panels("gqa_kv", lambda i, j: win[:, :, bass.ds(i * P + (D + j * 256), P)])
                    panels("gqa", lambda i, j: win[:, :, bass.ds(i * P + j * 512, P)])
                else:
                    win = a["lru_w_in"][0].rearrange("(k p) n -> p k n", p=P)
                    wo = a["lru_w_out"][0]
                    wg = a["lru_w_gate"][0].rearrange("d g b k j -> k (d g) b j")
                    panels("lru", lambda i, j: win[:, :, bass.ds(i * P + (1 - j) * D, P)] if j < 2
                           else wg[:, :, bass.ds(i, 1), :].rearrange("k g o j -> k g (o j)"), order=(1, 0, 2))
                wov = wo.rearrange("(k p) n -> p k n", p=P)
                panels(f"wo{layer}", lambda i, j: wov[:, :, bass.ds(i * 2 * P + j * P, P)])
                f_in = a["w_ffn_in"][layer].rearrange("(k p) n -> p k n", p=P)
                f_out = a["w_ffn_out"][layer].rearrange("(k p) n -> p k n", p=P)
                m0 = 0
                for ch, size in enumerate(FFN_CHUNKS):
                    panels(f"in{layer}.{ch}", lambda i, j: f_in[:, :, bass.ds(i * P + (m0 * P + j * FFN), P)],
                           mod_at(layer, ch, False))
                    panels(f"out{layer}.{ch}", lambda i, j: f_out[:, m0:m0 + size, bass.ds(i * 2 * P + j * P, P)],
                           mod_at(layer, ch, True))
                    m0 += size

        @block.gpsimd
        def _(pool):
            def turn(name, i, peeled=False):
                ph = phases[name]
                for j, s in enumerate(ph.slots):
                    n = ph.shape[j][0] * ph.shape[j][1]
                    pool.wait_ge(raw_in[s], i * 16 + 16 * (ph.landed[s] + 1))
                    if not peeled:
                        pool.wait_ge(gemm_done, i * ph.n + (ph.first + j + 1 - ph.n))
                    nc.gpsimd.tensor_tensor(w_hi[s][:, 0:n], raw[s][:, 0:n], ones[:, 0:1].to_broadcast([P, n]),
                                            ALU.mult).then_inc(pool_hi, 1)
                    pool.wait_ge(pool_hi, i * ph.n + (ph.first + j + 1))
                    nc.gpsimd.tensor_tensor(w_lo[s][:, 0:n], raw[s][:, 0:n], w_hi[s][:, 0:n].bitcast(F32),
                                            ALU.subtract).then_inc(split_done, 1)

            pool.wait_ge(const_in, 16)
            for name, ph in phases.items():
                if ph.first == 0:
                    turn(name, 0, peeled=True)
                    with pool.Fori(1, ph.turns) as i:
                        turn(name, i)
                else:
                    with pool.Fori(0, ph.turns) as i:
                        turn(name, i)

        @block.tensor
        def _(pe):
            def first_modulation():
                with pe.Fori(0, 2) as i:
                    for q in range(7):
                        if q < 6:
                            pe.wait_ge(first_mod_in[q % 3], i * 32 + (16 * (q // 3) + 16))
                            for kt in range(KT):
                                last = nc.tensor.matmul(psum[q % 2][0:2, 0, :], silu_c[:, kt * 2:kt * 2 + 2],
                                                        first_mod_w[q % 3][:, kt * 512:(kt + 1) * 512],
                                                        start=(kt == 0), stop=(kt == KT - 1))
                            last.then_inc(first_mod_used, 1)
                        if q:
                            pe.wait_ge(first_mod_row, i * 6 + q)
                            for k in range(4):
                                last = nc.tensor.matmul(psC[:, 1, bass.ds(i * 48 + ((q - 1) * 4 + k) * 2, 2)],
                                                        first_mod_rows[:, (q - 1) % 2, k * P:(k + 1) * P],
                                                        ident[0:2, 0:2], start=True, stop=True)
                            last.then_inc(first_mod_turned, 1)

            def mod_turn(mod, i):
                n = MCHUNKS * (mod[0] - 1) + mod[1]
                pe.wait_ge(mod_mac, i + (n + 1))
                pe.wait_ge(mod_summed, i + (n + 1))
                for k in range(4):
                    last = nc.tensor.transpose(psC[:, 0, k * P:(k + 1) * P], mod_acc[:, k * P:(k + 1) * P], ident)
                last.then_inc(mod_turned, 1)

            for att, pv, out, prep in (MLA, DIF, GQA):
                att[0].open(pe)
                prep[0].open(pe)
                pv.open(pe)
            DIF_SSO.open(pe)
            LRU_PE.open(pe)

            def norm(n):
                if n == 0:
                    pe.wait_ge(mod_ready, 1)
                pe.wait_ge(square_done, (n + 1) * KT)
                sum_rows(psC, ones, [square_sum if n else square_sum0], TH).then_inc(sums_done, 1)

            x_tiles = [KT]

            def project(name, kts, last_source, mod=None):
                base = x_tiles[0]
                with pe.Fori(0, KT // 2) as i:
                    for j in range(2):
                        slot = take_panel(pe, name, i, j)
                        pe.wait_ge(x_done, i * 2 + (base + j - 1))
                        products(pe, psum[j], slot, kts, P, 0, act_hi, act_lo, 0, T, TH,
                                 before_last=last_source if j == 0 else None).then_inc(gemm_done, 1)
                    if mod:
                        mod_turn(mod, i)
                x_tiles[0] += KT

            pes, acts, dves = PRE
            pe.wait_ge(const_in, 16)
            pe.wait_ge(x_in, 32)
            for kt in range(KT):
                if kt >= 2:
                    pe.wait_ge(x_done, kt - 1)
                d = psum[kt % 2]
                for t in range(QT):
                    last = nc.tensor.transpose(d[:, t // 4, (t % 4) * P:(t % 4 + 1) * P],
                                               x_tok[:, t * D + kt * P:t * D + (kt + 1) * P], ident)
                pes.mark(last, f"x{kt}")
            pe.wait_ge(const_in, 16 * 22)
            for k in range(2):
                last = nc.tensor.transpose(psC[:, 0, k * P:(k + 1) * P], vec_rows[k], ident)
            pes.mark(last, "vecs")
            nc.tensor.transpose(psD[:, 0, 0:P], vec_rows[2], ident)
            pes.mark(nc.tensor.transpose(psD[:, 0, P:2 * P], vec_rows[3], ident), "bmod")
            dves.wait(pe, "lamdiff")
            pes.mark(nc.tensor.matmul(psC[:, 1, 0:1], ones[0:1, :], lam_tmp[0:1, 4:5], start=True, stop=True), "lam")
            acts.wait(pe, "silu")
            dves.wait(pe, "bmod")
            dves.wait(pe, "lamall")
            pe.wait_ge(x_done, KT)
            first_modulation()

            for layer in range(DEPTH):
                norm(2 * layer)

                def h_tile(out, name, i, j, fresh=None):
                    slot = take_panel(pe, name, i, j)
                    return products(pe, out, slot, KT, P, 0, h_hi, h_lo, 0, T, TH, fresh=fresh)

                if layer == 0:
                    S = MIN
                    pes, acts, dves = S
                    for t in range(6):
                        if t >= 2:
                            acts.wait(pe, f"m{t - 2}")
                        h_tile(psum[t % 2], "mla_in", t // 2, t % 2, 0 if t == 0 else None).then_inc(gemm_done, 1)
                    acts.wait(pe, "m2")
                    pes.mark(sum_rows(psC, ones, mla_sq[0:3], TH), "sscq")
                    acts.wait(pe, "m4")
                    pes.mark(sum_rows(psD, ones, mla_sq[3:5], TH), "ssckv")
                    acts.wait(pe, "m5")
                    pes.mark(sum_rows(psA, blocks, mla_sq[5:6], TH), "sskr")
                    dves.wait(pe, "kr")
                    pes.mark(nc.tensor.matmul(psB[:, 0, 0:NLAT], rot64, kr_t[:, NCTX:T], start=True, stop=True), "rotkr")
                    pe.wait_ge(const_in, 16 * 24)
                    nc.tensor.transpose(psC[:, 0, 0:P], mla_cache[:, 0:P], ident)
                    nc.tensor.transpose(psC[:, 0, P:2 * P], mla_cache[:, P:2 * P], ident)
                    nc.tensor.transpose(psC[:, 0, 2 * P:3 * P], kr_cache, ident)
                    nc.tensor.transpose(psD[:, 0, 0:P], mla_raw[3][:, 0:P], ident)
                    nc.tensor.transpose(psD[:, 0, P:2 * P], mla_raw[4][:, 0:P], ident)
                    pes.mark(nc.tensor.transpose(psD[:, 0, 2 * P:3 * P], kr_t[:, 0:P], ident), "turned")
                    dves.wait(pe, "cache")
                    acts.wait(pe, "outs")
                    A, pv, out, (pes, acts, dves) = MLA

                    def uq(h, c0):
                        return products(pe, psD, 0, 3, 192, c0, h_hi, h_lo, CQ_AT, T, TH)

                    def ukv(h, c0):
                        return products(pe, psD, 1, 2, 256, c0, h_hi, h_lo, CKV_AT, NKEY, NKEY // 2)

                    def gqn(h):
                        acts.wait(pe, "v", h.last())
                        pe.wait_ge(split_done, phases["mla"].of_head(h, 0, 2))
                        pes.mark(uq(h, 0), "gqn")

                    def gqr(h):
                        acts.wait(pe, "evqn", h)
                        uq(h, 64).then_inc(gemm_done, 1)

                    def gkn(h):
                        pe.wait_ge(split_done, phases["mla"].of_head(h, 1, 2))
                        acts.wait(pe, "evqr", h)
                        pes.mark(ukv(h, 0), "gkn")

                    def ssqn(h):
                        acts.wait(pe, "evkn", h)
                        pes.mark(sum_rows(psD, ones, [sq_n], TH), "ssqn")

                    def ssqr(h):
                        acts.wait(pe, "rsqn", h)
                        pes.mark(sum_rows(psD, blocks, [sq_r], TH), "ssqr")

                    def sskn(h):
                        acts.wait(pe, "rsqr", h)
                        pes.mark(sum_rows(psD, ones, [sq_k], NKEY // 2), "sskn")

                    def gv(h):
                        acts.wait(pe, "rskn", h)
                        ukv(h, P).then_inc(gemm_done, 1)

                    def rotqr(h):
                        acts.wait(pe, "evv", h)
                        dves.wait(pe, "qr", h)
                        pes.mark(nc.tensor.matmul(psD[:, 0, 0:NLAT], rot64, qr_t[h.k % 2][:, NCTX:T],
                                                  start=True, stop=True), "rotqr")

                    def turned_v(h):
                        dves.wait(pe, "qroped", h)
                        for k in range(6):
                            last = nc.tensor.transpose(psD[:, k // 4, (k % 4) * P:(k % 4 + 1) * P],
                                                       vt_t[:, k * P:(k + 1) * P], ident)
                        pes.mark(last, "turned_v")

                    def pairs(h):
                        k = h.k % 2
                        return [[(qn_t[k], kn_t[k]), (qr_t[k][64:P], kr_t[64:P])]]

                    def first_scores(h):
                        for t in range(2):
                            pe_scores(pe, A, h, t, pairs(h))

                    def head(h, more):
                        n = h.next()
                        prep = (lambda step: step(n)) if more else (lambda step: None)
                        free = (out, "o")
                        prep(gqn)
                        pe_turned(pe, A, free, h, 0, m_probs)
                        prep(gqr)
                        pe_scores(pe, A, h, 2, pairs(h))
                        prep(gkn)
                        pe_turned(pe, A, free, h, 1, m_probs)
                        prep(ssqn)
                        pe_scores(pe, A, h, 3, pairs(h))
                        prep(ssqr)
                        pe_turned(pe, A, free, h, 2, m_probs)
                        prep(sskn)
                        pe_scores(pe, A, h, 4, pairs(h))
                        pe_turned(pe, A, free, h, 3, m_probs)
                        prep(gv)
                        pe_turned(pe, A, free, h, 4, m_probs)
                        prep(rotqr)
                        acts.wait(pe, "v", h)
                        pe_output(pe, A, pv, h, mV[h.k % 2], m_PT, m_PTp)
                        prep(turned_v)
                        prep(first_scores)

                    for step in (gqn, gqr, gkn, ssqn, ssqr, sskn, gv, rotqr, turned_v, first_scores):
                        step(Head(0, 0))
                    with pe.Fori(0, HEADS // 2 - 1) as i:
                        for k in range(2):
                            head(Head(i, k), True)
                    for k in range(2):
                        head(Head(HEADS // 2 - 1, k), k == 0)
                elif layer == 1:
                    A, pv, out, (pes, acts, dves) = DIF

                    def project_head(h, j):
                        pe.wait_ge(split_done, phases["diff"].of_head(h, j, 3))
                        products(pe, psD, (2, 0, 1)[j], KT, P, 0, h_hi, h_lo, 0, T, TH,
                                 fresh=2 if isinstance(h.i, int) and (h.i, h.k, j) == (0, 0, 0) else None
                                 ).then_inc(gemm_done, 1)

                    def gq(h):
                        acts.wait(pe, "v", h.last())
                        project_head(h, 0)

                    def gk(h):
                        acts.wait(pe, "evq", h)
                        project_head(h, 1)

                    def ssq(h):
                        acts.wait(pe, "evk", h)
                        pes.mark(sum_rows(psD, blocks, [dsq_q], TH), "ssq")

                    def ssk(h):
                        acts.wait(pe, "rsq", h)
                        pes.mark(sum_rows(psD, blocks, [dsq_k], TH), "ssk")

                    def rotq(h):
                        acts.wait(pe, "rsk", h)
                        dves.wait(pe, "q", h)
                        pes.mark(nc.tensor.matmul(psD[:, 0, 0:NLAT], rot64, dq_t[h.k % 2][:, NCTX:T],
                                                  start=True, stop=True), "rotq")

                    def gv(h):
                        dves.wait(pe, "qroped", h)
                        project_head(h, 2)

                    def rotk(h):
                        acts.wait(pe, "evv", h)
                        dves.wait(pe, "k", h)
                        nc.tensor.matmul(psD[:, 0, 0:NLAT], rot64, dk_t[h.k % 2][:, NCTX:T], start=True, stop=True)
                        pes.mark(nc.tensor.transpose(psD[:, 1, 0:P], dk_t[h.k % 2][:, 0:P], ident), "rotk")

                    def turned_v(h):
                        pe.wait_ge(cache_in, h.at(32, 32))
                        acts.wait(pe, "kout", h)
                        dves.wait(pe, "kroped", h)
                        for k in range(1, 5):
                            nc.tensor.transpose(psD[:, 0, (k - 1) * P:k * P], dvt[:, k * P:(k + 1) * P], ident)
                        nc.tensor.transpose(psD[:, 1, 0:P], dvt[:, 0:P], ident)
                        pes.mark(nc.tensor.transpose(psD[:, 1, P:2 * P], d_cache, ident), "turned_v")

                    def pairs(h):
                        q, k = dq_t[h.k % 2], dk_t[h.k % 2]
                        return [[(q[0:64], k[0:64])], [(q[64:P], k[64:P])]]

                    def first_scores(h):
                        acts.wait(pe, "v", h)
                        for t in range(2):
                            pe_scores(pe, A, h, t, pairs(h))

                    def head(h, more):
                        n = h.next()
                        prep = (lambda step: step(n)) if more else (lambda step: None)
                        free = (DIF_NORM, "rso")
                        prep(gq)
                        pe_turned(pe, A, free, h, 0, d_probs)
                        pe_scores(pe, A, h, 2, pairs(h))
                        prep(gk)
                        pe_turned(pe, A, free, h, 1, d_probs)
                        prep(ssq)
                        pe_scores(pe, A, h, 3, pairs(h))
                        prep(ssk)
                        pe_turned(pe, A, free, h, 2, d_probs)
                        prep(rotq)
                        pe_scores(pe, A, h, 4, pairs(h))
                        prep(gv)
                        pe_turned(pe, A, free, h, 3, d_probs)
                        prep(rotk)
                        pe_turned(pe, A, free, h, 4, d_probs)
                        pe_output(pe, A, pv, h, dV[h.k % 2], d_PT, d_PTp)
                        prep(turned_v)
                        prep(first_scores)
                        DIF_NORM.wait(pe, "evo", h)
                        DIF_SSO.mark(sum_rows(psC, ones, [do_sq], TH), "sso")

                    for step in (gq, gk, ssq, ssk, rotq, gv, rotk, turned_v, first_scores):
                        step(Head(0, 0))
                    with pe.Fori(0, HEADS // 2 - 1) as i:
                        for k in range(2):
                            head(Head(i, k), True)
                    for k in range(2):
                        head(Head(HEADS // 2 - 1, k), k == 0)
                elif layer == 2:
                    S = GKV
                    pes, acts, dves = S
                    for j in range(2):
                        h_tile(psA, "gqa_kv", j, 0, 4 if j == 0 else None).then_inc(gemm_done, 1)
                        h_tile(psB, "gqa_kv", j, 1).then_inc(gemm_done, 1)
                        acts.wait(pe, "evk", j)
                        pes.mark(sum_rows(psC, ones, [gsq], TH), "ssk")
                        dves.wait(pe, "k", j)
                        pes.mark(nc.tensor.matmul(psC[:, 0, 0:NLAT], rot128, gk_t[j][:, NCTX:T], start=True, stop=True),
                                 "rotk")
                        acts.wait(pe, "evv", j)
                        pe.wait_ge(gcache_in, 16 * 4)
                        for k in range(1, 5):
                            nc.tensor.transpose(psD[:, 0, (k - 1) * P:k * P], gvt[:, k * P:(k + 1) * P], ident)
                        nc.tensor.transpose(psD[:, 1, 0:P], gvt[:, 0:P], ident)
                        nc.tensor.transpose(psD[:, 1, P:2 * P], g_cache[j], ident)
                        pes.mark(nc.tensor.transpose(psD[:, 1, 2 * P:3 * P], gk_t[j][:, 0:P], ident), "turned_v")
                        dves.wait(pe, "kroped", j)
                        acts.wait(pe, "v", j)
                    A, pv, out, (pes, acts, dves) = GQA

                    def q_products(h, part):
                        if part[0] == 0:
                            pe.wait_ge(split_done, phases["gqa"].of_head(h))
                        last = products(pe, psD, h.k % 2, KT, P, 0, h_hi, h_lo, 0, T, TH, part)
                        if part[-1] == KT - 1:
                            last.then_inc(gemm_done, 1)

                    def q_sum(h):
                        acts.wait(pe, "evq", h)
                        pes.mark(sum_rows(psD, ones, [gsq], TH), "ssq")

                    def q_turn(h):
                        dves.wait(pe, "q", h)
                        pes.mark(nc.tensor.matmul(psD[:, 0, 0:NLAT], rot128, gq_t[h.k % 2][:, NCTX:T],
                                                  start=True, stop=True), "rotq")

                    def first_scores(h):
                        dves.wait(pe, "qroped", h)
                        for t in range(2):
                            pe_scores(pe, A, h, t, [[(gq_t[h.k % 2], gk_t[h.k % 2])]])

                    def head(h, more):
                        n = h.next()
                        pairs = [[(gq_t[h.k % 2], gk_t[h.k % 2])]]
                        if more:
                            q_products(n, range(0, 4))
                        pe_turned(pe, A, (out, "o"), h, 0, g_probs)
                        pe_scores(pe, A, h, 2, pairs)
                        if more:
                            q_products(n, range(4, KT))
                        pe_turned(pe, A, (out, "o"), h, 1, g_probs)
                        pe_scores(pe, A, h, 3, pairs)
                        pe_turned(pe, A, (out, "o"), h, 2, g_probs)
                        if more:
                            q_sum(n)
                        pe_scores(pe, A, h, 4, pairs)
                        pe_turned(pe, A, (out, "o"), h, 3, g_probs)
                        if more:
                            q_turn(n)
                        pe_turned(pe, A, (out, "o"), h, 4, g_probs)
                        pe_output(pe, A, pv, h, gV[h.k % 2], g_PT, g_PTp)
                        if more:
                            first_scores(n)

                    h0 = Head(0, 0)
                    q_products(h0, range(KT))
                    q_sum(h0)
                    q_turn(h0)
                    first_scores(h0)
                    with pe.Fori(0, HEADS // 2 - 1) as i:
                        for k in range(2):
                            head(Head(i, k), True)
                    for k in range(2):
                        head(Head(HEADS // 2 - 1, k), k == 0)
                else:

                    def block_products(i, fresh):
                        LRU_ACT.wait(pe, "trb", i - 1)
                        h_tile(psA, "lru", i, 0, fresh).then_inc(gemm_done, 1)
                        LRU_ACT.wait(pe, "t", i - 1)
                        h_tile(psB, "lru", i, 1).then_inc(gemm_done, 1)
                        slot = take_panel(pe, "lru", i, 2)
                        LRU_Y.wait(pe, "y", i)
                        for g, ps, name in ((2, psA, "rb"), (0, psC, "rf"), (1, psD, "if"), (3, psB, None)):
                            if g == 3:
                                LRU_ACT.wait(pe, "gelu", i)
                            for p_, (w, r) in enumerate(((w_hi, y_hi), (w_hi, y_lo), (w_lo, y_hi))):
                                for b in range(2):
                                    last = nc.tensor.matmul(ps[:, b, 0:LW // 2], w[slot][:, g * P:(g + 1) * P],
                                                            r[:, b * (LW // 2):(b + 1) * (LW // 2)],
                                                            start=(p_ == 0), stop=(p_ == 2))
                            if name:
                                LRU_PE.mark(last, name)
                            else:
                                last.then_inc(gemm_done, 1)

                    block_products(0, 6)
                    with pe.Fori(1, KT) as i:
                        block_products(i, None)
                mixed = LRU_DVE if layer == 3 else out
                if layer == 3:
                    LRU_ACT.wait(pe, "t", KT - 1)
                    LRU_DVE.wait(pe, "o", KT - 2)
                project(f"wo{layer}", KT, lambda: mixed.wait_turns(pe, KT))

                norm(2 * layer + 1)
                for ch, size in enumerate(FFN_CHUNKS):
                    base = layer * (FFN // P) + sum(FFN_CHUNKS[:ch])

                    def hidden_tile(i, fresh):
                        pe.wait_ge(x_done, x_tiles[0] - 1)
                        pe.wait_ge(silu_done, i + (base + 1))
                        h_tile(psA, f"in{layer}.{ch}", i, 0, fresh).then_inc(gemm_done, 1)
                        pe.wait_ge(hidden_done, i + (base + 1))
                        pe.wait_ge(x_done, x_tiles[0])
                        h_tile(psB, f"in{layer}.{ch}", i, 1).then_inc(gemm_done, 1)
                        if mod_at(layer, ch, False):
                            mod_turn(mod_at(layer, ch, False), i)

                    if ch == 0:
                        hidden_tile(0, 2 * layer + 1)
                    with pe.Fori(1 if ch == 0 else 0, size) as i:
                        hidden_tile(i, None)
                    pe.wait_ge(silu_done, base + size + 1)
                    project(f"out{layer}.{ch}", size, lambda: pe.wait_ge(hidden_done, base + size + 1),
                            mod_at(layer, ch, True))

            pe.wait_ge(x_done, x_tiles[0])
            for t in range(QT):
                if t >= 2:
                    pe.wait_ge(y_copied, t - 1)
                d = psum[t % 2]
                for kt in range(KT):
                    last = nc.tensor.transpose(d[:, kt // 4, (kt % 4) * P:(kt % 4 + 1) * P],
                                               x[:, kt * T + t * P:kt * T + (t + 1) * P], ident)
                last.then_inc(y_turned, 1)

        @block.scalar
        def _(act):
            pes, acts, dves = PRE
            act.dma_start(x_tok[:, 0:D], a["x_prompt"][0]).then_inc(x_in, 16)
            act.dma_start(x_tok[:, D:QT * D].rearrange("p (t n) -> p t n", t=4),
                          a["x_sample"][0].rearrange("(t p) n -> p t n", p=P)).then_inc(x_in, 16)
            act.wait_ge(const_in, 16)
            dves.wait(act, "ready")
            act.dma_start(lam_row[0:1, :], a["diff_lambda"].rearrange("l a d -> l (a d)")).then_inc(const_in, 16)
            for name, src in (("bgate", a["lru_b_gate"].rearrange("l d g (k n) -> (l d g k) n", n=P)),
                              ("lam", a["lru_lambda"].rearrange("l d (k n) -> (l d k) n", n=P)),
                              ("h0", a["state_lru_h"].rearrange("b l d (k n) -> (b l d k) n", n=P)),
                              ("convb", a["lru_conv_b"].rearrange("l (k n) -> (l k) n", n=P)),
                              ("convw", a["lru_conv_w"].rearrange("l w (k n) -> (l w k) n", n=P))):
                r = VEC[name]
                act.dma_start(vec_rows[r // P][r % P:r % P + src.shape[0], :], src).then_inc(const_in, 16)
            bm = a["b_mod"].rearrange("l (k n) -> (l k) n", n=P)
            act.dma_start(vec_rows[2][0:P, :], bm[0:P, :]).then_inc(const_in, 16)
            act.dma_start(vec_rows[3][0:64, :], bm[P:192, :]).then_inc(const_in, 16)
            act.dma_start(tables[:, :], a["tables"]).then_inc(tables_in, 16)
            for kt in range(KT):
                pes.wait(act, f"x{kt}")
                nc.scalar.activation(x[:, kt * T:kt * T + 4 * P], psum[kt % 2][:, 0, :], ACT.Copy)
                nc.scalar.activation(x[:, kt * T + 4 * P:(kt + 1) * T], psum[kt % 2][:, 1, 0:P],
                                     ACT.Copy).then_inc(x_done, 1)
            for att, pv, out, prep in (MLA, DIF, GQA):
                att[1].open(act)
                prep[1].open(act)
            DIF_NORM.open(act)
            LRU_XP.open(act)
            LRU_ACT.open(act)
            act.sem_inc(first_mod_turned, 2)
            pes.wait(act, "vecs")
            act.sem_inc(silu_done, 1)
            acts.mark(nc.scalar.activation(vecs[:, :], psC[:, 0, 0:2 * P], ACT.Copy), "vecs")
            act.drain()
            sc = silu_c[:, :].rearrange("p (k c) -> p k c", c=2)
            nc.scalar.activation(sc[:, :, 0], vecs[:, VEC["cctx"]:VEC["cctx"] + KT], ACT.Silu)
            acts.mark(nc.scalar.activation(sc[:, :, 1], vecs[:, VEC["c"]:VEC["c"] + KT], ACT.Silu), "silu")
            dves.wait(act, "lamsum")
            acts.mark(nc.scalar.activation(lam_tmp[0:1, 2:4], lam_tmp[0:1, 0:2], ACT.Exp), "lamexp")
            nc.scalar.activation(lru_small[:, 64:80],
                                 vecs[:, VEC["lam"]:VEC["lam"] + 16], ACT.Abs)
            act.drain()
            acts.mark(nc.scalar.activation(lru_small[:, 80:96], lru_small[:, 64:80], ACT.Exp, scale=-1.0), "sp")

            with act.Fori(0, 6) as i:
                for b in range(2):
                    act.wait_ge(first_mod_used, i * 2 + (b + 1))
                    act.wait_ge(first_mod_turned, i * 2 + (b + 1))
                    nc.scalar.activation(first_mod_rows[:, b, :], psum[b][0:2, 0, :],
                                         ACT.Copy).then_inc(first_mod_row, 1)

            x_tiles = [KT]
            outs = [0]

            def norm(n):
                layer, which = n // 2, n % 2
                nc.scalar.preload_act_table_set("natural_log_exp_and_others")
                act.wait_ge(sums_done, n + 1)
                rstd(act, rms, psC, D, TH).then_inc(rstd_done, 1)
                for kt in range(KT):
                    act.wait_ge(scaled_done, n * KT + kt + 1)
                    for cond, (t0, t1) in enumerate(((0, NCTX), (NCTX, T))):
                        s_ = scaled[:, kt * T + t0:kt * T + t1]
                        nc.scalar.activation(s_, s_, ACT.Identity, bias=mod_col(layer, 3 * which, kt, cond),
                                             scale=gains[:, cond * KT + kt:cond * KT + kt + 1])
                    act.drain()
                    nc.scalar.activation(h_hi[:, kt * T:(kt + 1) * T], scaled[:, kt * T:(kt + 1) * T],
                                         ACT.Copy).then_inc(h_hi_done, 1)
                act.wait_ge(h_done, (n + 1) * KT)

            def exp_and_ln():
                nc.scalar.preload_act_table_set("natural_log_exp_and_others")

            def g_panel(name, i, j):
                act.wait_ge(gemm_done, phases[name].number(i, j))

            for layer in range(DEPTH):
                norm(2 * layer)
                if layer < 3:
                    exp_and_ln()
                if layer == 0:
                    S = MIN
                    pes, acts, dves = S
                    act.dma_start(mla_cache, a["cache_mla_ckv"][0, 0]).then_inc(const_in, 16)
                    dves_pre = PRE[2]
                    act.wait_ge(kr_cleared, 1)
                    act.dma_start(kr_cache[:, 64:P], a["cache_mla_krope"][0, 0]).then_inc(const_in, 16)
                    for t in range(6):
                        g_panel("mla_in", t // 2, t % 2)
                        acts.mark(evacuate(mla_raw[t], mla_sq[t], psum[t % 2], TH), f"m{t}")
                    pes.wait(act, "sscq")
                    acts.mark(rstd(act, mla_rs[0], psC, MLA_QR, TH), "rscq")
                    pes.wait(act, "ssckv")
                    acts.mark(rstd(act, mla_rs[1], psD, MLA_KVR, TH), "rsckv")
                    pes.wait(act, "sskr")
                    acts.mark(rstd(act, mla_rs[2], psA, 64, TH), "rskr")
                    pes.wait(act, "turned")
                    acts.mark(nc.scalar.activation(mla_out, psD[:, 0, 0:3 * P], ACT.Copy), "outs")
                    act.wait_ge(acts.sem, len(acts.names))
                    act.dma_start(a["new_mla_ckv"][0, 0], mla_out[:, 0:2 * P]).then_inc(outs_done, 16)
                    act.dma_start(a["new_mla_krope"][0, 0], mla_out[:, 2 * P + 64:3 * P]).then_inc(outs_done, 16)
                    outs[0] = 32
                    A, pv, out, (pes, acts, dves) = MLA
                    act.wait_ge(MIN[2].sem, len(MIN[2].names))
                    act.wait_ge(outs_done, 32)
                    scale = 192 ** -0.5

                    def evqn(h):
                        pes.wait(act, "gqn", h)
                        acts.mark(evacuate(qn_t[h.k % 2], sq_n, psD, TH), "evqn")

                    def evqr(h):
                        act.wait_ge(gemm_done, phases["mla"].of_head(h, 0, 2))
                        acts.mark(evacuate(qr_t[h.k % 2], sq_r, psD, TH), "evqr")

                    def evkn(h):
                        pes.wait(act, "gkn", h)
                        acts.mark(evacuate(kn_t[h.k % 2], sq_k, psD, NKEY // 2), "evkn")

                    def rsqn(h):
                        pes.wait(act, "ssqn", h)
                        acts.mark(rstd(act, sq_n, psD, P, TH), "rsqn")

                    def rsqr(h):
                        pes.wait(act, "ssqr", h)
                        acts.mark(rstd(act, sq_r, psD, 64, TH), "rsqr")

                    def rskn(h):
                        pes.wait(act, "sskn", h)
                        acts.mark(rstd(act, sq_k, psD, P, NKEY // 2), "rskn")

                    def evv(h):
                        act.wait_ge(gemm_done, phases["mla"].of_head(h, 1, 2))
                        dves.wait(act, "kn", h)
                        acts.mark(nc.scalar.activation(halves(vt_t, NKEY // 2), psD[:, :, 0:NKEY // 2], ACT.Copy),
                                  "evv")

                    def values(h):
                        pes.wait(act, "turned_v", h)
                        nc.scalar.activation(mV[h.k % 2][:, 0:4 * P], psD[:, 0, :], ACT.Copy)
                        acts.mark(nc.scalar.activation(mV[h.k % 2][:, 4 * P:6 * P], psD[:, 1, 0:2 * P], ACT.Copy), "v")

                    def head(h, more):
                        n = h.next()
                        prep = (lambda step: step(n)) if more else (lambda step: None)
                        for t in range(2):
                            act_exp(act, A, h, t, 1, scale, m_probs, m_stats)
                        prep(evqn)
                        act_pt(act, A, h, 0, m_PT, m_PTp)
                        prep(evqr)
                        act_exp(act, A, h, 2, 1, scale, m_probs, m_stats)
                        prep(evkn)
                        act_pt(act, A, h, 1, m_PT, m_PTp)
                        prep(rsqn)
                        act_exp(act, A, h, 3, 1, scale, m_probs, m_stats)
                        prep(rsqr)
                        act_pt(act, A, h, 2, m_PT, m_PTp)
                        prep(rskn)
                        act_exp(act, A, h, 4, 1, scale, m_probs, m_stats)
                        act_pt(act, A, h, 3, m_PT, m_PTp)
                        prep(evv)
                        act_pt(act, A, h, 4, m_PT, m_PTp)
                        prep(values)

                    for step in (evqn, evqr, evkn, rsqn, rsqr, rskn, evv, values):
                        step(Head(0, 0))
                    with act.Fori(0, HEADS // 2 - 1) as i:
                        for k in range(2):
                            head(Head(i, k), True)
                    for k in range(2):
                        head(Head(HEADS // 2 - 1, k), k == 0)
                elif layer == 1:
                    A, pv, out, (pes, acts, dves) = DIF
                    kc = a["cache_diff_k"][0, 0].rearrange("t h c d -> t (h c d)")
                    vc = a["cache_diff_v"][0, 0].rearrange("t h d -> t (h d)")
                    ko = a["new_diff_k"][0, 0].rearrange("t h c d -> t (h c d)")
                    vo = a["new_diff_v"][0, 0].rearrange("t h d -> t (h d)")
                    scale = 64 ** -0.5

                    def cached(h):
                        act.dma_start(d_cache, kc[:, bass.ds(h.at(P, 0), P)]).then_inc(cache_in, 16)
                        act.dma_start(dV[h.k % 2][:, 5 * P:6 * P], vc[:, bass.ds(h.at(P, 0), P)]).then_inc(cache_in, 16)

                    def evq(h):
                        act.wait_ge(gemm_done, phases["diff"].of_head(h, 0, 3))
                        acts.mark(evacuate(dq_t[h.k % 2], dsq_q, psD, TH), "evq")

                    def evk(h):
                        act.wait_ge(gemm_done, phases["diff"].of_head(h, 1, 3))
                        acts.mark(evacuate(dk_t[h.k % 2][:, 0:T], dsq_k, psD, TH), "evk")

                    def rsq(h):
                        pes.wait(act, "ssq", h)
                        acts.mark(rstd(act, dsq_q, psD, 64, TH), "rsq")

                    def rsk(h):
                        pes.wait(act, "ssk", h)
                        acts.mark(rstd(act, dsq_k, psD, 64, TH), "rsk")

                    def evv(h):
                        act.wait_ge(gemm_done, phases["diff"].of_head(h, 2, 3))
                        dves.wait(act, "k", h)
                        acts.mark(nc.scalar.activation(halves(dvt, TH), psD[:, :, 0:TH], ACT.Copy), "evv")

                    def kout(h):
                        act.wait_ge(outs_done, h.at(32, 32))
                        pes.wait(act, "rotk", h)
                        acts.mark(nc.scalar.activation(d_kout, psD[:, 1, 0:P], ACT.Copy), "kout")

                    def values(h):
                        pes.wait(act, "turned_v", h)
                        V = dV[h.k % 2]
                        nc.scalar.activation(V[:, P:5 * P], psD[:, 0, :], ACT.Copy)
                        nc.scalar.activation(V[:, 0:P], psD[:, 1, 0:P], ACT.Copy)
                        acts.mark(nc.scalar.activation(dk_t[h.k % 2][:, T:NKEY], psD[:, 1, P:2 * P], ACT.Copy), "v")
                        acts.wait(act, "v", h)
                        act.dma_start(ko[:, bass.ds(h.at(P, 0), P)], d_kout).then_inc(outs_done, 16)
                        act.dma_start(vo[:, bass.ds(h.at(P, 0), P)], V[:, 0:P]).then_inc(outs_done, 16)

                    def output(h):
                        out.wait(act, "o", h.last())
                        pv.wait(act, "pv", h)
                        nc.scalar.activation(do_t[:, NCTX:T], psC[:, 0, 0:NLAT], ACT.Copy)
                        nc.scalar.activation(do_t[:, 0:NCTX], psC[:, 1, 0:P], ACT.Copy)
                        nc.scalar.activation(do_sq[:, NCTX:T], psC[:, 0, 0:NLAT], ACT.Square)
                        DIF_NORM.mark(nc.scalar.activation(do_sq[:, 0:NCTX], psC[:, 1, 0:P], ACT.Square), "evo")

                    def first_exp(h):
                        act_exp(act, A, h, 0, 2, scale, d_probs, d_stats)

                    def head(h, more):
                        n = h.next()
                        prep = (lambda step: step(n)) if more else (lambda step: None)
                        prep(cached)
                        act_exp(act, A, h, 1, 2, scale, d_probs, d_stats)
                        prep(evq)
                        act_pt(act, A, h, 0, d_PT, d_PTp)
                        act_exp(act, A, h, 2, 2, scale, d_probs, d_stats)
                        prep(evk)
                        act_pt(act, A, h, 1, d_PT, d_PTp)
                        prep(rsq)
                        act_exp(act, A, h, 3, 2, scale, d_probs, d_stats)
                        prep(rsk)
                        act_pt(act, A, h, 2, d_PT, d_PTp)
                        act_exp(act, A, h, 4, 2, scale, d_probs, d_stats)
                        prep(evv)
                        act_pt(act, A, h, 3, d_PT, d_PTp)
                        prep(kout)
                        act_pt(act, A, h, 4, d_PT, d_PTp)
                        output(h)
                        prep(values)
                        prep(first_exp)
                        DIF_SSO.wait(act, "sso", h)
                        DIF_NORM.mark(rstd(act, do_sq, psC, P, TH), "rso")

                    for step in (cached, evq, evk, rsq, rsk, evv, kout, values, first_exp):
                        step(Head(0, 0))
                    with act.Fori(0, HEADS // 2 - 1) as i:
                        for k in range(2):
                            head(Head(i, k), True)
                    for k in range(2):
                        head(Head(HEADS // 2 - 1, k), k == 0)
                    outs[0] += 32 * HEADS
                elif layer == 2:
                    S = GKV
                    pes, acts, dves = S
                    kc = a["cache_gqa_k"][0, 0]
                    vc = a["cache_gqa_v"][0, 0]
                    act.wait_ge(outs_done, outs[0])
                    for j in range(2):
                        act.dma_start(g_cache[j], kc[:, j, :]).then_inc(gcache_in, 16)
                        act.dma_start(gV[j][:, 5 * P:6 * P], vc[:, j, :]).then_inc(gcache_in, 16)
                    for j in range(2):
                        g_panel("gqa_kv", j, 0)
                        acts.mark(evacuate(gk_t[j][:, 0:T], gsq, psA, TH), "evk")
                        g_panel("gqa_kv", j, 1)
                        acts.mark(nc.scalar.activation(halves(gvt, TH), psB[:, :, 0:TH], ACT.Copy), "evv")
                        pes.wait(act, "ssk", j)
                        acts.mark(rstd(act, gsq, psC, P, TH), "rsk")
                        pes.wait(act, "turned_v", j)
                        nc.scalar.activation(gV[j][:, P:5 * P], psD[:, 0, :], ACT.Copy)
                        nc.scalar.activation(gV[j][:, 0:P], psD[:, 1, 0:P], ACT.Copy)
                        nc.scalar.activation(gk_t[j][:, T:NKEY], psD[:, 1, P:2 * P], ACT.Copy)
                        acts.mark(nc.scalar.activation(g_kout[j], psD[:, 1, 2 * P:3 * P], ACT.Copy), "v")
                        acts.wait(act, "v", j)
                        act.dma_start(a["new_gqa_k"][0, 0][:, j, :], g_kout[j]).then_inc(outs_done, 16)
                        act.dma_start(a["new_gqa_v"][0, 0][:, j, :], gV[j][:, 0:P]).then_inc(outs_done, 16)
                        dves.wait(act, "k", j)
                    outs[0] += 64
                    A, pv, out, (pes, acts, dves) = GQA
                    scale = P ** -0.5

                    def q_taken(h):
                        act.wait_ge(gemm_done, phases["gqa"].of_head(h))
                        acts.mark(evacuate(gq_t[h.k % 2], gsq, psD, TH), "evq")

                    def q_rstd(h):
                        pes.wait(act, "ssq", h)
                        acts.mark(rstd(act, gsq, psD, P, TH), "rsq")

                    def head(h, more):
                        n = h.next()
                        act_exp(act, A, h, 0, 1, scale, g_probs, g_stats)
                        act_exp(act, A, h, 1, 1, scale, g_probs, g_stats)
                        act_pt(act, A, h, 0, g_PT, g_PTp)
                        act_exp(act, A, h, 2, 1, scale, g_probs, g_stats)
                        if more:
                            q_taken(n)
                        act_pt(act, A, h, 1, g_PT, g_PTp)
                        act_exp(act, A, h, 3, 1, scale, g_probs, g_stats)
                        act_pt(act, A, h, 2, g_PT, g_PTp)
                        if more:
                            q_rstd(n)
                        act_exp(act, A, h, 4, 1, scale, g_probs, g_stats)
                        act_pt(act, A, h, 3, g_PT, g_PTp)
                        act_pt(act, A, h, 4, g_PT, g_PTp)

                    q_taken(Head(0, 0))
                    q_rstd(Head(0, 0))
                    with act.Fori(0, HEADS // 2 - 1) as i:
                        for k in range(2):
                            head(Head(i, k), True)
                    for k in range(2):
                        head(Head(HEADS // 2 - 1, k), k == 0)
                else:
                    act.wait_ge(outs_done, outs[0])
                    act.wait_ge(lru_ready, 1)

                    def conv_input(panel_done):
                        act.wait_ge(gemm_done, panel_done)
                        nc.scalar.activation(l_xp[:, 1:1 + NCTX], psA[:, 0, 0:NCTX], ACT.Copy)
                        nc.scalar.activation(l_xp[:, LAT0 + 1:LAT0 + 1 + TH - NCTX], psA[:, 0, NCTX:TH], ACT.Copy)
                        LRU_XP.mark(nc.scalar.activation(l_xp[:, LAT0 + 1 + TH - NCTX:LAT0 + 1 + NLAT],
                                                         psA[:, 1, 0:TH], ACT.Copy), "xp")

                    def lru_block(i, more):
                        hw = LW // 2
                        nc.scalar.preload_act_table_set("gelu_apprx_tanh_and_others")
                        g_panel("lru", i, 1)
                        LRU_ACT.mark(nc.scalar.activation(halves(l_gelu[:, bass.ds(i * T, T)], TH), psB[:, :, 0:TH],
                                                          ACT.Gelu_apprx_tanh), "gelu")
                        LRU_DVE.wait(act, "u", i - 1)
                        for g, ps, dst, ready, read in ((2, psA, l_tr[1], "rb", "trb"), (0, psC, l_tr[0], "rf", None),
                                                        (1, psD, l_ti[0], "if", None), (3, psB, l_ti[1], None, "t")):
                            if ready == "if":
                                LRU_DVE.wait(act, "h", i - 1)
                            if ready:
                                LRU_PE.wait(act, ready, i)
                            else:
                                g_panel("lru", i, 2)
                            last = nc.scalar.activation(halves(dst, hw), ps[:, :, 0:hw], ACT.Tanh,
                                                        bias=hb[:, bass.ds(i + g * KT, 1)], scale=0.5)
                            if read:
                                LRU_ACT.mark(last, read)
                        act.drain()
                        LRU_DVE.wait(act, "g", i - 1)
                        for d in range(2):
                            s_ = sp4[:, bass.ds(i + d * KT, 1)]
                            nc.scalar.activation(l_th[d], l_tr[d], ACT.Tanh, bias=s_, scale=s_)
                        for d in range(2):
                            s_ = neg_sp4[:, bass.ds(i + d * KT, 1)]
                            nc.scalar.activation(l_a[d], l_tr[d], ACT.Exp, bias=s_, scale=s_)
                        act.drain()
                        for d in range(2):
                            last = nc.scalar.activation(l_tr[d], l_a[d], ACT.Square)
                        LRU_ACT.mark(last, "a2")
                        if more:
                            conv_input(phases["lru"].number(i + 1, 0))
                        LRU_DVE.wait(act, "m", i)
                        for d in range(2):
                            last = nc.scalar.activation(l_tr[d], l_th[d], ACT.Sqrt)
                        LRU_ACT.mark(last, "sq")

                    conv_input(phases["lru"].number(0, 0))
                    with act.Fori(0, KT - 1) as i:
                        lru_block(i, True)
                    lru_block(KT - 1, False)
                x_tiles[0] += KT
                norm(2 * layer + 1)
                if layer == 3:
                    with nc.allow_non_contiguous_dma(reason="1024 floats per direction"):
                        act.dma_start(a["new_lru_h"][0, 0].rearrange("d (k p) -> p d k", p=P),
                                      l_state.rearrange("p (d k) -> p d k", d=2)).then_inc(outs_done, 16)
                    outs[0] += 16
                for ch, size in enumerate(FFN_CHUNKS):
                    base = layer * (FFN // P) + sum(FFN_CHUNKS[:ch])
                    with act.Fori(0, size) as i:
                        g_panel(f"in{layer}.{ch}", i, 0)
                        act.wait_ge(hidden_done, i + (base + 1))
                        nc.scalar.activation(halves(gate_silu, TH), psA[:, :, 0:TH], ACT.Silu).then_inc(silu_done, 1)
                    x_tiles[0] += KT
            for t in range(QT):
                act.wait_ge(y_turned, t + 1)
                nc.scalar.activation(y_tok[:, t * D:(t + 1) * D].rearrange("p (b n) -> p b n", b=2),
                                     psum[t % 2][:, :, :], ACT.Copy).then_inc(y_copied, 1)
                act.wait_ge(y_copied, t + 1)
                dst = a["y_prompt"][0] if t == 0 else a["y_sample"][0, (t - 1) * P:t * P, :]
                act.dma_start(dst, y_tok[:, t * D:(t + 1) * D]).then_inc(y_out, 16)
            act.wait_ge(y_out, 16 * QT)
            act.wait_ge(outs_done, outs[0])

        @block.vector
        def _(dve):
            pes, acts, dves = PRE
            dve.sem_inc(mod_summed, 1)
            for att, pv, out, prep in (MLA, DIF, GQA):
                att[2].open(dve)
                prep[2].open(dve)
                out.open(dve)
            LRU_Y.open(dve)
            LRU_DVE.open(dve)
            dve.sem_inc(hidden_done, 1)
            for k in range(4):
                last = nc.vector.memset(vec_rows[k], 0.0)
            nc.vector.memset(eps, EPS)
            dve.drain()
            dves.mark(nc.vector.memset(lam_tmp[:, :], 0.0), "ready")
            dve.drain()

            def add_squares(x_, sq, total):
                nc.vector.tensor_tensor(sq, x_, x_, ALU.mult)
                dve.drain()
                nc.vector.tensor_tensor(total, total, sq, ALU.add).then_inc(square_done, 1)

            nc.vector.memset(square_sum0, 0.0)
            for kt in range(KT):
                dve.wait_ge(x_done, kt + 1)
                add_squares(x[:, kt * T:(kt + 1) * T], square0, square_sum0)
                dve.drain()
            dve.wait_ge(const_in, 16 * 22)
            lr = lam_row[0:1, :].rearrange("p (a b d) -> p a b d", a=2, b=2)
            nc.vector.tensor_tensor(lam_tmp[0:1, 4:132].rearrange("p (a d) -> p a d", a=2), lr[:, :, 0, :],
                                    lr[:, :, 1, :], ALU.mult)
            dve.drain()
            dves.mark(nc.vector.tensor_reduce(lam_tmp[0:1, 0:2],
                                              lam_tmp[0:1, 4:132].rearrange("p (a d) -> p a d", a=2),
                                              AX.X, ALU.add), "lamsum")
            acts.wait(dve, "lamexp")
            nc.vector.tensor_tensor(lam_tmp[0:1, 4:5], lam_tmp[0:1, 3:4], lam_tmp[0:1, 2:3], ALU.subtract)
            dve.drain()
            dves.mark(nc.vector.tensor_scalar(lam_tmp[0:1, 4:5], lam_tmp[0:1, 4:5], -LAMBDA_INIT, None, ALU.add),
                      "lamdiff")
            pes.wait(dve, "lam")
            dves.mark(nc.vector.tensor_copy(neg_lambda, psC[:, 1, 0:1]), "lamall")
            pes.wait(dve, "bmod")
            dves.mark(nc.vector.tensor_copy(bmod[:, :], psD[:, 0, 0:192]), "bmod")
            dve.wait_ge(tables_in, 16)
            nc.vector.tensor_copy(small[:, 44:45], eps).then_inc(scratch_free, 1)
            acts.wait(dve, "sp")
            ys, s_, s2, acc, tmp = (lru_small[:, 80 + 16 * k:96 + 16 * k] for k in range(5))
            nc.vector.tensor_scalar(tmp, ys, 2.0, None, ALU.add)
            dve.drain()
            nc.vector.reciprocal(tmp, tmp)
            dve.drain()
            nc.vector.tensor_tensor(s_, ys, tmp, ALU.mult)
            dve.drain()
            nc.vector.tensor_tensor(s2, s_, s_, ALU.mult)
            nc.vector.memset(acc, 1.0 / 17)
            dve.drain()
            for k in (15, 13, 11, 9, 7, 5, 3, 1):
                nc.vector.tensor_tensor(acc, acc, s2, ALU.mult)
                dve.drain()
                nc.vector.tensor_scalar(acc, acc, 1.0 / k, None, ALU.add)
                dve.drain()
            nc.vector.tensor_tensor(acc, acc, s_, ALU.mult)
            nc.vector.tensor_scalar(tmp, vecs[:, VEC["lam"]:VEC["lam"] + 16], -1.0, 0.0, ALU.mult, ALU.max)
            dve.drain()
            nc.vector.tensor_scalar(tmp, tmp, 4.0, None, ALU.mult)
            dve.drain()
            nc.vector.scalar_tensor_tensor(sp4, acc, 8.0, tmp, ALU.mult, ALU.add)
            dve.drain()
            nc.vector.tensor_scalar(neg_sp4, sp4, -1.0, None, ALU.mult)
            nc.vector.tensor_scalar(hb, vecs[:, VEC["bgate"]:VEC["bgate"] + 32], 0.5, None, ALU.mult)
            dves.mark(nc.vector.tensor_scalar(small[:, 43:44], vecs[:, VEC["dsub"]:VEC["dsub"] + 1],
                                              1.0 - LAMBDA_INIT, None, ALU.mult), "splog")
            dve.drain()

            def vec(name, k=0, n=1):
                return vecs[:, VEC[name] + k:VEC[name] + k + n]

            x_tiles = [KT]
            dve.wait_ge(first_mod_turned, 2 + 12)
            for cond in range(2):
                last = nc.vector.tensor_tensor(mods[0][:, :].rearrange("p (k c) -> p k c", c=2)[:, :, cond],
                                               psC[:, 1, 0:96].rearrange("p (k c) -> p k c", c=2)[:, :, cond],
                                               bmod[:, 0:48], ALU.add)
            last.then_inc(mod_ready, 1)
            dve.wait_ge(mod_ready, 1)

            def mod_products(mod, i, b):
                n = MCHUNKS // 2 * (mod[0] - 1) + mod[1] // 2
                dve.wait_ge(mod_in[b], i * 16 + 16 * (n + 1))
                for kt in range(KT):
                    for cond in range(2):
                        w_ = mod_w[b][:, kt * MCOLS:(kt + 1) * MCOLS].rearrange("p (h n) -> p h n", h=2)
                        c_ = silu_c[:, kt * 2 + cond:kt * 2 + cond + 1]
                        acc = mod_acc_[:, :, cond, :]
                        if kt == 0:
                            last = nc.vector.tensor_scalar(acc, w_, c_, None, ALU.mult)
                        else:
                            last = nc.vector.scalar_tensor_tensor(acc, w_, c_, acc, ALU.mult, ALU.add)
                    if kt < KT - 1:
                        dve.drain()
                last.then_inc(mod_mac, 1)

            def mod_sums(mod, i, b):
                n = MCHUNKS * (mod[0] - 1) + mod[1]
                dve.wait_ge(mod_turned, i * 2 + (n + b + 1))
                nc.vector.tensor_reduce(mods[mod[0] % 2][:, bass.ds(i * 8 + (mod[1] + b) * 4, 4)],
                                        psC[:, 0, :].rearrange("p (k n) -> p k n", k=4), AX.X,
                                        ALU.add).then_inc(mod_summed, 1)

            def mod_bias(layer):
                m = mods[layer % 2][:, :].rearrange("p (k c) -> p k c", c=2)
                dve.wait_ge(mod_summed, MCHUNKS * layer + 1)
                for cond in range(2):
                    nc.vector.tensor_tensor(m[:, :, cond], m[:, :, cond], bmod[:, layer * 48:layer * 48 + 48], ALU.add)
                dve.drain()

            def norm(n):
                layer, which = n // 2, n % 2
                if layer and which == 0:
                    mod_bias(layer)
                m = mods[layer % 2][:, :].rearrange("p (v k c) -> p v k c", v=6, c=2)
                for cond in range(2):
                    nc.vector.scalar_tensor_tensor(gains[:, cond * KT:(cond + 1) * KT], m[:, 3 * which + 1, :, cond],
                                                   1.0, vec("gn1" if which == 0 else "gn2", layer * KT, KT),
                                                   ALU.add, ALU.mult)
                dve.drain()
                dve.wait_ge(rstd_done, n + 1)
                lead = 2
                for kt in range(KT + lead):
                    if kt < KT:
                        nc.vector.tensor_tensor(scaled[:, kt * T:(kt + 1) * T], x[:, kt * T:(kt + 1) * T], rms,
                                                ALU.mult).then_inc(scaled_done, 1)
                    if kt >= lead:
                        o = (kt - lead) * T
                        dve.wait_ge(h_hi_done, n * KT + kt - lead + 1)
                        nc.vector.tensor_tensor(h_lo[:, o:o + T], scaled[:, o:o + T], h_hi[:, o:o + T].bitcast(F32),
                                                ALU.subtract).then_inc(h_done, 1)
                dve.wait_ge(h_done, (n + 1) * KT)

            def add_projection(name, layer, kind, mod=None, stores=None):
                m = mods[layer % 2]
                if stores is not None:
                    if stores:
                        dve.wait_ge(outs_done, stores)
                    nc.vector.memset(square_sum, 0.0)
                k_turns = 2 if mod else 1
                with dve.Fori(0, KT // 2 // k_turns) as i:
                    for k in range(k_turns):
                        if mod:
                            mod_products(mod, i, k)
                        for j in range(2):
                            q = k * 2 + j
                            dve.wait_ge(gemm_done, i * (2 * k_turns) + (phases[name].first + q + 1))
                            for cond, b, c0, t0, n in ((0, 0, 0, 0, NCTX), (1, 0, NCTX, NCTX, TH - NCTX),
                                                       (1, 1, 0, TH, TH)):
                                xs = x[:, bass.ds(i * (2 * k_turns * T) + (q * T + t0), n)]
                                last = nc.vector.scalar_tensor_tensor(
                                    xs, psum[j][:, b, c0:c0 + n],
                                    m[:, bass.ds(i * (4 * k_turns) + ((kind * KT + q) * 2 + cond), 1)], xs,
                                    ALU.mult, ALU.add)
                            last.then_inc(x_done, 1)
                            if stores is not None:
                                dve.drain()
                                add_squares(x[:, bass.ds(i * (2 * k_turns * T) + q * T, T)], square, square_sum)
                        if mod:
                            mod_sums(mod, i, k)
                x_tiles[0] += KT
                dve.wait_ge(x_done, x_tiles[0])

            for layer in range(DEPTH):
                norm(2 * layer)
                if layer == 0:
                    S = MIN
                    pes, acts, dves = S
                    nc.vector.memset(kr_cache, 0.0).then_inc(kr_cleared, 1)
                    acts.wait(dve, "rscq")
                    for t in range(3):
                        normed(mla_raw[t], vec("cq", t), mla_rs[0])
                    dve.drain()
                    for t in range(3):
                        nc.vector.tensor_copy(h_hi[:, CQ_AT + t * T:CQ_AT + (t + 1) * T], mla_raw[t])
                    dve.drain()
                    for t in range(3):
                        last = nc.vector.tensor_tensor(h_lo[:, CQ_AT + t * T:CQ_AT + (t + 1) * T], mla_raw[t],
                                                       h_hi[:, CQ_AT + t * T:CQ_AT + (t + 1) * T].bitcast(F32),
                                                       ALU.subtract)
                    dves.mark(last, "cq")
                    acts.wait(dve, "rsckv")
                    for t in range(2):
                        normed(mla_raw[3 + t], vec("ckv", t), mla_rs[1])
                    dve.drain()
                    for t in range(2):
                        o = CKV_AT + t * NKEY
                        last = split(dve, h_hi[:, o:o + T], h_lo[:, o:o + T], mla_raw[3 + t])
                    dves.mark(last, "ckv")
                    acts.wait(dve, "rskr")
                    dves.mark(nc.vector.scalar_tensor_tensor(kr_t[:, 0:T], mla_raw[5], vec("mqr", 1), mla_rs[2],
                                                             ALU.mult, ALU.mult), "kr")
                    pes.wait(dve, "rotkr")
                    dves.mark(roped(dve, kr_t, psB, cos64, sin64, mla_tmp), "kr_roped")
                    pes.wait(dve, "turned")
                    for t in range(2):
                        o = CKV_AT + t * NKEY + T
                        split(dve, h_hi[:, o:o + P], h_lo[:, o:o + P], psC[:, 0, t * P:(t + 1) * P])
                    dves.mark(nc.vector.tensor_copy(kr_t[:, T:NKEY], psC[:, 0, 2 * P:3 * P]), "cache")
                    A, pv, out, (pes, acts, dves) = MLA

                    def q_nope(h):
                        acts.wait(dve, "rsqn", h)
                        dves.mark(normed(qn_t[h.k % 2], vec("mqk", 0), sq_n), "qn")

                    def q_rope(h):
                        acts.wait(dve, "rsqr", h)
                        dves.mark(normed(qr_t[h.k % 2], vec("mqr", 0), sq_r), "qr")

                    def k_nope(h):
                        acts.wait(dve, "rskn", h)
                        dves.mark(normed(kn_t[h.k % 2], vec("mqk", 1), sq_k), "kn")

                    def q_roped(h):
                        pes.wait(dve, "rotqr", h)
                        dves.mark(roped(dve, qr_t[h.k % 2], psD, cos64, sin64, m_tmp), "qroped")
                        dve.drain()

                    def head(h, more):
                        n = h.next()
                        prep = (lambda step: step(n)) if more else (lambda step: None)
                        for t in range(QT):
                            if t == 3:
                                prep(q_nope)
                            if t == 4:
                                prep(q_rope)
                                prep(k_nope)
                            dve_tile(dve, A, h, t, 1, 192 ** -0.5, m_probs, m_stats)
                        prep(q_roped)
                        pv.wait(dve, "pv", h)
                        out.mark(split_head(dve, h.at(T, 0)), "o")

                    for step in (q_nope, q_rope, k_nope, q_roped):
                        step(Head(0, 0))
                    with dve.Fori(0, HEADS // 2 - 1) as i:
                        for k in range(2):
                            head(Head(i, k), True)
                    for k in range(2):
                        head(Head(HEADS // 2 - 1, k), k == 0)
                elif layer == 1:
                    A, pv, out, (pes, acts, dves) = DIF
                    scale = 64 ** -0.5

                    def q_normed(h):
                        acts.wait(dve, "rsq", h)
                        dves.mark(normed(dq_t[h.k % 2], vec("dqk", 0), dsq_q), "q")

                    def k_normed(h):
                        acts.wait(dve, "rsk", h)
                        dves.mark(normed(dk_t[h.k % 2][:, 0:T], vec("dqk", 1), dsq_k), "k")

                    def q_roped(h):
                        pes.wait(dve, "rotq", h)
                        dves.mark(roped(dve, dq_t[h.k % 2], psD, cos64, sin64, d_tmp), "qroped")
                        dve.drain()

                    def k_roped(h):
                        pes.wait(dve, "rotk", h)
                        dves.mark(roped(dve, dk_t[h.k % 2], psD, cos64, sin64, d_tmp), "kroped")
                        dve.drain()

                    def first_tiles(h):
                        for t in range(2):
                            dve_tile(dve, A, h, t, 2, scale, d_probs, d_stats)

                    def output(h):
                        DIF_NORM.wait(dve, "rso", h)
                        normed(do_t, small[:, 43:44], do_sq)
                        dve.drain()
                        o = bass.ds(h.at(T, 0), T)
                        out.mark(split(dve, act_hi[:, o], act_lo[:, o], do_t), "o")

                    def head(h, more):
                        n = h.next()
                        prep = (lambda step: step(n)) if more else (lambda step: None)
                        dve_tile(dve, A, h, 2, 2, scale, d_probs, d_stats)
                        prep(q_normed)
                        dve_tile(dve, A, h, 3, 2, scale, d_probs, d_stats)
                        prep(k_normed)
                        prep(q_roped)
                        dve_tile(dve, A, h, 4, 2, scale, d_probs, d_stats)
                        prep(k_roped)
                        prep(first_tiles)
                        output(h)

                    for step in (q_normed, k_normed, q_roped, k_roped, first_tiles):
                        step(Head(0, 0))
                    with dve.Fori(0, HEADS // 2 - 1) as i:
                        for k in range(2):
                            head(Head(i, k), True)
                    for k in range(2):
                        head(Head(HEADS // 2 - 1, k), k == 0)
                elif layer == 2:
                    S = GKV
                    pes, acts, dves = S
                    for j in range(2):
                        acts.wait(dve, "rsk", j)
                        dves.mark(normed(gk_t[j][:, 0:T], vec("gqk", 1), gsq), "k")
                        pes.wait(dve, "rotk", j)
                        dves.mark(roped(dve, gk_t[j], psC, cos128, sin128, g_tmp), "kroped")
                        dve.drain()
                    A, pv, out, (pes, acts, dves) = GQA

                    def q_normed(h):
                        acts.wait(dve, "rsq", h)
                        dves.mark(normed(gq_t[h.k % 2], vec("gqk", 0), gsq), "q")

                    def q_roped(h):
                        pes.wait(dve, "rotq", h)
                        dves.mark(roped(dve, gq_t[h.k % 2], psD, cos128, sin128, g_tmp), "qroped")
                        dve.drain()

                    def head(h, more):
                        n = h.next()
                        for t in range(QT):
                            dve_tile(dve, A, h, t, 1, P ** -0.5, g_probs, g_stats)
                            if t == 3 and more:
                                q_normed(n)
                        if more:
                            q_roped(n)
                        pv.wait(dve, "pv", h)
                        out.mark(split_head(dve, h.i * T + h.k * (HEADS // 2 * T)), "o")

                    q_normed(Head(0, 0))
                    q_roped(Head(0, 0))
                    with dve.Fori(0, HEADS // 2 - 1) as i:
                        for k in range(2):
                            head(Head(i, k), True)
                    for k in range(2):
                        head(Head(HEADS // 2 - 1, k), k == 0)
                else:
                    nc.vector.memset(l_xp, 0.0).then_inc(lru_ready, 1)

                    def convolved(i):
                        LRU_XP.wait(dve, "xp", i)
                        cw = [vecs[:, bass.ds(i + (VEC["convw"] + k * KT), 1)] for k in range(4)]
                        cb = vecs[:, bass.ds(i + VEC["convb"], 1)]
                        nc.vector.tensor_scalar(l_y, l_xp[:, 0:LW], cw[0], cb, ALU.mult, ALU.add)
                        for k in range(1, 4):
                            dve.drain()
                            nc.vector.scalar_tensor_tensor(l_y, l_xp[:, k:k + LW], cw[k], l_y, ALU.mult, ALU.add)
                        dve.drain()
                        LRU_Y.mark(split(dve, y_hi[:, :], y_lo[:, :], l_y), "y")

                    def lru_tail(i, more):
                        LRU_ACT.wait(dve, "t", i)
                        for d in range(2):
                            nc.vector.scalar_tensor_tensor(l_ti[d], l_ti[d], 1.0, l_y, ALU.add, ALU.mult)
                        LRU_ACT.wait(dve, "a2", i)
                        for d in range(2):
                            last = nc.vector.scalar_tensor_tensor(l_th[d], l_tr[d], 1.0, l_th[d], ALU.add, ALU.mult)
                        LRU_DVE.mark(last, "m")
                        dve.drain()
                        if more:
                            convolved(i + 1)
                        LRU_ACT.wait(dve, "sq", i)
                        for d in range(2):
                            last = nc.vector.scalar_tensor_tensor(l_ti[d], l_ti[d], 0.5, l_tr[d], ALU.mult, ALU.mult)
                        LRU_DVE.mark(last, "u")
                        dve.drain()
                        for d in range(2):
                            for t0, n, init in ((0, NCTX, 0.0), (LAT0, NLAT, vecs[:, bass.ds(i + (VEC["h0"] + d * KT), 1)])):
                                o, a_, u_ = (b_[d][:, t0:t0 + n] for b_ in (l_th, l_a, l_ti))
                                if d:
                                    o, a_, u_ = o[:, ::-1], a_[:, ::-1], u_[:, ::-1]
                                last = nc.vector.tensor_tensor_scan(o, a_, u_, init, ALU.mult, ALU.add)
                        LRU_DVE.mark(last, "h")
                        dve.drain()
                        nc.vector.tensor_copy(l_state[:, bass.ds(i, 1)], l_th[0][:, NCTX - 1:NCTX])
                        nc.vector.tensor_copy(l_state[:, bass.ds(i + KT, 1)], l_th[1][:, 0:1])
                        dve.drain()
                        for t0, n, g0 in ((0, NCTX, 0), (LAT0, NLAT, NCTX)):
                            nc.vector.tensor_tensor(l_th[0][:, t0:t0 + n], l_th[0][:, t0:t0 + n],
                                                    l_th[1][:, t0:t0 + n], ALU.add)
                        dve.drain()
                        for t0, n, g0 in ((0, NCTX, 0), (LAT0, NLAT, NCTX)):
                            out = l_gelu[:, bass.ds(i * T + g0, n)]
                            last = nc.vector.tensor_tensor(out, l_th[0][:, t0:t0 + n], out, ALU.mult)
                        LRU_DVE.mark(last, "g")
                        dve.drain()
                        o = bass.ds(i * T, T)
                        LRU_DVE.mark(split(dve, act_hi[:, o], act_lo[:, o], l_gelu[:, o]), "o")

                    convolved(0)
                    with dve.Fori(0, KT - 1) as i:
                        lru_tail(i, True)
                    lru_tail(KT - 1, False)
                add_projection(f"wo{layer}", layer, 2, stores=(32, 32 + 32 * HEADS, 96 + 32 * HEADS, 96 + 32 * HEADS)[layer])
                norm(2 * layer + 1)
                for ch, size in enumerate(FFN_CHUNKS):
                    base = layer * (FFN // P) + sum(FFN_CHUNKS[:ch])
                    mod = mod_at(layer, ch, False)
                    k_turns = 2 if mod else 1
                    with dve.Fori(0, size // k_turns) as i:
                        for k in range(k_turns):
                            if mod:
                                mod_products(mod, i, k)
                            dve.wait_ge(silu_done, i * k_turns + (base + k + 2))
                            dve.wait_ge(gemm_done, i * (2 * k_turns) + (phases[f"in{layer}.{ch}"].first + 2 * k + 2))
                            dve.wait_ge(hidden_done, i * k_turns + (base + k + 1))
                            nc.vector.tensor_tensor(halves(prod, TH), halves(gate_silu, TH), psB[:, :, 0:TH], ALU.mult)
                            dve.drain()
                            o = bass.ds(i * (k_turns * T) + k * T, T)
                            split(dve, act_hi[:, o], act_lo[:, o], prod).then_inc(hidden_done, 1)
                            if mod:
                                mod_sums(mod, i, k)
                    ends = ch == len(FFN_CHUNKS) - 1 and layer + 1 < DEPTH
                    add_projection(f"out{layer}.{ch}", layer, 5, mod_at(layer, ch, True), 0 if ends else None)


def host_tables():
    ident = np.eye(P, dtype=np.float32)
    ones = np.ones((P, P), np.float32)
    blocks = np.kron(np.eye(2), np.ones((64, 64))).astype(np.float32)

    def rotation(dim):
        r = np.zeros((P, P), np.float32)
        for m in range(P):
            if m % dim < dim // 2:
                r[m + dim // 2, m] = -1.0
            else:
                r[m - dim // 2, m] = 1.0
        return r

    consts = np.concatenate([ident, ones, blocks, rotation(64), rotation(128)], axis=1)

    def rotary(dim):
        grid_w, n_freq = 64, dim // 4
        tok = np.arange(NLAT)
        inv = np.float32(10000.0) ** (-np.arange(n_freq, dtype=np.float32) / n_freq)
        ang = np.concatenate([(tok // grid_w).astype(np.float32)[:, None] * inv,
                              (tok % grid_w).astype(np.float32)[:, None] * inv], axis=1)
        full = np.tile(ang, (1, P // (dim // 2))).T.astype(np.float32)
        return np.cos(full), np.sin(full)

    tables = np.concatenate([*rotary(64), *rotary(128)], axis=1).astype(np.float32)
    return np.ascontiguousarray(consts), np.ascontiguousarray(tables)


_OUTS = [("y_prompt", (1, 128, 1024)), ("y_sample", (1, 512, 1024)), ("new_mla_ckv", (1, 1, 128, 256)),
         ("new_mla_krope", (1, 1, 128, 64)), ("new_diff_k", (1, 1, 128, 8, 2, 64)),
         ("new_diff_v", (1, 1, 128, 8, 128)), ("new_gqa_k", (1, 1, 128, 2, 128)),
         ("new_gqa_v", (1, 1, 128, 2, 128)), ("new_lru_h", (1, 1, 2, 1024))]


def kernel(**inputs):
    import concourse.bacc as _bacc
    from concourse.bass_utils import run_bass_kernel_spmd as _run

    nc = _bacc.Bacc("TRN2", target_bir_lowering=False, num_devices=1)
    arrays, aps = {}, {}
    consts, tables = host_tables()
    for name, value in list(inputs.items()) + [("consts", consts), ("tables", tables)]:
        v = np.ascontiguousarray(value)
        arrays[f"in_{name}"] = v
        aps[name] = nc.dram_tensor(f"in_{name}", v.shape, mybir.dt.from_np(v.dtype), kind="ExternalInput").ap()
    for name, shape in _OUTS:
        aps[name] = nc.dram_tensor(f"out_{name}", shape, F32, kind="ExternalOutput").ap()
    build(nc, aps)
    r = _run(nc, [arrays], core_ids=[0])
    return tuple(r.results[0][f"out_{name}"] for name, _ in _OUTS)
```
